# Optimizing a Trainium2 kernel written in Bass

```python
import math
import jax
import jax.numpy as jnp
from jax import lax
import numpy as np

D_MODEL = 1024
BATCH = 1
SEQ = 256
DEPTH = 2

GRID_W = 64
CTX_LEN = 256
ROPE_THETA = 10000.0
RMS_EPS = 1e-6
Q_BLOCK = 128
HEAD_DIM = 64
N_BRANCH = 4
BRANCH_HEADS = D_MODEL // (N_BRANCH * HEAD_DIM)
BRANCH_WIDTH = BRANCH_HEADS * HEAD_DIM
NA_WIN_H = 8
NA_WIN_W = 16
GQA_KV_HEADS = 2
DIFF_QK_DIM = 32
MLA_Q_RANK = D_MODEL // 4
MLA_KV_RANK = D_MODEL // 8
MLA_NOPE_DIM = 64
MLA_ROPE_DIM = 32
MLA_QK_DIM = MLA_NOPE_DIM + MLA_ROPE_DIM
D_FF = 128 * ((8 * D_MODEL // 3 + 127) // 128)
N_MOD = 9
NA_COLS = 3 * BRANCH_WIDTH
GQA_COLS = BRANCH_WIDTH + 2 * GQA_KV_HEADS * HEAD_DIM
DIFF_COLS = 2 * BRANCH_HEADS * 2 * DIFF_QK_DIM + BRANCH_WIDTH
MLA_COLS = MLA_Q_RANK + MLA_KV_RANK + MLA_ROPE_DIM
IN_COLS = NA_COLS + GQA_COLS + DIFF_COLS + MLA_COLS
IN_SPLITS = (NA_COLS, NA_COLS + GQA_COLS, NA_COLS + GQA_COLS + DIFF_COLS)

kernel_name = 'hybrid_gated_multimixer_diffusion_trunk'

def rms_norm(x, g):
    xf = x.astype(jnp.float32)
    y = xf * lax.rsqrt(jnp.mean(jnp.square(xf), axis=-1, keepdims=True) + RMS_EPS)
    return (y * g.astype(jnp.float32)).astype(x.dtype)

def modulate(x, g, shift, scale):
    return rms_norm(x, g) * (1 + scale[:, None, :]) + shift[:, None, :]

def ffn_half_step(x, g, shift, scale, gate, w1, w3, w2):
    h = modulate(x, g, shift, scale)
    return x + 0.5 * gate[:, None, :] * ((jax.nn.silu(h @ w1) * (h @ w3)) @ w2)

def axial_rope_tables(n_tok, rot_dim):
    t = jnp.arange(n_tok, dtype=jnp.int32)
    row = (t // GRID_W).astype(jnp.float32)
    col = (t % GRID_W).astype(jnp.float32)
    n_freq = rot_dim // 4
    inv = ROPE_THETA ** (-jnp.arange(n_freq, dtype=jnp.float32) / n_freq)
    ar = row[:, None] * inv[None, :]
    ac = col[:, None] * inv[None, :]
    ang = jnp.concatenate([ar, ar, ac, ac], axis=-1)
    return jnp.cos(ang), jnp.sin(ang)

def apply_axial_rope(x, cos, sin):
    xf = x.astype(jnp.float32)
    x1, x2, x3, x4 = jnp.split(xf, 4, axis=-1)
    rot = jnp.concatenate([-x2, x1, -x4, x3], axis=-1)
    shp = (x.shape[1],) + (1,) * (x.ndim - 3) + (x.shape[-1],)
    return (xf * cos.reshape(shp) + rot * sin.reshape(shp)).astype(x.dtype)

def ctx_attention(q, k, v, scale):
    s = jnp.einsum('bqgrd,bkgd->bgrqk', q, k, preferred_element_type=jnp.float32) * scale
    p = jax.nn.softmax(s, axis=-1).astype(v.dtype)
    return jnp.einsum('bgrqk,bkgd->bqgrd', p, v)

def joint_attention(q_pos, q_nopos, k_lat, v_lat, k_ctx, v_ctx, scale):
    B, S, G, R, dk = q_pos.shape
    nb = S // Q_BLOCK

    def to_blocks(q):
        return jnp.moveaxis(q.reshape(B, nb, Q_BLOCK, G, R, dk), 1, 0)

    def block(qs):
        qb, qcb = qs
        s_lat = jnp.einsum('bqgrd,bkgd->bgrqk', qb, k_lat, preferred_element_type=jnp.float32)
        s_ctx = jnp.einsum('bqgrd,bkgd->bgrqk', qcb, k_ctx, preferred_element_type=jnp.float32)
        p = jax.nn.softmax(jnp.concatenate([s_lat, s_ctx], axis=-1) * scale, axis=-1).astype(v_lat.dtype)
        return (jnp.einsum('bgrqk,bkgd->bqgrd', p[..., :S], v_lat)
                + jnp.einsum('bgrqk,bkgd->bqgrd', p[..., S:], v_ctx))

    o = lax.map(block, (to_blocks(q_pos), to_blocks(q_nopos)))
    return jnp.moveaxis(o, 0, 1).reshape(B, S, G, R, v_lat.shape[-1])

def neighbourhood_attention(q, k, v, k_ctx, v_ctx, rpb, scale):
    B, S, H, d = q.shape
    rows = S // GRID_W
    wh = min(NA_WIN_H, rows)
    r = jnp.arange(rows)
    r0 = jnp.clip(r - wh // 2, 0, rows - wh)
    key_rows = r0[:, None] + jnp.arange(wh)[None, :]
    col = jnp.arange(GRID_W)
    c0 = jnp.clip(col - NA_WIN_W // 2, 0, GRID_W - NA_WIN_W)
    in_win = (col[None, :] >= c0[:, None]) & (col[None, :] < c0[:, None] + NA_WIN_W)
    qg = q.reshape(B, rows, GRID_W, H, d)
    kg = k.reshape(B, rows, GRID_W, H, d)[:, key_rows]
    vg = v.reshape(B, rows, GRID_W, H, d)[:, key_rows]
    s_nb = jnp.einsum('brqhd,brakhd->bhrqak', qg, kg, preferred_element_type=jnp.float32) * scale
    d_row = key_rows - r[:, None] + (NA_WIN_H - 1)
    d_col = jnp.clip(col[None, :] - col[:, None], -(NA_WIN_W - 1), NA_WIN_W - 1) + (NA_WIN_W - 1)
    bias = rpb[:, d_row[:, None, :, None], d_col[None, :, None, :]]
    s_nb = jnp.where(in_win[:, None, :], s_nb + bias.astype(jnp.float32), -jnp.inf)
    s_nb = s_nb.reshape(B, H, rows, GRID_W, wh * GRID_W)
    s_ctx = jnp.einsum('brqhd,blhd->bhrql', qg, k_ctx, preferred_element_type=jnp.float32) * scale
    p = jax.nn.softmax(jnp.concatenate([s_nb, s_ctx], axis=-1), axis=-1).astype(v.dtype)
    p_nb = p[..., :wh * GRID_W].reshape(B, H, rows, GRID_W, wh, GRID_W)
    o = (jnp.einsum('bhrqak,brakhd->brqhd', p_nb, vg)
         + jnp.einsum('bhrql,blhd->brqhd', p[..., wh * GRID_W:], v_ctx))
    return o.reshape(B, S, H, d)

def mixer_na(p_lat, p_ctx, g_q, g_k, rpb, need_ctx):
    def project(p):
        b, n = p.shape[:2]
        p = p.reshape(b, n, 3, BRANCH_HEADS, HEAD_DIM)
        return rms_norm(p[:, :, 0], g_q), rms_norm(p[:, :, 1], g_k), p[:, :, 2]
    q, k, v = project(p_lat)
    qc, kc, vc = project(p_ctx)
    scale = HEAD_DIM ** -0.5
    o_lat = neighbourhood_attention(q, k, v, kc, vc, rpb, scale).reshape(p_lat.shape[0], p_lat.shape[1], BRANCH_WIDTH)
    o_ctx = None
    if need_ctx:
        o_ctx = ctx_attention(qc[:, :, :, None], kc, vc, scale).reshape(p_ctx.shape[0], p_ctx.shape[1], BRANCH_WIDTH)
    return o_lat, o_ctx

def mixer_gqa(p_lat, p_ctx, g_q, g_k, cos, sin, need_ctx):
    R = BRANCH_HEADS // GQA_KV_HEADS
    def project(p):
        b, n = p.shape[:2]
        q, k, v = jnp.split(p, [BRANCH_WIDTH, BRANCH_WIDTH + GQA_KV_HEADS * HEAD_DIM], axis=-1)
        q = rms_norm(q.reshape(b, n, GQA_KV_HEADS, R, HEAD_DIM), g_q)
        k = rms_norm(k.reshape(b, n, GQA_KV_HEADS, HEAD_DIM), g_k)
        return q, k, v.reshape(b, n, GQA_KV_HEADS, HEAD_DIM)
    q, k, v = project(p_lat)
    qc, kc, vc = project(p_ctx)
    scale = HEAD_DIM ** -0.5
    o = joint_attention(apply_axial_rope(q, cos, sin), q, apply_axial_rope(k, cos, sin), v, kc, vc, scale)
    o_lat = o.reshape(p_lat.shape[0], p_lat.shape[1], BRANCH_WIDTH)
    o_ctx = None
    if need_ctx:
        o_ctx = ctx_attention(qc, kc, vc, scale).reshape(p_ctx.shape[0], p_ctx.shape[1], BRANCH_WIDTH)
    return o_lat, o_ctx

def mixer_diff(p_lat, p_ctx, g_q, g_k, lam_vecs, g_sub, lam_init, cos, sin, need_ctx):
    H, dq = BRANCH_HEADS, DIFF_QK_DIM
    def project(p):
        b, n = p.shape[:2]
        q, k, v = jnp.split(p, [H * 2 * dq, 2 * H * 2 * dq], axis=-1)
        q = rms_norm(q.reshape(b, n, H, 2, dq), g_q)
        k = rms_norm(k.reshape(b, n, H, 2, dq), g_k)
        return q, k, v.reshape(b, n, H, HEAD_DIM)
    q, k, v = project(p_lat)
    qc, kc, vc = project(p_ctx)
    lv = lam_vecs.astype(jnp.float32)
    lam = (jnp.exp(jnp.sum(lv[0] * lv[1])) - jnp.exp(jnp.sum(lv[2] * lv[3])) + lam_init).astype(v.dtype)
    scale = dq ** -0.5

    def combine(o1, o2):
        b, n = o1.shape[:2]
        return (rms_norm(o1 - lam * o2, g_sub) * (1 - lam_init)).reshape(b, n, BRANCH_WIDTH)

    qr, kr = apply_axial_rope(q, cos, sin), apply_axial_rope(k, cos, sin)
    o1 = joint_attention(qr[:, :, :, 0:1], q[:, :, :, 0:1], kr[:, :, :, 0], v, kc[:, :, :, 0], vc, scale)
    o2 = joint_attention(qr[:, :, :, 1:2], q[:, :, :, 1:2], kr[:, :, :, 1], v, kc[:, :, :, 1], vc, scale)
    o_lat = combine(o1, o2)
    o_ctx = None
    if need_ctx:
        o_ctx = combine(ctx_attention(qc[:, :, :, 0:1], kc[:, :, :, 0], vc, scale),
                        ctx_attention(qc[:, :, :, 1:2], kc[:, :, :, 1], vc, scale))
    return o_lat, o_ctx

def mixer_mla(p_lat, p_ctx, g_cq, g_ckv, w_uq, w_ukv, g_q, g_k, cos, sin, need_ctx):
    H = BRANCH_HEADS
    def project(p):
        b, n = p.shape[:2]
        c_q, c_kv, k_rope = jnp.split(p, [MLA_Q_RANK, MLA_Q_RANK + MLA_KV_RANK], axis=-1)
        q = (rms_norm(c_q, g_cq) @ w_uq).reshape(b, n, H, MLA_QK_DIM)
        kv = (rms_norm(c_kv, g_ckv) @ w_ukv).reshape(b, n, H, MLA_NOPE_DIM + HEAD_DIM)
        k = jnp.concatenate([kv[..., :MLA_NOPE_DIM],
                             jnp.broadcast_to(k_rope[:, :, None, :], (b, n, H, MLA_ROPE_DIM))], axis=-1)
        return rms_norm(q, g_q)[:, :, :, None], rms_norm(k, g_k), kv[..., MLA_NOPE_DIM:]

    def rope_tail(t):
        return jnp.concatenate([t[..., :MLA_NOPE_DIM], apply_axial_rope(t[..., MLA_NOPE_DIM:], cos, sin)], axis=-1)

    q, k, v = project(p_lat)
    qc, kc, vc = project(p_ctx)
    scale = MLA_QK_DIM ** -0.5
    o = joint_attention(rope_tail(q), q, rope_tail(k), v, kc, vc, scale)
    o_lat = o.reshape(p_lat.shape[0], p_lat.shape[1], BRANCH_WIDTH)
    o_ctx = None
    if need_ctx:
        o_ctx = ctx_attention(qc, kc, vc, scale).reshape(p_ctx.shape[0], p_ctx.shape[1], BRANCH_WIDTH)
    return o_lat, o_ctx

def merge_branches(n, outs, w_gate, b_gate, w_branch, w_out):
    y = jax.nn.sigmoid(n @ w_gate[0] + b_gate[0]) * (outs[0] @ w_branch[0])
    for j in range(1, N_BRANCH):
        y = y + jax.nn.sigmoid(n @ w_gate[j] + b_gate[j]) * (outs[j] @ w_branch[j])
    return y @ w_out

def setup_inputs(seed: int = 0) -> dict:
    key = jax.random.key(seed)
    keys = iter(jax.random.split(key, 32))
    f32 = jnp.float32

    def normal(shape, std):
        return jax.random.normal(next(keys), shape, f32) * std

    def gain(shape):
        return 1.0 + normal(shape, 0.05)

    L, D = DEPTH, D_MODEL
    return {
        'x': normal((BATCH, SEQ, D), 1.0),
        'c': normal((BATCH, D), 1.0),
        'ctx': normal((BATCH, CTX_LEN, D), 1.0),
        'c_ctx': normal((D,), 1.0),
        'w_ada': normal((L, D, N_MOD * D), 0.5 * D ** -0.5),
        'b_ada': normal((L, N_MOD * D), 0.02),
        'norm_g': gain((L, 3, D)),
        'ffn_w1': normal((L, 2, D, D_FF), D ** -0.5),
        'ffn_w3': normal((L, 2, D, D_FF), D ** -0.5),
        'ffn_w2': normal((L, 2, D_FF, D), D_FF ** -0.5),
        'w_in': normal((L, D, IN_COLS), D ** -0.5),
        'na_g_q': gain((L, HEAD_DIM)),
        'na_g_k': gain((L, HEAD_DIM)),
        'na_rpb': normal((L, BRANCH_HEADS, 2 * NA_WIN_H - 1, 2 * NA_WIN_W - 1), 0.1),
        'gqa_g_q': gain((L, HEAD_DIM)),
        'gqa_g_k': gain((L, HEAD_DIM)),
        'diff_g_q': gain((L, DIFF_QK_DIM)),
        'diff_g_k': gain((L, DIFF_QK_DIM)),
        'diff_lambda': normal((L, 4, DIFF_QK_DIM), 0.1),
        'diff_g_sub': gain((L, HEAD_DIM)),
        'mla_g_cq': gain((L, MLA_Q_RANK)),
        'mla_g_ckv': gain((L, MLA_KV_RANK)),
        'mla_w_uq': normal((L, MLA_Q_RANK, BRANCH_HEADS * MLA_QK_DIM), MLA_Q_RANK ** -0.5),
        'mla_w_ukv': normal((L, MLA_KV_RANK, BRANCH_HEADS * (MLA_NOPE_DIM + HEAD_DIM)), MLA_KV_RANK ** -0.5),
        'mla_g_q': gain((L, MLA_QK_DIM)),
        'mla_g_k': gain((L, MLA_QK_DIM)),
        'w_gate': normal((L, N_BRANCH, D, D), D ** -0.5),
        'b_gate': normal((L, N_BRANCH, D), 0.02),
        'w_branch': normal((L, N_BRANCH, BRANCH_WIDTH, D), BRANCH_WIDTH ** -0.5),
        'w_out': normal((L, D, D), D ** -0.5),
    }

def reference(x, c, ctx, c_ctx, w_ada, b_ada, norm_g, ffn_w1, ffn_w3, ffn_w2, w_in,
              na_g_q, na_g_k, na_rpb, gqa_g_q, gqa_g_k, diff_g_q, diff_g_k, diff_lambda, diff_g_sub,
              mla_g_cq, mla_g_ckv, mla_w_uq, mla_w_ukv, mla_g_q, mla_g_k,
              w_gate, b_gate, w_branch, w_out):
    S = x.shape[1]
    cos64, sin64 = axial_rope_tables(S, HEAD_DIM)
    cos_d, sin_d = axial_rope_tables(S, DIFF_QK_DIM)
    cos_m, sin_m = axial_rope_tables(S, MLA_ROPE_DIM)
    silu_c = jax.nn.silu(c)
    silu_cc = jax.nn.silu(c_ctx)[None, :]
    xl, xc = x, ctx
    for i in range(DEPTH):
        need_ctx = i < DEPTH - 1
        mod_l = jnp.split(silu_c @ w_ada[i] + b_ada[i], N_MOD, axis=-1)
        mod_c = jnp.split(silu_cc @ w_ada[i] + b_ada[i], N_MOD, axis=-1)
        xl = ffn_half_step(xl, norm_g[i, 0], mod_l[0], mod_l[1], mod_l[2], ffn_w1[i, 0], ffn_w3[i, 0], ffn_w2[i, 0])
        xc = ffn_half_step(xc, norm_g[i, 0], mod_c[0], mod_c[1], mod_c[2], ffn_w1[i, 0], ffn_w3[i, 0], ffn_w2[i, 0])
        nl = modulate(xl, norm_g[i, 1], mod_l[3], mod_l[4])
        nc = modulate(xc, norm_g[i, 1], mod_c[3], mod_c[4])
        pl = jnp.split(nl @ w_in[i], IN_SPLITS, axis=-1)
        pc = jnp.split(nc @ w_in[i], IN_SPLITS, axis=-1)
        lam_init = 0.8 - 0.6 * math.exp(-0.3 * i)
        outs = [
            mixer_na(pl[0], pc[0], na_g_q[i], na_g_k[i], na_rpb[i], need_ctx),
            mixer_gqa(pl[1], pc[1], gqa_g_q[i], gqa_g_k[i], cos64, sin64, need_ctx),
            mixer_diff(pl[2], pc[2], diff_g_q[i], diff_g_k[i], diff_lambda[i], diff_g_sub[i], lam_init,
                       cos_d, sin_d, need_ctx),
            mixer_mla(pl[3], pc[3], mla_g_cq[i], mla_g_ckv[i], mla_w_uq[i], mla_w_ukv[i], mla_g_q[i], mla_g_k[i],
                      cos_m, sin_m, need_ctx),
        ]
        xl = xl + mod_l[5][:, None, :] * merge_branches(nl, [o[0] for o in outs], w_gate[i], b_gate[i], w_branch[i], w_out[i])
        if need_ctx:
            xc = xc + mod_c[5][:, None, :] * merge_branches(nc, [o[1] for o in outs], w_gate[i], b_gate[i], w_branch[i], w_out[i])
            xc = ffn_half_step(xc, norm_g[i, 2], mod_c[6], mod_c[7], mod_c[8], ffn_w1[i, 1], ffn_w3[i, 1], ffn_w2[i, 1])
        xl = ffn_half_step(xl, norm_g[i, 2], mod_l[6], mod_l[7], mod_l[8], ffn_w1[i, 1], ffn_w3[i, 1], ffn_w2[i, 1])
    return xl


_drawn_inputs = setup_inputs


def setup_inputs(seed=0):
    import zlib

    import numpy as np

    out = dict(_drawn_inputs(seed))
    spreads = {}
    factors = {'norm_g': 3.183,
     'na_g_q': 8.0,
     'na_g_k': 8.0,
     'na_rpb': 8.0,
     'gqa_g_q': 8.0,
     'gqa_g_k': 8.0,
     'diff_g_q': 8.0,
     'diff_g_k': 8.0,
     'diff_lambda': 7.375,
     'diff_g_sub': 6.539,
     'mla_g_cq': 8.0,
     'mla_g_ckv': 8.0,
     'mla_g_q': 8.0,
     'mla_g_k': 8.0,
     'b_gate': 8.0}
    for name, (base, spread) in spreads.items():
        noise = np.random.default_rng([zlib.crc32(name.encode()), seed]).standard_normal(out[name].shape)
        drawn = base * np.exp(spread * noise) if base else spread * noise
        out[name] = jnp.asarray(drawn.astype(out[name].dtype))
    for name, factor in factors.items():
        out[name] = (out[name] * factor).astype(out[name].dtype)
    return out
```

```python
import math
from contextlib import ExitStack

import concourse.bass as bass
from concourse import mybir
from concourse.alu_op_type import AluOpType as ALU

F32 = mybir.dt.float32
F32R = mybir.dt.float32r
ACT = mybir.ActivationFunctionType
AX_X = mybir.AxisListType.X

P = 128
D = 1024
KC = D // P
S = 256
NT = 512
TT = NT // P
LT = S // P
DEPTH = 2
GRID_W = 64
EPS = 1e-6
FC = 22
GROUPS = [(0, 8), (8, 8), (16, 6)]
NMOD = 9
IN_COLS = 2464
RPB = 15 * 31
RING = 4
ADA_PRE = 17
ADA_A = 5
ADA_MID = 6
ADA_B = 6
ADA_L = NMOD * KC
LAM_INIT = [0.8 - 0.6 * math.exp(-0.3 * i) for i in range(DEPTH)]
assert ADA_PRE + 11 * ADA_A == ADA_L and ADA_MID + 11 * ADA_B == ADA_L

NA0, GQA0, DIFF0, MLA0, PIN_END = 0, 3072, 5120, 8192, 9856
Q0, P0, PT0, OUT0, BM0, TMP0, ARENA = 9856, 12416, 13440, 13952, 14976, 16000, 17536
SEGMENTS = [(0, 768, NA0, 768), (768, 1280, GQA0, 512), (1280, 2048, DIFF0, 768), (2048, 2464, MLA0, 416)]
CHUNKS = [(0, 512), (512, 512), (1024, 512), (1536, 512), (2048, 416)]

G_NA, G_GQA, G_DIFF, G_SUB, G_CQ, G_CKV, G_MQ, G_MK, G_END = 0, 128, 320, 384, 448, 704, 832, 928, 1024

VAR0 = {"na": 0, "gqa": 32, "diff": 56, "mlac": 120, "mlaqk": 128, "sub": 160}
VAR_END = 176

BRANCHES = ["na", "gqa", "diff", "mla0", "mla1"]
HEAD_D = {"na": 64, "gqa": 64, "diff": 32, "mla0": 96, "mla1": 96}
SCALE = {b: float(d) ** -0.5 for b, d in HEAD_D.items()}


def spread(steps, pieces):
    out, done = [], 0
    for i, s in enumerate(steps):
        out += s if isinstance(s, list) else [s]
        want = (i + 1) * len(pieces) // len(steps)
        out += pieces[done:want]
        done = want
    return out + pieces[done:]


def job_pieces(kind, *a):
    return [(kind, *a, h) for h in range(2)]


def merge_jobs(b, ms):
    out = []
    for m in ms:
        out += job_pieces("gate", b, m) + [("branch", b, m)]
    return out


def heads_of(b):
    if b == "mla0":
        return [0, 1]
    if b == "mla1":
        return [2, 3]
    return list(range(8 if b == "diff" else 4))


class Plan:

    def __init__(self):
        self.timelines = []
        self.units = []
        self.head_last = []
        self.slabs = 0
        self.norms = 0
        n = RING
        self.ffn_n0 = {}
        self.need_drained = {}
        self.jobs = {}
        for layer in range(DEPTH):
            n = self.place_ffn(layer, 0, n)
            self.timelines.append(self.timeline(layer, n))
            n = self.n
            n = self.place_ffn(layer, 1, n)
        self.total = n

    def place_ffn(self, layer, which, n):
        self.ffn_n0[layer, which] = n
        return n + 2 * FC + KC * len(GROUPS)

    def timeline(self, layer, n):
        nt = TT if layer == 0 else LT

        def slabs(b):
            nq = 2
            out = [("slab", b, "qu", s) for s in range(nq)]
            if b != "na":
                out += [("slab", b, "qr", s) for s in range(nq)]
            return out + [("slab", b, "k", s) for s in range(1 if b == "gqa" else 2)]

        def attention(b):
            us = [(b, h, t) for h in heads_of(b) for t in range(nt)]
            out = []
            for i in range(len(us) + 2):
                turn = []
                if i >= 2:
                    turn.append(("mix", *us[i - 2]))
                    if us[i - 2][2] == nt - 1:
                        turn.append(("head", us[i - 2][0], us[i - 2][1]))
                if 1 <= i <= len(us):
                    turn.append(("turn", *us[i - 1]))
                if i < len(us):
                    turn.append(("score", *us[i]))
                out.append(turn)
            return out

        outs = [("turn_out", s) for s in range(2)]
        proj = [x for c in range(len(CHUNKS)) for kp in range(4) for x in job_pieces("proj", c, kp)]
        steps = [("gain",)]
        steps += proj[:16]
        na = [("norm", "na")] + slabs("na") + attention("na")
        rest = proj[16:]
        steps += spread([("norm", "na")] + slabs("na") + attention("na"), rest)
        steps += [("norm", "gqa")]
        steps += outs
        steps += spread([("norm", "diff"), ("norm", "mlac")] + slabs("gqa") + attention("gqa"), merge_jobs(0, range(8)))
        steps += outs
        d = attention("diff")
        cut = len(d) // 2
        steps += spread(slabs("diff") + [("turn_c", s) for s in range(3)] + d[:cut], merge_jobs(1, range(4)))
        steps += job_pieces("up", "q") + job_pieces("up", "kv")
        steps += spread([("norm", "mlaqk")] + d[cut:], merge_jobs(1, range(4, 8)))
        steps += [("norm", "sub")] + outs
        steps += spread(slabs("mla0") + attention("mla0") + slabs("mla1") + attention("mla1"), merge_jobs(2, range(8)))
        steps += outs
        steps += merge_jobs(3, range(8))
        steps += [("y_last",)]
        steps += [x for m in range(8) for x in job_pieces("out", m)]

        done, bank_user = [], {b: n - 4 + ((b - n) % 4) for b in range(4)}
        order = [s for s in steps]
        self.n = n
        unit_of, cur = {}, None
        for s in order:
            kind = s[0]
            rec = {"step": s, "kind": kind}
            if kind in ("proj", "gate", "up", "out"):
                if s[-1] == 0:
                    cur = self.n
                    self.n += 1
                rec["n"] = cur
                self.jobs[cur] = s
            elif kind == "branch":
                rec["n"] = self.n
                self.jobs[self.n] = s
                self.n += 1
            elif kind == "score":
                unit_of[s[1:]] = len(self.units)
                rec["u"] = len(self.units)
                self.units.append((layer, *s[1:]))
            elif kind in ("turn", "mix"):
                rec["u"] = unit_of[s[1:]]
            elif kind == "head":
                rec["h"] = len(self.head_last)
                rec["u"] = unit_of[(s[1], s[2], nt - 1)]
                self.head_last.append(rec["u"])
            elif kind in ("slab", "turn_out", "turn_c"):
                rec["x"] = self.slabs
                self.slabs += 1
            elif kind == "norm":
                rec["v"] = self.norms
                self.norms += 1
            done.append(rec)
        for rec in done:
            if "n" not in rec or rec["n"] in self.need_drained:
                continue
            m, s = rec["n"], rec["step"]
            if s[0] == "proj":
                c0 = m - s[2]
                self.need_drained[m] = None
            elif s[0] == "up":
                self.need_drained[m] = m
                for b in range(4):
                    bank_user[b] = m
            else:
                self.need_drained[m] = bank_user[m % 4] + 1 if m % 4 in bank_user else m - 3
                self.need_drained[m] = max(self.need_drained[m], m - 3)
                bank_user[m % 4] = m
        return done


def build(nc, A, out):
    plan = Plan()
    scratch = nc.dram_tensor("rpb_rows", [64, DEPTH * 4 * RPB], F32, kind="Internal").ap()
    row = DEPTH * 4 * RPB

    with ExitStack() as ctx:
        def sb(name, shape, dt=F32):
            return ctx.enter_context(nc.sbuf_tensor(name, shape, dt))

        def sem(name):
            return ctx.enter_context(nc.semaphore(name))

        x = sb("x", [P, KC, NT])
        h_hi, h_lo = sb("h_hi", [P, KC, NT], F32R), sb("h_lo", [P, KC, NT], F32R)
        a_hi, a_lo = sb("a_hi", [P, 8, NT], F32R), sb("a_lo", [P, 8, NT], F32R)
        w_raw = sb("w_raw", [P, RING, 1024])
        w_hi, w_lo = sb("w_hi", [P, RING, 1024], F32R), sb("w_lo", [P, RING, 1024], F32R)
        arena = sb("arena", [P, ARENA])
        rope = sb("rope", [P, LT, 192])
        gains = sb("gains", [P, G_END])
        mods = sb("mods", [P, DEPTH * ADA_L, 2])
        vecs = sb("vecs", [P, P])
        b_ada = sb("b_ada", [P, DEPTH * ADA_L])
        cond = sb("cond", [P, KC, 2])
        ident = sb("ident", [P, P])
        mean = sb("mean", [P, 2])
        mask = sb("mask", [P, GRID_W])
        scale_g = sb("scale_g", [P, KC, 2])
        gate_s = sb("gate_s", [P, KC, 2])
        var = sb("var", [P, VAR_END])
        tok_var = sb("tok_var", [P, 4])
        rowsum = sb("rowsum", [P, 2, 4])
        rinv = sb("rinv", [P, 4])
        top = sb("top", [P, 2])
        neg_top = sb("neg_top", [P, 2])
        neg_lam = sb("neg_lam", [P, DEPTH])
        lam_t = sb("lam_t", [P, 8])
        half_b = sb("half_b", [P, 64])
        banks = [ctx.enter_context(nc.psum_tensor(f"bank{i}", [P, 512], F32)) for i in range(8)]
        b_score, b_turn, b_slab, b_o = banks[4], banks[5], banks[6], banks[7]
        b_ada_ps = banks[4]
        b_rstd, b_ms = banks[5], banks[6]

        def at(o, *shape):
            v = arena[:, o:o + math.prod(shape)]
            if len(shape) == 1:
                return v
            names = "abcd"[:len(shape)]
            return v.rearrange(f"p ({' '.join(names)}) -> p {' '.join(names)}",
                               **{k: n for k, n in zip(names, shape)})

        ada_w = [at(1024 * i, KC, P) for i in range(6)]
        na_in, gqa_in, diff_in, mla_in = at(NA0, 4, 768), at(GQA0, 4, 512), at(DIFF0, 4, 768), at(MLA0, 4, 416)
        kv_up = at(GQA0, 4, 512)
        qT_u, qT_r, kT = at(Q0, 2, 512), at(Q0 + 1024, 2, 256), at(Q0 + 1536, 2, 512)
        prob = at(P0, 512)
        gate_buf = at(P0 + 512, 512)
        probT = at(PT0, 4, P)
        outs = at(OUT0, 4, 256)
        bias_m = at(BM0, 2, LT, 256)
        sq_t = at(TMP0, 512)
        swap_t = at(TMP0 + 512, 256)
        rot_q = at(TMP0 + 768, 2, 256)
        rot_m = at(TMP0 + 768, 2, 384)
        th = at(Q0, 2, 512)
        s_t = at(Q0 + 1024, 512)
        a_t = at(Q0 + 1536, 2, 512)
        n_sq = at(6144, 2, 512)
        n_acc, n_rb, n_t = at(7168, 512), at(7680, 4, P), at(8192, 2, 512)

        def y_of(m, T=NT):
            return arena[:, m * 512:m * 512 + T] if m < 6 else arena[:, BM0 + (m - 6) * 512:BM0 + (m - 6) * 512 + T]

        oT_hi, oT_lo = a_hi[:, 6:8, :], a_lo[:, 6:8, :]
        cT_hi, cT_lo = a_hi[:, 0:3, :], a_lo[:, 0:3, :]

        in_land = sem("in_land"); const_land = sem("const_land"); rpb_land = sem("rpb_land")
        gain_land = sem("gain_land"); bias_land = [sem(f"bias_land{i}") for i in range(2)]
        landed = [sem(f"landed{i}") for i in range(RING)]
        hi_done = sem("hi_done"); lo_done = sem("lo_done"); job_done = sem("job_done"); drained = sem("drained")
        ada_land = [sem(f"ada_land{i}") for i in range(6)]
        ada_done = sem("ada_done"); ada_saved = sem("ada_saved")
        set_turned = sem("set_turned"); set_saved = sem("set_saved")
        cond_th = sem("cond_th"); cond_done = sem("cond_done"); lam_sum = sem("lam_sum"); lam_exp = sem("lam_exp")
        x_done = sem("x_done"); sq_done = sem("sq_done"); acc_done = sem("acc_done"); ms_done = sem("ms_done")
        mv_done = sem("mv_done"); mr_done = sem("mr_done"); rb_done = sem("rb_done"); rstd_done = sem("rstd_done")
        t_done = sem("t_done"); hh_done = sem("hh_done"); h_ready = sem("h_ready")
        th_done = sem("th_done"); ah_done = sem("ah_done"); a_ready = sem("a_ready")
        nv_done = sem("nv_done"); nr_done = sem("nr_done"); normed = sem("normed")
        slab_done = sem("slab_done"); slab_saved = sem("slab_saved"); slab_hi = sem("slab_hi")
        score_done = sem("score_done"); top_done = sem("top_done"); exp_done = sem("exp_done")
        turn_done = sem("turn_done"); turn_saved = sem("turn_saved"); mix_done = sem("mix_done")
        head_done = sem("head_done"); bias_built = sem("bias_built")
        gate_th = sem("gate_th"); y_sum = sem("y_sum"); yh_done = sem("yh_done"); y_ready = sem("y_ready")
        k_built = sem("k_built"); res_saved = sem("res_saved"); table_land = sem("table_land"); out_done = sem("out_done")
        dve_step = sem("dve_step"); pool_step = sem("pool_step")

        NORM_T = {(0, 0): NT, (0, 1): NT, (0, 2): NT, (1, 0): NT, (1, 1): NT, (1, 2): S}
        norm_no = {k: i for i, k in enumerate(sorted(NORM_T))}
        tiles_of = lambda l: TT if l == 0 else LT
        toks_of = lambda l: NT if l == 0 else S
        ffn_T = lambda l, w: S if (l, w) == (1, 1) else NT
        ffn_no = lambda l, w: 2 * l + w

        def ada_per_turn(l, w):
            return 0 if l else (ADA_A if w == 0 else ADA_B)

        ada_j0 = {(0, 0): ADA_PRE, (0, 1): ADA_L + ADA_MID}
        ada_sv0 = {(0, 0): 1, (0, 1): 13}

        def mod(l, i, m=None):
            o = l * ADA_L + i * KC
            return mods[:, o:o + KC, :] if m is None else mods[:, o + m, :]

        def halves(T):
            return [(0, slice(0, S))] + ([(1, slice(S, NT))] if T == NT else [])

        def unit_ap(b, head):
            if b == "na":
                return head // 2, head // 2, 64 * (head % 2), 64
            if b == "gqa":
                return head % 2, 0, 64 * (head // 2), 64
            if b == "diff":
                return head // 4, head // 4, 32 * (head % 4), 32
            return head % 2, head % 2, 0, 96

        def value_ap(b, head, t):
            if b == "na":
                return na_in[:, t, 512 + 64 * head:576 + 64 * head]
            if b == "gqa":
                return gqa_in[:, t, 384 + 64 * (head // 2):448 + 64 * (head // 2)]
            if b == "diff":
                return diff_in[:, t, 512 + 64 * (head // 2):576 + 64 * (head // 2)]
            return kv_up[:, t, 128 * head + 64:128 * head + 128]

        def slab_source(b, what, s, t):
            if b == "na":
                o = (0 if what == "qu" else 256) + 128 * s
                return na_in[:, t, o:o + 128]
            if b == "gqa":
                if what == "k":
                    return gqa_in[:, t, 256:384]
                return (gqa_in if what == "qu" else rot_q)[:, t, 128 * s:128 * s + 128]
            if b == "diff":
                if what == "qr":
                    return rot_q[:, t, 128 * s:128 * s + 128]
                o = (0 if what == "qu" else 256) + 128 * s
                return diff_in[:, t, o:o + 128]
            hh = 2 * int(b[-1]) + s
            if what == "k":
                return diff_in[:, t, 96 * hh:96 * hh + 96]
            return (mla_in if what == "qu" else rot_m)[:, t, 96 * hh:96 * hh + 96]

        def slab_tiles(l, what):
            return {"qu": tiles_of(l), "qr": LT, "k": TT}[what]

        def slab_dest(what, s):
            return {"qu": qT_u, "qr": qT_r, "k": kT}[what][:, s, :]

        def norm_views(name, t):
            def g(o, n, d, rep):
                v = gains[:, o:o + n * d].rearrange("p (n d) -> p n d", n=n)
                return v.unsqueeze(2).broadcast_to([P, n, rep, d])
            if name == "na":
                return [(na_in[:, t, 0:512], 8, 64, (2, 4), g(G_NA, 2, 64, 4))]
            if name == "gqa":
                return [(gqa_in[:, t, 0:384], 6, 64, (3, 2), g(G_GQA, 3, 64, 2))]
            if name == "diff":
                return [(diff_in[:, t, 0:512], 16, 32, (2, 8), g(G_DIFF, 2, 32, 8))]
            if name == "mlac":
                return [(mla_in[:, t, 0:256], 1, 256, (1, 1), g(G_CQ, 1, 256, 1)),
                        (mla_in[:, t, 256:384], 1, 128, (1, 1), g(G_CKV, 1, 128, 1))]
            if name == "mlaqk":
                return [(mla_in[:, t, 0:384], 4, 96, (1, 4), g(G_MQ, 1, 96, 4)),
                        (diff_in[:, t, 0:384], 4, 96, (1, 4), g(G_MK, 1, 96, 4))]
            return [(outs[:, t, :], 4, 64, (1, 4), g(G_SUB, 1, 64, 4))]

        def norm_tiles(name, l):
            return tiles_of(l) if name == "sub" else TT

        def norm_var(name, t):
            o = VAR0[name]
            out = []
            for _, n, *_ in reversed(norm_views(name, t)):
                out.append(var[:, o + t * n:o + t * n + n])
                o += TT * n
            return out[::-1]

        def var_cols(name, l):
            n = sum(v[1] for t in range(norm_tiles(name, l)) for i, v in enumerate(norm_views(name, t))
                    if not skip_part(name, l, t, i))
            return VAR0[name], VAR0[name] + n

        def skip_part(name, l, t, i):
            return name == "mlaqk" and i == 0 and t >= tiles_of(l)

        x_jobs = {norm_no[l, 1]: plan.ffn_n0[l, 0] + 2 * FC + 2 * KC for l in range(DEPTH)}
        x_jobs.update({norm_no[l, 2]: plan.ffn_n0[l, 1] - KC for l in range(DEPTH)})
        x_jobs[norm_no[1, 0]] = plan.ffn_n0[0, 1] + 2 * FC + 2 * KC
        ada_saved_by = [1, 12, 13, 24, 24, 24]

        def shift_no(l, w):
            return l * ADA_L + 3 * w * KC

        def slab_shape(l, s):
            return (96 if s[1].startswith("mla") else P), P * slab_tiles(l, s[2])

        def width(n):
            if n in plan.jobs:
                s = plan.jobs[n]
                if s[0] == "proj":
                    return 2 * CHUNKS[s[1]][1]
                if s[0] == "up":
                    return 768 if s[1] == "q" else 512
                return 256 if s[0] == "branch" else 1024
            for (l, w), n0 in plan.ffn_n0.items():
                for f0, nf in GROUPS:
                    n0 += 2 * nf
                    if n0 <= n < n0 + KC:
                        return nf * P
                    n0 += KC
            return 1024

        gate_no, prev_branch, y_last_job, up_job = {}, {}, {}, {}
        slab_for, o_slab, c_slab, slab_hi_no, rot_free = {}, {}, {}, {}, {}
        normed_for, heads_before, sub_before, head_seq, head_first = {}, {}, {}, {}, {}
        n_head, n_sub, last_branch = 0, 0, 0
        for l, line in enumerate(plan.timelines):
            n_outs = 0
            for rec in line:
                s, kind = rec["step"], rec["kind"]
                if kind == "gate" and s[-1] == 1:
                    gate_no[rec["n"]] = len(gate_no)
                    prev_branch[rec["n"]] = last_branch
                elif kind == "branch":
                    last_branch = y_last_job[l] = rec["n"]
                elif kind == "up":
                    up_job[l] = rec["n"]
                elif kind == "slab":
                    slab_for[l, s[1]] = rec["x"]
                    if s[2] == "qr":
                        after = {"gqa": (l, "diff"), "diff": (l, "mlaqk"), "mla0": None, "mla1": (l + 1, "gqa")}[s[1]]
                        if after:
                            rot_free[after] = rec["x"] + 1
                    if s[1] == "diff":
                        rot_free[l, "mlaqk"] = rec["x"] + 1
                elif kind in ("turn_out", "turn_c"):
                    slab_hi_no[rec["x"]] = len(slab_hi_no)
                    if kind == "turn_c":
                        c_slab[l] = rec["x"]
                    else:
                        o_slab[l, n_outs // 2] = rec["x"]
                        heads_before[rec["x"]] = n_head
                        if n_outs // 2 == 2:
                            sub_before[rec["x"]] = n_sub
                        n_outs += 1
                elif kind == "norm":
                    normed_for[l, s[1]] = rec["v"] + 1
                    if s[1] == "mlaqk":
                        normed_for[l, "mla0"] = normed_for[l, "mla1"] = rec["v"] + 1
                    if s[1] == "sub":
                        n_sub = rec["v"] + 1
                elif kind == "head":
                    head_seq[rec["u"]] = n_head
                    n_head += 1
                elif kind == "score" and s[3] == 0:
                    head_first[rec["u"]] = len(head_first)

        rpb_t = A["na_rpb"].tensor
        block = ctx.enter_context(nc.Block())

        @block.sync
        def _(sp):
            stage_x = at(Q0, 4, D)
            sp.dma_start(stage_x[:, 0:2, :], A["x"][0].rearrange("(t p) d -> p t d", p=P)).then_inc(in_land, 16)
            sp.dma_start(stage_x[:, 2:4, :], A["ctx"][0].rearrange("(t p) d -> p t d", p=P)).then_inc(in_land, 16)

            def load(n, dst, src):
                sp.wait_ge(lo_done, n - RING + 1)
                sp.dma_start(dst, src).then_inc(landed[n % RING], 16)

            def ffn(l, w):
                n0 = plan.ffn_n0[l, w]
                w13 = [A[k][l, w].rearrange("(k p) n -> p k n", p=P) for k in ("ffn_w1", "ffn_w3")]
                w2 = A["ffn_w2"][l, w].rearrange("(k p) n -> p k n", p=P)

                def slot(n, blocks):
                    return w_raw[:, n % RING, 0:blocks * P].rearrange("p (k c) -> p k c", k=blocks)

                for f0, nf in GROUPS:
                    with sp.Fori(0, nf // 2) as i:
                        for j in range(4):
                            sp.wait_ge(lo_done, 4 * i + (n0 + j - RING + 1))
                            sp.dma_start(slot(n0 + j, KC), w13[j % 2][:, :, bass.ds(2 * P * i + (f0 + j // 2) * P, P)])\
                                .then_inc(landed[(n0 + j) % RING], 16)
                    n0 += 2 * nf
                    with sp.Fori(0, KC // 4) as i:
                        for j in range(4):
                            sp.wait_ge(lo_done, 4 * i + (n0 + j - RING + 1))
                            sp.dma_start(slot(n0 + j, nf), w2[:, f0:f0 + nf, bass.ds(4 * P * i + j * P, P)])\
                                .then_inc(landed[(n0 + j) % RING], 16)
                    n0 += KC

            def mixer(l):
                w_in = A["w_in"][l].rearrange("(k p) n -> p k n", p=P)
                w_gate = A["w_gate"][l].rearrange("b (k p) n -> b p k n", p=P)
                w_br = A["w_branch"][l].rearrange("b (k p) n -> b p k n", p=P)
                w_out = A["w_out"][l].rearrange("(k p) n -> p k n", p=P)
                for rec in plan.timelines[l]:
                    s, kind = rec["step"], rec["kind"]
                    if "n" not in rec or (kind != "branch" and s[-1] == 1):
                        continue
                    n = rec["n"]
                    if kind == "proj":
                        c0, cw = CHUNKS[s[1]]
                        src = w_in[:, 2 * s[2]:2 * s[2] + 2, c0:c0 + cw]
                    elif kind == "gate":
                        src = w_gate[s[1]][:, :, s[2] * P:(s[2] + 1) * P]
                    elif kind == "branch":
                        src = w_br[s[1]][:, :, s[2] * P:(s[2] + 1) * P]
                    elif kind == "up" and s[1] == "q":
                        src = A["mla_w_uq"][l].rearrange("(k p) n -> p k n", p=P)
                    elif kind == "up":
                        src = A["mla_w_ukv"][l].rearrange("(k p) n -> p k n", p=P)
                    else:
                        src = w_out[:, :, s[1] * P:(s[1] + 1) * P]
                    k, w = src.shape[1], src.shape[2]
                    load(n, w_raw[:, n % RING, 0:k * w].rearrange("p (k c) -> p k c", k=k), src)

            for l in range(DEPTH):
                ffn(l, 0)
                mixer(l)
                ffn(l, 1)
            sp.wait_ge(res_saved, 4)
            sp.dma_start(out[0].rearrange("(t p) d -> p t d", p=P), at(0, LT, D)).then_inc(out_done, 16)
            sp.wait_ge(out_done, 16)

        @block.gpsimd
        def _(pool):
            ada_src = [A["w_ada"][l].rearrange("(k p) n -> p k n", p=P) for l in range(DEPTH)]
            count = [0]

            def link(ins):
                count[0] += 1
                ins.then_inc(pool_step, 1)
                pool.wait_ge(pool_step, count[0])

            last_user = {}

            def ada_straight(jobs, ring):
                for k, j in enumerate(jobs):
                    slot = k % ring
                    if slot in last_user:
                        pool.wait_ge(ada_done, last_user[slot] + 1)
                    last_user[slot] = j
                    l, jj = divmod(j, ADA_L)
                    pool.dma_start(ada_w[slot], ada_src[l][:, :, jj * P:(jj + 1) * P]).then_inc(ada_land[slot], 16)

            def ada_loops(l, w):
                per, j0 = ada_per_turn(l, w), ada_j0.get((l, w), 0)
                if not per:
                    return
                ada_straight(range(j0, j0 + per), per)
                src, jj = ada_src[j0 // ADA_L], j0 % ADA_L
                with pool.Fori(1, 11) as i:
                    for j in range(per):
                        pool.wait_ge(ada_done, per * i + (j0 + j - per + 1))
                        pool.dma_start(ada_w[j], src[:, :, bass.ds(per * P * i + (jj + j) * P, P)])\
                            .then_inc(ada_land[j], 16)
                for j in range(per):
                    last_user[j] = j0 + 10 * per + j

            pool.dma_start(ident[:, :], A["ident"]).then_inc(const_land, 16)
            stage = at(TMP0, 4, P)
            pool.dma_start(stage[0:48, 0, :], A["norm_g"].rearrange("l w (m p) -> (l w m) p", p=P)).then_inc(const_land, 16)
            pool.dma_start(stage[48:112, 0, :], A["b_gate"].rearrange("l w (m p) -> (l w m) p", p=P)).then_inc(const_land, 16)
            pool.dma_start(stage[112:120, 0, :], A["c"].rearrange("b (m p) -> (b m) p", p=P)).then_inc(const_land, 16)
            pool.dma_start(stage[120:128, 0, :], A["c_ctx"].rearrange("(m p) -> m p", p=P)).then_inc(const_land, 16)
            pool.dma_start(stage[0:ADA_L, 1:3, :], A["b_ada"].rearrange("l (m p) -> m l p", p=P)).then_inc(const_land, 16)
            ada_straight(range(0, 6), 6)
            pool.dma_start(mask[:, :], A["mask"]).then_inc(table_land, 16)
            pool.dma_start(rope[:, :, :], A["rope"].rearrange("(t p) c -> p t c", p=P)).then_inc(table_land, 16)
            lam_s = at(TMP0 + 512, DEPTH, 4, 32)
            pool.dma_start(lam_s, A["diff_lambda"].unsqueeze(0).broadcast_to([P, DEPTH, 4, 32])).then_inc(table_land, 16)
            for k, j in enumerate(range(6, ADA_PRE)):
                slot = j % 6
                pool.wait_ge(ada_done, j - 5)
                last_user[slot] = j
                pool.dma_start(ada_w[slot], ada_src[0][:, :, j * P:(j + 1) * P]).then_inc(ada_land[slot], 16)
            pool.dma_start(scratch, bass.AP(rpb_t, 0, [[0, 64], [1, row]])).then_inc(rpb_land, 16)

            def load_gains(l):
                for o, name in ((G_NA, "na_g_q"), (G_NA + 64, "na_g_k"), (G_GQA, "gqa_g_q"), (G_GQA + 64, "gqa_g_q"),
                                (G_GQA + 128, "gqa_g_k"), (G_DIFF, "diff_g_q"), (G_DIFF + 32, "diff_g_k"),
                                (G_SUB, "diff_g_sub"), (G_CQ, "mla_g_cq"), (G_CKV, "mla_g_ckv"), (G_MQ, "mla_g_q"),
                                (G_MK, "mla_g_k")):
                    v = A[name][l:l + 1, :]
                    pool.dma_start(gains[:, o:o + v.shape[1]], v.broadcast_to([P, v.shape[1]])).then_inc(gain_land, 16)

            def load_bias(l, head):
                for t in range(LT):
                    for r in range(2):
                        o = (l * 4 + head) * RPB + (7 - (2 * t + r)) * 31 + 15
                        src = bass.AP(scratch.tensor, o, [[row - 1, 64], [31, 4], [1, 64]])
                        dst = bias_m[64 * r:64 * r + 64, head % 2, t, :].rearrange("p (a c) -> p a c", a=4)
                        pool.dma_start(dst, src).then_inc(bias_land[head % 2], 16)

            def norm(l, name, v):
                if name == "mlaqk":
                    pool.wait_ge(drained, up_job[l] + 1)
                    pool.wait_ge(slab_done, rot_free[l, "mlaqk"])
                    for t in range(TT):
                        k = diff_in[:, t, 0:384].rearrange("p (h d) -> p h d", h=4)
                        link(pool.tensor_copy(k[:, :, 0:64],
                                              kv_up[:, t, :].rearrange("p (h d) -> p h d", h=4)[:, :, 0:64]))
                        last = pool.tensor_copy(k[:, :, 64:96], mla_in[:, t:t + 1, 384:416].broadcast_to([P, 4, 32]))
                        if t == TT - 1:
                            last.then_inc(k_built, 1)
                        else:
                            link(last)
                pool.wait_ge(nr_done, v + 1)
                for t in range(norm_tiles(name, l)):
                    for i, ((ap, n, d, gd, g), vv) in enumerate(zip(norm_views(name, t), norm_var(name, t))):
                        if skip_part(name, l, t, i):
                            continue
                        x3 = ap.rearrange("p (n d) -> p n d", n=n)
                        link(pool.tensor_tensor(x3, x3, vv.unsqueeze(2).broadcast_to([P, n, d]), ALU.mult))
                        x4 = ap.rearrange("p (a b d) -> p a b d", a=gd[0], b=gd[1])
                        link(pool.tensor_tensor(x4, x4, g, ALU.mult))
                if name in ("gqa", "diff", "mlaqk"):
                    if (l, name) != (0, "gqa"):
                        pool.wait_ge(slab_done, rot_free[l, name])
                    rotate(l, name)
                pool.sem_inc(normed, 1)

            def rotate(l, name):
                for t in range(LT):
                    if name == "mlaqk":
                        heads, d, o = 4, 32, 128
                        k = diff_in[:, t, 0:384].rearrange("p (h d) -> p h d", h=4)[:, :, 64:96]
                        qs = mla_in[:, t, 0:384].rearrange("p (h d) -> p h d", h=4)[:, :, 64:96]
                        q = rot_m[:, t, :].rearrange("p (h d) -> p h d", h=4)
                        link(pool.tensor_copy(rot_m[:, t, :], mla_in[:, t, 0:384]))
                        parts = [(k, k, 4), (qs, q[:, :, 64:96], 4)]
                    elif name == "gqa":
                        d, o = 64, 0
                        parts = [(gqa_in[:, t, 256:384].rearrange("p (h d) -> p h d", h=2),) * 2 + (2,),
                                 (gqa_in[:, t, 0:256].rearrange("p (h d) -> p h d", h=4),
                                  rot_q[:, t, :].rearrange("p (h d) -> p h d", h=4), 4)]
                    else:
                        d, o = 32, 128
                        parts = [(diff_in[:, t, 256:512].rearrange("p (h d) -> p h d", h=8),) * 2 + (8,),
                                 (diff_in[:, t, 0:256].rearrange("p (h d) -> p h d", h=8),
                                  rot_q[:, t, :].rearrange("p (h d) -> p h d", h=8), 8)]
                    cos, sin = rope[:, t, o:o + d], rope[:, t, o + d:o + 2 * d]
                    for src, dst, n in parts:
                        e = d // 4
                        sw = swap_t[:, 0:n * d].rearrange("p (h d) -> p h d", h=n)
                        for half in range(2):
                            for pair in range(2):
                                a, b = (2 * pair + half) * e, (2 * pair + 1 - half) * e
                                link(pool.tensor_tensor(sw[:, :, a:a + e], src[:, :, b:b + e],
                                                        sin[:, a:a + e].unsqueeze(1).broadcast_to([P, n, e]), ALU.mult))
                        link(pool.tensor_tensor(dst, src, cos.unsqueeze(1).broadcast_to([P, n, d]), ALU.mult))
                        link(pool.tensor_tensor(dst, dst, sw, ALU.add))

            load_gains(0)
            pool.wait_ge(table_land, 16 * 3)
            for l in range(DEPTH):
                if l == 0:
                    pool.wait_ge(ada_done, ADA_PRE)
                ada_loops(l, 0)
                if l == 0:
                    pool.wait_ge(ada_done, ADA_L)
                    ada_straight(range(ADA_L, ADA_L + ADA_MID), 6)
                pool.wait_ge(rpb_land, 16)
                pool.wait_ge(gain_land, 16 * 12 * (l + 1))
                load_bias(l, 0)
                load_bias(l, 1)
                for rec in plan.timelines[l]:
                    s = rec["step"]
                    if rec["kind"] == "norm":
                        norm(l, s[1], rec["v"])
                    elif rec["kind"] == "head" and s[1] == "na" and s[2] < 2:
                        pool.wait_ge(mix_done, rec["u"] + 1)
                        load_bias(l, s[2] + 2)
                if l == 0:
                    pool.wait_ge(y_ready, KC * (l + 1))
                    load_gains(1)
                    ada_loops(l, 1)

        @block.scalar
        def _(act):
            def hi_loop(n, i):
                act.wait_ge(landed[n % RING], 16 * i + 16 * (n // RING))
                act.wait_ge(job_done, 4 * i + (n - RING + 1))
                act.activation(w_hi[:, n % RING, :], w_raw[:, n % RING, :], ACT.Copy).then_inc(hi_done, 1)

            def hi_mixed(n):
                if n >= plan.total:
                    return
                act.wait_ge(landed[n % RING], 16 * (n // RING))
                act.wait_ge(job_done, n - RING + 1)
                act.activation(w_hi[:, n % RING, 0:width(n)], w_raw[:, n % RING, 0:width(n)], ACT.Copy).then_inc(hi_done, 1)

            def norm(l, w):
                T, v = NORM_T[l, w], norm_no[l, w]
                for m in range(KC):
                    if v == 0:
                        act.wait_ge(x_done, m + 1)
                    else:
                        act.wait_ge(drained, x_jobs[v] + m + 1)
                    if m >= 3:
                        act.wait_ge(acc_done, (KC - 1) * v + m - 2)
                    dst = n_acc if m == 0 else n_sq[:, m % 2, :]
                    act.activation(dst[:, 0:T], x[:, m, 0:T], ACT.Square).then_inc(sq_done, 1)
                act.wait_ge(mv_done, v + 1)
                act.activation(tok_var[:, 0:T // P], tok_var[:, 0:T // P], ACT.Sqrt).then_inc(mr_done, 1)
                for k in range(KC):
                    act.wait_ge(t_done, KC * v + k + 1)
                    for c, cols in halves(T):
                        last = act.activation(h_hi[:, k, cols], n_t[:, k % 2, cols], ACT.Identity,
                                              bias=mods[:, shift_no(l, w) + k, c:c + 1])
                    last.then_inc(hh_done, 1)

            def ffn(l, w):
                T, n0 = ffn_T(l, w), plan.ffn_n0[l, w]
                a0 = FC * ffn_no(l, w)
                last_group = len(GROUPS) - 1
                for gi, (f0, nf) in enumerate(GROUPS):
                    with act.Fori(0, nf // 2) as i:
                        for j in range(2):
                            n, f = n0 + 2 * j, a0 + f0 + j
                            act.wait_ge(job_done, 4 * i + (n + 1))
                            act.wait_ge(drained, 4 * i + (n - 3))
                            act.activation(th[:, j, 0:T], banks[n % 4][:, 0:T], ACT.Tanh, scale=0.5).then_inc(th_done, 1)
                            hi_loop(n + 4, i)
                            act.wait_ge(drained, 4 * i + (n + 2))
                            act.wait_ge(hi_done, n + 4)
                            act.activation(a_hi[:, bass.ds(2 * i + j, 1), 0:T], a_t[:, j:j + 1, 0:T],
                                           ACT.Copy).then_inc(ah_done, 1)
                            hi_loop(n + 5, i)
                    n0 += 2 * nf
                    final = l == DEPTH - 1 and w == 1 and gi == last_group
                    if gi < last_group:
                        with act.Fori(0, 2) as i:
                            for j in range(4):
                                hi_loop(n0 + j + 4, i)
                    else:
                        for m in range(KC):
                            hi_mixed(n0 + m + 4)
                    n0 += KC

            def mixer(l):
                T, nt = toks_of(l), tiles_of(l)
                for rec in plan.timelines[l]:
                    s, kind = rec["step"], rec["kind"]
                    if kind in ("proj", "up") and s[-1] == 1:
                        hi_mixed(rec["n"] + 4)
                    elif kind == "gate" and s[-1] == 1:
                        n = rec["n"]
                        hi_mixed(n + 4)
                        act.wait_ge(job_done, n + 1)
                        g = gate_no[n]
                        if g >= 1:
                            act.wait_ge(drained, prev_branch[n] + 1)
                        o = l * 32 + s[1] * KC + s[2]
                        act.activation(gate_buf[:, 0:T], banks[n % 4][:, 0:T], ACT.Tanh, scale=0.5,
                                       bias=half_b[:, o:o + 1]).then_inc(gate_th, 1)
                    elif kind == "branch":
                        hi_mixed(rec["n"] + 4)
                        if s[1] == 3 and s[2] < 6:
                            act.wait_ge(y_sum, 24 * l + 16 + s[2] + 1)
                            act.activation(a_hi[:, s[2], 0:T], y_of(s[2], T), ACT.Copy).then_inc(yh_done, 1)
                    elif kind == "y_last":
                        for m in (6, 7):
                            act.wait_ge(y_sum, 24 * l + 16 + m + 1)
                            act.wait_ge(job_done, y_last_job[l] + 1)
                            act.activation(a_hi[:, m, 0:T], y_of(m, T), ACT.Copy).then_inc(yh_done, 1)
                    elif kind == "out" and s[-1] == 1:
                        hi_mixed(rec["n"] + 4)
                    elif kind == "norm":
                        v = rec["v"]
                        act.wait_ge(nv_done, v + 1)
                        o0, o1 = var_cols(s[1], l)
                        act.activation(var[:, o0:o1], var[:, o0:o1], ACT.Sqrt).then_inc(nr_done, 1)
                    elif kind == "score":
                        u = rec["u"]
                        b, head, t = s[1:]
                        keys = NT if t < LT else S
                        act.wait_ge(top_done, u + 1)
                        if u:
                            act.wait_ge(turn_done, u)
                        act.activation(prob[:, 0:keys], b_score[:, 0:keys], ACT.Exp,
                                       bias=neg_top[:, u % 2:u % 2 + 1], scale=SCALE[b],
                                       accum_out=rowsum[:, head % 2, t:t + 1]).then_inc(exp_done, 1)
                    elif kind == "turn" and rec["u"] % 2 == 1:
                        u = rec["u"]
                        keys = NT if s[3] < LT else S
                        act.wait_ge(turn_done, u + 1)
                        act.wait_ge(mix_done, u)
                        act.activation(arena[:, PT0:PT0 + keys], b_turn[:, 0:keys], ACT.Copy).then_inc(turn_saved, 1)
                    elif kind == "slab" and rec["x"] % 2 == 1:
                        act.wait_ge(slab_done, rec["x"] + 1)
                        w_, n_ = slab_shape(l, s)
                        act.activation(slab_dest(s[2], s[3])[0:w_, 0:n_], b_slab[0:w_, 0:n_], ACT.Copy)\
                           .then_inc(slab_saved, 1)
                    elif kind == "turn_out":
                        act.wait_ge(slab_done, rec["x"] + 1)
                        act.activation(oT_hi[:, s[1], 0:T], b_slab[:, 0:T], ACT.Copy).then_inc(slab_hi, 1)
                    elif kind == "turn_c":
                        act.wait_ge(slab_done, rec["x"] + 1)
                        act.activation(cT_hi[:, s[1], :], b_slab[:, :], ACT.Copy).then_inc(slab_hi, 1)

            act.wait_ge(set_saved, 2)
            act.activation(n_sq[:, 0, 0:16], vecs[:, 112:128], ACT.Tanh, scale=0.5).then_inc(cond_th, 1)
            act.wait_ge(lam_sum, 1)
            act.activation(lam_t[:, 0:4], lam_t[:, 0:4], ACT.Exp).then_inc(lam_exp, 1)
            act.sem_inc(hi_done, RING)
            for n in range(RING, 2 * RING):
                hi_mixed(n)
            for l in range(DEPTH):
                norm(l, 0)
                ffn(l, 0)
                norm(l, 1)
                mixer(l)
                norm(l, 2)
                ffn(l, 1)

        @block.vector
        def _(dve):
            count = [0]

            def link(ins):
                count[0] += 1
                ins.then_inc(dve_step, 1)
                dve.wait_ge(dve_step, count[0])

            def lo(n, w=1024):
                dve.wait_ge(hi_done, n + 1)
                dve.tensor_tensor(w_lo[:, n % RING, 0:w], w_raw[:, n % RING, 0:w], w_hi[:, n % RING, 0:w].bitcast(F32),
                                  ALU.subtract).then_inc(lo_done, 1)

            def lo_loop(n, i):
                dve.wait_ge(hi_done, 4 * i + (n + 1))
                dve.tensor_tensor(w_lo[:, n % RING, :], w_raw[:, n % RING, :], w_hi[:, n % RING, :].bitcast(F32),
                                  ALU.subtract).then_inc(lo_done, 1)

            def lo_mixed(n):
                if n < plan.total:
                    lo(n, width(n))

            def ada_save(j0, cnt, i=None, per=0, done=None):
                if i is None:
                    dve.wait_ge(ada_done, j0 + cnt)
                    dst, bia = mods[:, j0:j0 + cnt, :], b_ada[:, j0:j0 + cnt]
                else:
                    dve.wait_ge(ada_done, per * i + (j0 + cnt))
                    dst, bia = mods[:, bass.ds(per * i + j0, cnt), :], b_ada[:, bass.ds(per * i + j0, cnt)]
                dve.tensor_tensor(dst, b_ada_ps[:, 0:2 * cnt].rearrange("p (j c) -> p j c", c=2),
                                  bia.unsqueeze(2).broadcast_to([P, cnt, 2]), ALU.add).then_inc(ada_saved, 1)

            def norm(l, w):
                T, v = NORM_T[l, w], norm_no[l, w]
                ntile = T // P
                g0 = l * 24 + w * KC
                sc, gt = shift_no(l, w) + KC, shift_no(l, w) + 2 * KC
                if v == 1:
                    ada_save(ADA_L, ADA_MID)
                dve.wait_ge(ada_saved, ada_saved_by[v])
                link(dve.scalar_tensor_tensor(scale_g[:, :, :], mods[:, sc:sc + KC, :], 1.0,
                                              vecs[:, g0:g0 + KC].unsqueeze(2).broadcast_to([P, KC, 2]), ALU.add, ALU.mult))
                for m in range(1, KC):
                    dve.wait_ge(sq_done, KC * v + m + 1)
                    if m >= 2:
                        dve.wait_ge(acc_done, (KC - 1) * v + m - 1)
                    dve.tensor_tensor(n_acc[:, 0:T], n_acc[:, 0:T], n_sq[:, m % 2, 0:T], ALU.add).then_inc(acc_done, 1)
                dve.wait_ge(ms_done, v + 1)
                link(dve.tensor_scalar(tok_var[:, 0:ntile], b_ms[:, 0:2 * ntile:2], EPS, None, ALU.add))
                dve.reciprocal(tok_var[:, 0:ntile], tok_var[:, 0:ntile]).then_inc(mv_done, 1)
                dve.wait_ge(mr_done, v + 1)
                dve.tensor_copy(n_rb[:, 0:ntile, :], tok_var[:, 0:ntile].unsqueeze(2).broadcast_to([P, ntile, P]))\
                    .then_inc(rb_done, 1)
                dve.wait_ge(rstd_done, v + 1)

                def times(k):
                    if k >= 2:
                        dve.wait_ge(h_ready, KC * v + k - 1)
                    for c, cols in halves(T):
                        last = dve.scalar_tensor_tensor(n_t[:, k % 2, cols], x[:, k, cols], scale_g[:, k, c:c + 1],
                                                        b_rstd[:, cols], ALU.mult, ALU.mult)
                    last.then_inc(t_done, 1)

                def rest(k):
                    dve.wait_ge(hh_done, KC * v + k + 1)
                    for c, cols in halves(T):
                        last = dve.scalar_tensor_tensor(h_lo[:, k, cols], n_t[:, k % 2, cols],
                                                        mods[:, shift_no(l, w) + k, c:c + 1],
                                                        h_hi[:, k, cols].bitcast(F32), ALU.add, ALU.subtract)
                    last.then_inc(h_ready, 1)

                for k in range(KC + 1):
                    if k < KC:
                        times(k)
                    if k:
                        rest(k - 1)

            def gates(l, w):
                gt = shift_no(l, w) + 2 * KC
                link(dve.tensor_scalar(gate_s[:, :, :], mods[:, gt:gt + KC, :], 0.5 if w == 1 else 0.25, None, ALU.mult))

            def ffn(l, w):
                T, n0 = ffn_T(l, w), plan.ffn_n0[l, w]
                a0 = FC * ffn_no(l, w)
                per = ada_per_turn(l, w)
                turns = 0
                for gi, (f0, nf) in enumerate(GROUPS):
                    with dve.Fori(0, nf // 2) as i:
                        for j in range(2):
                            n, f = n0 + 2 * j, a0 + f0 + j
                            dve.wait_ge(th_done, 2 * i + (f + 1))
                            dve.scalar_tensor_tensor(s_t[:, 0:T], th[:, j, 0:T], 1.0, banks[n % 4][:, 0:T],
                                                     ALU.add, ALU.mult).then_inc(drained, 1)
                            lo_loop(n + 4, i)
                            dve.wait_ge(drained, 4 * i + (n + 1))
                            dve.wait_ge(job_done, 4 * i + (n + 2))
                            dve.tensor_tensor(a_t[:, j, 0:T], s_t[:, 0:T], banks[(n + 1) % 4][:, 0:T],
                                              ALU.mult).then_inc(drained, 1)
                            dve.wait_ge(ah_done, 2 * i + (f + 1))
                            dve.tensor_tensor(a_lo[:, bass.ds(2 * i + j, 1), 0:T], a_t[:, j:j + 1, 0:T],
                                              a_hi[:, bass.ds(2 * i + j, 1), 0:T].bitcast(F32),
                                              ALU.subtract).then_inc(a_ready, 1)
                            lo_loop(n + 5, i)
                        if per:
                            ada_save(ada_j0[l, w] + per * turns, per, i, per)
                    turns += nf // 2
                    if gi == 0:
                        if (l, w) == (0, 0):
                            dve.wait_ge(ada_saved, ada_sv0[l, w] + turns)
                        gates(l, 0 if w == 0 else 2)
                    n0 += 2 * nf

                    if gi < len(GROUPS) - 1:
                        with dve.Fori(0, 2) as i:
                            for j in range(4):
                                n = n0 + j
                                dve.wait_ge(job_done, 4 * i + (n + 1))
                                for c, cols in halves(T):
                                    xs = x[:, bass.ds(4 * i + j, 1), cols]
                                    last = dve.scalar_tensor_tensor(
                                        xs, banks[n % 4][:, cols].unsqueeze(1), gate_s[:, bass.ds(4 * i + j, 1), c],
                                        xs, ALU.mult, ALU.add)
                                last.then_inc(drained, 1)
                                lo_loop(n + 4, i)
                    else:
                        for m in range(KC):
                            n = n0 + m
                            dve.wait_ge(job_done, n + 1)
                            for c, cols in halves(T):
                                last = dve.scalar_tensor_tensor(x[:, m, cols], banks[n % 4][:, cols],
                                                                gate_s[:, m, c:c + 1], x[:, m, cols], ALU.mult, ALU.add)
                            last.then_inc(drained, 1)
                            lo_mixed(n + 4)
                    n0 += KC

            def mixer(l):
                T, nt = toks_of(l), tiles_of(l)
                for rec in plan.timelines[l]:
                    s, kind = rec["step"], rec["kind"]
                    if kind == "gain":
                        dve.wait_ge(gain_land, 16 * 12 * (l + 1))
                        g = gains[:, G_SUB:G_SUB + 64]
                        link(dve.tensor_scalar(g, g, 1.0 - LAM_INIT[l], None, ALU.mult))
                        gates(l, 1)
                    elif kind == "proj" and s[-1] == 1:
                        n, c = rec["n"], s[1]
                        if s[2] == 3:
                            dve.wait_ge(job_done, n + 1)
                            c0, cw = CHUNKS[c]
                            first = n - 3
                            for t in range(TT):
                                for a, b, base, width_ in SEGMENTS:
                                    u, v = max(a, c0), min(b, c0 + cw)
                                    if u < v:
                                        o = base + t * width_ + u - a
                                        dst, src = arena[:, o:o + v - u], banks[(first + t) % 4][:, u - c0:v - c0]
                                        if base == GQA0 and c == 1:
                                            dst = dst.rearrange("p (r g d) -> p r g d", r=2, g=2)
                                            src = src.rearrange("p (g r d) -> p r g d", r=2, g=2)
                                        last = dve.tensor_copy(dst, src)
                                last.then_inc(drained, 1)
                        lo_mixed(n + 4)
                    elif kind == "up" and s[-1] == 1:
                        n = rec["n"]
                        dve.wait_ge(job_done, n + 1)
                        for t in range(nt if s[1] == "q" else TT):
                            dst = mla_in[:, t, 0:384] if s[1] == "q" else kv_up[:, t, :]
                            last = dve.tensor_copy(dst, banks[t][:, 0:dst.shape[1]])
                        last.then_inc(drained, 1)
                        lo_mixed(n + 4)
                    elif kind == "gate" and s[-1] == 1:
                        lo_mixed(rec["n"] + 4)
                    elif kind == "branch":
                        n, b, m = rec["n"], s[1], s[2]
                        dve.wait_ge(gate_th, gate_no[n - 1] + 1)
                        dve.wait_ge(job_done, n + 1)
                        y = y_of(m, T)
                        if b == 0:
                            dve.scalar_tensor_tensor(y, gate_buf[:, 0:T], 1.0, banks[n % 4][:, 0:T], ALU.add, ALU.mult)\
                               .then_inc(drained, 2)
                        else:
                            dve.scalar_tensor_tensor(sq_t[:, 0:T], gate_buf[:, 0:T], 1.0, banks[n % 4][:, 0:T],
                                                     ALU.add, ALU.mult).then_inc(drained, 2)
                            dve.wait_ge(drained, n + 1)
                            dve.tensor_tensor(y, y, sq_t[:, 0:T], ALU.add).then_inc(y_sum, 1)
                        lo_mixed(n + 4)
                        if b:
                            dve.wait_ge(y_sum, 24 * l + 8 * (b - 1) + m + 1)
                        if b == 3 and m < 6:
                            y_low(l, m, T)
                    elif kind == "y_last":
                        y_low(l, 6, T)
                        y_low(l, 7, T)
                    elif kind == "out" and s[-1] == 1:
                        n, m = rec["n"], s[1]
                        dve.wait_ge(job_done, n + 1)
                        for c, cols in halves(T):
                            last = dve.scalar_tensor_tensor(x[:, m, cols], banks[n % 4][:, cols],
                                                            gate_s[:, m, c:c + 1], x[:, m, cols], ALU.mult, ALU.add)
                        last.then_inc(drained, 1)
                        lo_mixed(n + 4)
                    elif kind == "norm":
                        head_norm(l, s[1], rec["v"])
                    elif kind == "score":
                        u = rec["u"]
                        b, head, t = s[1:]
                        keys = NT if t < LT else S
                        dve.wait_ge(score_done, u + 1)
                        link(dve.reduce_max(top[:, u % 2:u % 2 + 1], b_score[:, 0:keys], AX_X))
                        dve.tensor_scalar(neg_top[:, u % 2:u % 2 + 1], top[:, u % 2:u % 2 + 1], -SCALE[b], None,
                                          ALU.mult).then_inc(top_done, 1)
                    elif kind == "turn" and rec["u"] % 2 == 0:
                        u = rec["u"]
                        keys = NT if s[3] < LT else S
                        dve.wait_ge(turn_done, u + 1)
                        if u:
                            dve.wait_ge(mix_done, u)
                        dve.tensor_copy(arena[:, PT0:PT0 + keys], b_turn[:, 0:keys]).then_inc(turn_saved, 1)
                    elif kind == "head":
                        head_out(l, s[1], s[2], rec["u"])
                    elif kind == "slab" and rec["x"] % 2 == 0:
                        dve.wait_ge(slab_done, rec["x"] + 1)
                        w_, n_ = slab_shape(l, s)
                        dve.tensor_copy(slab_dest(s[2], s[3])[0:w_, 0:n_], b_slab[0:w_, 0:n_]).then_inc(slab_saved, 1)
                    elif kind in ("turn_out", "turn_c"):
                        dve.wait_ge(slab_hi, slab_hi_no[rec["x"]] + 1)
                        dst, hi_ = (oT_lo, oT_hi) if kind == "turn_out" else (cT_lo, cT_hi)
                        W = T if kind == "turn_out" else NT
                        dve.tensor_tensor(dst[:, s[1], 0:W], b_slab[:, 0:W], hi_[:, s[1], 0:W].bitcast(F32),
                                          ALU.subtract).then_inc(slab_saved, 1)
                    if kind == "slab" and s[1] == "na" and s[2:] == ("qu", 0):
                        build_bias(l, 0)
                        build_bias(l, 1)
                    if kind == "score" and s[1] == "na" and s[2] in (1, 2) and s[3] == nt - 1:
                        build_bias(l, s[2] + 1)

            def build_bias(l, head):
                dve.wait_ge(bias_land[head % 2], 64 * (2 * l + head // 2 + 1))
                for t in range(LT):
                    v = bias_m[:, head % 2, t, :].rearrange("p (a c) -> p a c", a=4)
                    last = dve.scalar_tensor_tensor(v, v, 1.0 / SCALE["na"], mask[:, :].unsqueeze(1).broadcast_to([P, 4, 64]),
                                                    ALU.mult, ALU.add)
                last.then_inc(bias_built, 1)

            def y_low(l, m, T):
                dve.wait_ge(yh_done, 8 * l + m + 1)
                dve.tensor_tensor(a_lo[:, m, 0:T], y_of(m, T), a_hi[:, m, 0:T].bitcast(F32), ALU.subtract)\
                   .then_inc(y_ready, 1)

            def head_norm(l, name, v):
                if name == "mlaqk":
                    dve.wait_ge(k_built, l + 1)
                for t in range(norm_tiles(name, l)):
                    for i, ((ap, n, d, gd, g), vv) in enumerate(zip(norm_views(name, t), norm_var(name, t))):
                        if skip_part(name, l, t, i):
                            continue
                        sq = sq_t[:, 0:n * d]
                        link(dve.tensor_tensor(sq, ap, ap, ALU.mult))
                        link(dve.tensor_reduce(vv, sq.rearrange("p (n d) -> p n d", n=n), AX_X, ALU.add))
                        link(dve.tensor_scalar(vv, vv, 1.0 / d, EPS, ALU.mult, ALU.add))
                o0, o1 = var_cols(name, l)
                dve.reciprocal(var[:, o0:o1], var[:, o0:o1]).then_inc(nv_done, 1)

            def head_out(l, b, head, u):
                nt = tiles_of(l)
                dve.wait_ge(mix_done, u + 1)
                link(dve.reciprocal(rinv[:, 0:nt], rowsum[:, head % 2, 0:nt]))
                o = b_o[:, 0:nt * 64].rearrange("p (t d) -> p t d", t=nt)
                if b == "diff":
                    dst = outs[:, 0:nt, 64 * (head // 2):64 * (head // 2) + 64]
                    if head % 2:
                        link(dve.tensor_scalar(rinv[:, 0:nt], rinv[:, 0:nt], neg_lam[:, l:l + 1], None, ALU.mult))
                        for t in range(nt):
                            last = dve.scalar_tensor_tensor(dst[:, t, :], o[:, t, :], rinv[:, t:t + 1], dst[:, t, :],
                                                            ALU.mult, ALU.add)
                        last.then_inc(head_done, 1)
                        dve.wait_ge(head_done, head_seq[u] + 1)
                        return
                else:
                    dst = outs[:, 0:nt, 64 * head:64 * head + 64]
                dve.tensor_tensor(dst, o, rinv[:, 0:nt].unsqueeze(2).broadcast_to([P, nt, 64]), ALU.mult)\
                    .then_inc(head_done, 1)
                dve.wait_ge(head_done, head_seq[u] + 1)

            dve.sem_inc(drained, RING)
            dve.sem_inc(lo_done, RING)
            dve.memset(mean[:, :], 1.0 / D).then_inc(set_saved, 1)
            dve.wait_ge(set_turned, 1)
            dve.tensor_copy(vecs[:, :], b_slab[:, 0:P]).then_inc(set_saved, 1)
            for g in range(2):
                last = dve.tensor_copy(b_ada[:, g * ADA_L:(g + 1) * ADA_L], b_slab[:, P + g * P:P + g * P + ADA_L])
            link(last)
            dve.wait_ge(cond_th, 1)
            for c in range(2):
                last = dve.scalar_tensor_tensor(cond[:, :, c], n_sq[:, 0, 8 * c:8 * c + 8], 1.0,
                                                vecs[:, 112 + 8 * c:120 + 8 * c], ALU.add, ALU.mult)
            link(last)
            dve.tensor_scalar(cond[:, :, :], cond[:, :, :], 0.5, None, ALU.mult).then_inc(cond_done, 1)
            dve.tensor_scalar(half_b[:, :], vecs[:, 48:112], 0.5, None, ALU.mult).then_inc(cond_done, 1)
            dve.wait_ge(table_land, 16 * 3)
            lam_s = at(TMP0 + 512, DEPTH, 4, 32)
            for l in range(DEPTH):
                link(dve.tensor_tensor(n_t[:, 0, 0:64].rearrange("p (a d) -> p a d", a=2), lam_s[:, l, 0:4:2, :],
                                       lam_s[:, l, 1:4:2, :], ALU.mult))
                link(dve.tensor_reduce(lam_t[:, 2 * l:2 * l + 2], n_t[:, 0, 0:64].rearrange("p (a d) -> p a d", a=2),
                                       AX_X, ALU.add))
            dve.sem_inc(lam_sum, 1)
            dve.wait_ge(lam_exp, 1)
            for l in range(DEPTH):
                link(dve.tensor_tensor(neg_lam[:, l:l + 1], lam_t[:, 2 * l + 1:2 * l + 2], lam_t[:, 2 * l:2 * l + 1],
                                       ALU.subtract))
                link(dve.tensor_scalar(neg_lam[:, l:l + 1], neg_lam[:, l:l + 1], -LAM_INIT[l], None, ALU.add))
            for m in range(KC):
                dve.wait_ge(set_turned, m + 2)
                dve.tensor_copy(x[:, m, :], banks[m % 4][:, :]).then_inc(x_done, 1)
            for n in range(RING, 2 * RING):
                lo(n)
            ada_save(0, ADA_PRE)
            for l in range(DEPTH):
                norm(l, 0)
                ffn(l, 0)
                norm(l, 1)
                mixer(l)
                norm(l, 2)
                ffn(l, 1)
            res = at(0, LT, D)
            for g in range(4):
                dve.wait_ge(set_turned, 10 + g)
                dve.tensor_copy(res[:, g // 2, 512 * (g % 2):512 * (g % 2) + 512], banks[g][:, :]).then_inc(res_saved, 1)

        @block.tensor
        def _(pe):
            def block_products(out_ap, wh, wl, xh, xl, first, last):
                pe.matmul(out_ap, wh, xh, start=first, stop=False)
                pe.matmul(out_ap, wh, xl, start=False, stop=False)
                return pe.matmul(out_ap, wl, xh, start=False, stop=last)

            def wblock(w, n, k, width_=P):
                return w[:, n % RING, k * width_:(k + 1) * width_]

            def ada_job(slot, col, land):
                pe.wait_ge(ada_land[slot], land)
                for k in range(KC):
                    last = pe.matmul(b_ada_ps[:, 2 * col:2 * col + 2], ada_w[slot][:, k, :], cond[:, k, :],
                                     start=(k == 0), stop=(k == KC - 1))
                last.then_inc(ada_done, 1)

            ada_lands = {}

            def ada_straight(slots):
                for col, slot in enumerate(slots):
                    ada_lands[slot] = ada_lands.get(slot, 0) + 16
                    ada_job(slot, col, ada_lands[slot])

            def norm(l, w):
                T, v = NORM_T[l, w], norm_no[l, w]
                pe.wait_ge(acc_done, (KC - 1) * (v + 1))
                for t in range(T // P):
                    last = pe.matmul(b_ms[:, 2 * t:2 * t + 2], n_acc[:, t * P:(t + 1) * P], mean[:, :], start=True, stop=True)
                last.then_inc(ms_done, 1)
                pe.wait_ge(rb_done, v + 1)
                for t in range(T // P):
                    last = pe.matmul(b_rstd[:, t * P:(t + 1) * P], n_rb[:, t, :], ident[:, :], start=True, stop=True)
                last.then_inc(rstd_done, 1)

            def ffn(l, w):
                T, n0 = ffn_T(l, w), plan.ffn_n0[l, w]
                v = norm_no[l, 0 if w == 0 else 2]
                a0 = FC * ffn_no(l, w)
                per = ada_per_turn(l, w)
                j0 = ada_j0.get((l, w), 0)
                after = {0: [0] * 4, 5: [1, 1, 1, 2], 6: [1, 2, 1, 2]}[per]
                turns = 0
                for gi, (f0, nf) in enumerate(GROUPS):
                    with pe.Fori(0, nf // 2) as i:
                        slot = 0
                        for j in range(4):
                            n = n0 + j
                            pe.wait_ge(lo_done, 4 * i + (n + 1))
                            pe.wait_ge(drained, 4 * i + (n - 3))
                            for k in range(KC):
                                if gi == 0 and j == 0:
                                    pe.wait_ge(h_ready, KC * v + k + 1)
                                last = block_products(banks[n % 4][:, 0:T], wblock(w_hi, n, k), wblock(w_lo, n, k),
                                                      h_hi[:, k, 0:T], h_lo[:, k, 0:T], k == 0, k == KC - 1)
                            last.then_inc(job_done, 1)
                            for _ in range(after[j]):
                                if slot == 0:
                                    pe.wait_ge(ada_saved, 1 * i + (ada_sv0[l, w] + turns))
                                ada_job(slot, slot, 16 * i + (ada_lands.get(slot, 0) + 16))
                                slot += 1
                    for q in range(per):
                        ada_lands[q] = ada_lands.get(q, 0) + 16 * (nf // 2)
                    turns += nf // 2
                    n0 += 2 * nf

                    def down(n, i=None):
                        if i is None:
                            pe.wait_ge(lo_done, n + 1)
                            pe.wait_ge(drained, n - 3)
                        else:
                            pe.wait_ge(lo_done, 4 * i + (n + 1))
                            pe.wait_ge(drained, 4 * i + (n - 3))
                        for k in range(nf):
                            if (n - n0) % 4 == 0:
                                pe.wait_ge(a_ready, a0 + f0 + k + 1)
                            last = block_products(banks[n % 4][:, 0:T], wblock(w_hi, n, k), wblock(w_lo, n, k),
                                                  a_hi[:, k, 0:T], a_lo[:, k, 0:T], k == 0, k == nf - 1)
                        last.then_inc(job_done, 1)

                    with pe.Fori(0, KC // 4) as i:
                        for j in range(4):
                            down(n0 + j, i)
                    n0 += KC

            def mixer(l):
                T, nt = toks_of(l), tiles_of(l)
                v = norm_no[l, 1]
                for rec in plan.timelines[l]:
                    s, kind = rec["step"], rec["kind"]
                    if kind == "proj":
                        n, c, kp, half = rec["n"], s[1], s[2], s[3]
                        first = n - kp
                        cw = CHUNKS[c][1]
                        if half == 0:
                            pe.wait_ge(lo_done, n + 1)
                        for t in (2 * half, 2 * half + 1):
                            if kp == 0:
                                pe.wait_ge(drained, first + t - 3)
                            for kk in range(2):
                                k = 2 * kp + kk
                                if c == 0 and t == 0:
                                    pe.wait_ge(h_ready, KC * v + k + 1)
                                o = banks[(first + t) % 4][:, 0:cw]
                                toks = slice(t * P, (t + 1) * P)
                                wh = w_hi[:, n % RING, kk * cw:(kk + 1) * cw]
                                wl = w_lo[:, n % RING, kk * cw:(kk + 1) * cw]
                                pe.matmul(o, h_hi[:, k, toks], wh, start=(k == 0), stop=False)
                                pe.matmul(o, h_hi[:, k, toks], wl, start=False, stop=False)
                                last = pe.matmul(o, h_lo[:, k, toks], wh, start=False, stop=(k == KC - 1))
                        if half == 1:
                            last.then_inc(job_done, 1)
                    elif kind == "up":
                        if s[-1] == 1:
                            continue
                        n = rec["n"]
                        pe.wait_ge(lo_done, n + 1)
                        pe.wait_ge(drained, n)
                        pe.wait_ge(slab_saved, c_slab[l] + 1)
                        ks, cw = ([0, 1], 384) if s[1] == "q" else ([2], 512)
                        for t in range(nt if s[1] == "q" else TT):
                            toks = slice(t * P, (t + 1) * P)
                            for q, k in enumerate(ks):
                                o = banks[t][:, 0:cw]
                                wh, wl = (w_[:, n % RING, q * cw:(q + 1) * cw] for w_ in (w_hi, w_lo))
                                pe.matmul(o, cT_hi[:, k, toks], wh, start=(q == 0), stop=False)
                                pe.matmul(o, cT_hi[:, k, toks], wl, start=False, stop=False)
                                last = pe.matmul(o, cT_lo[:, k, toks], wh, start=False, stop=(q == len(ks) - 1))
                        last.then_inc(job_done, 1)
                    elif kind in ("gate", "out"):
                        n, half = rec["n"], s[-1]
                        if half == 0:
                            pe.wait_ge(lo_done, n + 1)
                            pe.wait_ge(drained, plan.need_drained[n])
                        src_hi, src_lo = (h_hi, h_lo) if kind == "gate" else (a_hi, a_lo)
                        for k in range(4 * half, 4 * half + 4):
                            if kind == "out" and s[1] == 0:
                                pe.wait_ge(y_ready, KC * l + k + 1)
                            last = block_products(banks[n % 4][:, 0:T], wblock(w_hi, n, k), wblock(w_lo, n, k),
                                                  src_hi[:, k, 0:T], src_lo[:, k, 0:T], k == 0, k == KC - 1)
                        if half == 1:
                            last.then_inc(job_done, 1)
                    elif kind == "branch":
                        n = rec["n"]
                        pe.wait_ge(lo_done, n + 1)
                        pe.wait_ge(drained, plan.need_drained[n])
                        pe.wait_ge(slab_saved, o_slab[l, s[1]] + 1)
                        for k in range(2):
                            last = block_products(banks[n % 4][:, 0:T], wblock(w_hi, n, k), wblock(w_lo, n, k),
                                                  oT_hi[:, k, 0:T], oT_lo[:, k, 0:T], k == 0, k == 1)
                        last.then_inc(job_done, 1)
                    elif kind in ("slab", "turn_out", "turn_c"):
                        xno = rec["x"]
                        if kind == "slab":
                            pe.wait_ge(normed, normed_for[l, s[1]])
                            tiles = slab_tiles(l, s[2])
                            srcs = [slab_source(s[1], s[2], s[3], t) for t in range(tiles)]
                        elif kind == "turn_out":
                            pe.wait_ge(head_done, heads_before[xno])
                            if xno in sub_before:
                                pe.wait_ge(normed, sub_before[xno])
                            srcs = [outs[:, t, s[1] * P:(s[1] + 1) * P] for t in range(nt)]
                        else:
                            pe.wait_ge(normed, normed_for[l, "mlac"])
                            srcs = [mla_in[:, t, s[1] * P:(s[1] + 1) * P] for t in range(TT)]
                        if xno:
                            pe.wait_ge(slab_saved, xno)
                        for t, src in enumerate(srcs):
                            w_ = math.prod(src.shape[1:])
                            last = pe.transpose(b_slab[0:w_, t * P:(t + 1) * P], src, ident[:, :])
                        last.then_inc(slab_done, 1)
                    elif kind == "score":
                        u = rec["u"]
                        b, head, t = s[1:]
                        sq, sk, p0, d = unit_ap(b, head)
                        pe.wait_ge(slab_saved, slab_for[l, b] + 1)
                        if u:
                            pe.wait_ge(exp_done, u)
                        rows = slice(p0, p0 + d)
                        toks = slice(t * P, (t + 1) * P)
                        qu = qT_u[rows, sq, toks]
                        if t >= LT:
                            last = pe.matmul(b_score[:, 0:S], qu, kT[rows, sk, S:NT], start=True, stop=True)
                        elif b == "na":
                            pe.wait_ge(bias_built, 4 * l + head + 1)
                            pe.matmul(b_score[:, 0:S], qu, kT[rows, sk, 0:S], start=True, stop=False)
                            pe.matmul(b_score[:, 0:S], ident[:, :], bias_m[:, head % 2, t, :], start=False, stop=True)
                            last = pe.matmul(b_score[:, S:NT], qu, kT[rows, sk, S:NT], start=True, stop=True)
                        else:
                            pe.matmul(b_score[:, 0:S], qT_r[rows, sq, toks], kT[rows, sk, 0:S], start=True, stop=True)
                            last = pe.matmul(b_score[:, S:NT], qu, kT[rows, sk, S:NT], start=True, stop=True)
                        last.then_inc(score_done, 1)
                    elif kind == "turn":
                        u, t = rec["u"], s[3]
                        pe.wait_ge(exp_done, u + 1)
                        if u:
                            pe.wait_ge(turn_saved, u)
                        for q in range(4 if t < LT else 2):
                            last = pe.transpose(b_turn[:, q * P:(q + 1) * P], prob[:, q * P:(q + 1) * P], ident[:, :])
                        last.then_inc(turn_done, 1)
                    elif kind == "mix":
                        u = rec["u"]
                        b, head, t = s[1:]
                        pe.wait_ge(turn_saved, u + 1)
                        if t == 0 and head_first[u]:
                            pe.wait_ge(head_done, head_first[u])
                        tiles = range(TT) if t < LT else range(LT, TT)
                        for q, kt in enumerate(tiles):
                            last = pe.matmul(b_o[:, 64 * t:64 * t + 64], probT[:, q, :], value_ap(b, head, kt),
                                             start=(q == 0), stop=(q == len(tiles) - 1))
                        last.then_inc(mix_done, 1)

            pe.sem_inc(job_done, RING)
            stage = at(TMP0, 4, P)
            stage_x = at(Q0, 4, D)
            pe.wait_ge(const_land, 16 * 6)
            pe.transpose(b_slab[:, 0:P], stage[:, 0, :], ident[:, :])
            for g in range(2):
                last = pe.transpose(b_slab[:, P + g * P:P + g * P + ADA_L], stage[0:ADA_L, 1 + g, :],
                                    ident[0:ADA_L, 0:ADA_L])
            last.then_inc(set_turned, 1)
            pe.wait_ge(in_land, 32)
            for m in range(KC):
                if m >= 4:
                    pe.wait_ge(x_done, m - 3)
                for t in range(TT):
                    last = pe.transpose(banks[m % 4][:, t * P:(t + 1) * P], stage_x[:, t, m * P:(m + 1) * P], ident[:, :])
                last.then_inc(set_turned, 1)
            pe.wait_ge(cond_done, 1)
            ada_straight([j % 6 for j in range(ADA_PRE)])
            pe.wait_ge(set_saved, 1)
            for l in range(DEPTH):
                norm(l, 0)
                ffn(l, 0)
                if l == 0:
                    pe.wait_ge(ada_saved, 12)
                    ada_straight(range(ADA_MID))
                norm(l, 1)
                mixer(l)
                norm(l, 2)
                ffn(l, 1)
            for g in range(4):
                t, half = g // 2, g % 2
                pe.wait_ge(drained, plan.total)
                for q in range(4):
                    last = pe.transpose(banks[g][:, q * P:(q + 1) * P], x[:, 4 * half + q, t * P:(t + 1) * P], ident[:, :])
                last.then_inc(set_turned, 1)


_INS = ["x", "c", "ctx", "c_ctx", "w_ada", "b_ada", "norm_g", "ffn_w1", "ffn_w3", "ffn_w2", "w_in", "na_g_q", "na_g_k",
        "na_rpb", "gqa_g_q", "gqa_g_k", "diff_g_q", "diff_g_k", "diff_lambda", "diff_g_sub", "mla_g_cq", "mla_g_ckv",
        "mla_w_uq", "mla_w_ukv", "mla_g_q", "mla_g_k", "w_gate", "b_gate", "w_branch", "w_out"]


def shape_tables():
    import numpy as np
    col = np.arange(GRID_W)
    c0 = np.clip(col - 8, 0, GRID_W - 16)
    inside = (col[None, :] >= c0[:, None]) & (col[None, :] < c0[:, None] + 16)
    window = np.where(inside, 0.0, -1e30).astype(np.float32)
    tok = np.arange(S)
    tables = []
    for d in (64, 32):
        n = d // 4
        inv = (np.float32(10000.0) ** (-np.arange(n, dtype=np.float32) / np.float32(n))).astype(np.float32)
        ar = (tok // GRID_W).astype(np.float32)[:, None] * inv[None, :]
        ac = (tok % GRID_W).astype(np.float32)[:, None] * inv[None, :]
        ang = np.concatenate([ar, ar, ac, ac], axis=1).astype(np.float64)
        sign = np.concatenate([-np.ones(n), np.ones(n), -np.ones(n), np.ones(n)])
        tables += [np.cos(ang), np.sin(ang) * sign]
    return {"ident": np.eye(P, dtype=np.float32), "mask": np.concatenate([window, window], axis=0),
            "rope": np.concatenate(tables, axis=1).astype(np.float32)}


def kernel(**inputs):
    import numpy as _np
    import concourse.bacc as _bacc
    from concourse import mybir as _mybir
    from concourse.bass_utils import run_bass_kernel_spmd as _run

    nc = _bacc.Bacc("TRN2", target_bir_lowering=False, num_devices=1)
    arrays, A = {}, {}
    for name in _INS:
        arrays[f"in_{name}"] = _np.ascontiguousarray(inputs[name])
    for name, a in shape_tables().items():
        arrays[f"in_{name}"] = a
    for name, a in arrays.items():
        A[name[3:]] = nc.dram_tensor(name, a.shape, _mybir.dt.from_np(a.dtype), kind="ExternalInput").ap()
    out = nc.dram_tensor("out_0", (1, S, D), F32, kind="ExternalOutput").ap()
    build(nc, A, out)
    r = _run(nc, [arrays], core_ids=[0])
    return r.results[0]["out_0"]
```

```python
import math
from contextlib import ExitStack

import concourse.bass as bass
from concourse import mybir
from concourse.alu_op_type import AluOpType as ALU

F32 = mybir.dt.float32
F32R = mybir.dt.float32r
ACT = mybir.ActivationFunctionType
AX_X = mybir.AxisListType.X

P = 128
D = 1024
KC = D // P
S = 256
NT = 512
TT = NT // P
LT = S // P
DEPTH = 2
GRID_W = 64
EPS = 1e-6
FC = 22
GROUPS = [(0, 8), (8, 8), (16, 6)]
NMOD = 9
IN_COLS = 2464
RPB = 15 * 31
RING = 4
ADA_W = 512
ADA_Q = ADA_W // P
ADA_JOBS = 4
ADA_L = NMOD * KC
ADA_LC = ADA_L // ADA_Q
ADA_PRE = 2 * KC // ADA_Q
UP = [0, 1, 2, 3]
UP_ADA = [0, "a", 1, "a", 2, "a", "a", 3]
LAM_INIT = [0.8 - 0.6 * math.exp(-0.3 * i) for i in range(DEPTH)]

NA0, GQA0, DIFF0, MLA0, PIN_END = 0, 3072, 5120, 8192, 9856
Q0, P0, PT0, OUT0, BM0, TMP0, ARENA = 9856, 12416, 13440, 13952, 14976, 16000, 17536
SEGMENTS = [(0, 768, NA0, 768), (768, 1280, GQA0, 512), (1280, 2048, DIFF0, 768), (2048, 2464, MLA0, 416)]
CHUNKS = [(0, 512), (512, 512), (1024, 512), (1536, 512), (2048, 416)]

G_NA, G_GQA, G_DIFF, G_SUB, G_CQ, G_CKV, G_MQ, G_MK, G_END = 0, 128, 320, 384, 448, 704, 832, 928, 1024

VAR0 = {"na": 0, "gqa": 32, "diff": 56, "mlac": 120, "mlaqk": 128, "sub": 160}
VAR_END = 176

BRANCHES = ["na", "gqa", "diff", "mla0", "mla1"]
HEAD_D = {"na": 64, "gqa": 64, "diff": 32, "mla0": 96, "mla1": 96}
SCALE = {b: float(d) ** -0.5 for b, d in HEAD_D.items()}


PIECES = 4


def spread(steps, pieces):
    out, done = [], 0
    for i, s in enumerate(steps):
        out += s if isinstance(s, list) else [s]
        want = (i + 1) * len(pieces) // len(steps)
        out += pieces[done:want]
        done = want
    return out + pieces[done:]


def job_pieces(kind, *a):
    return [(kind, *a, piece) for piece in range(PIECES)]


def finishes(s):
    return s[-1] == PIECES - 1


def merge_jobs(b, ms):
    out = []
    for m in ms:
        out += job_pieces("gate", b, m) + [("branch", b, m)]
    return out


def heads_of(b):
    if b == "mla0":
        return [0, 1]
    if b == "mla1":
        return [2, 3]
    return list(range(8 if b == "diff" else 4))


class Group:
    pass


class Plan:

    def __init__(self):
        self.timelines = []
        self.units = []
        self.head_last = []
        self.slabs = 0
        self.norms = 0
        n = RING
        self.ada_n0 = {}
        self.groups = {}
        self.chunks = 0
        for _ in range(ADA_PRE):
            n = self.place_chunk(n)
        self.ffn_n0 = {}
        self.need_drained = {}
        self.jobs = {}
        for layer in range(DEPTH):
            n = self.place_ffn(layer, 0, n)
            self.timelines.append(self.timeline(layer, n))
            n = self.n
            n = self.place_ffn(layer, 1, n)
        self.total = n

    def place_chunk(self, n):
        self.ada_n0[self.chunks] = n
        self.chunks += 1
        return n + ADA_JOBS

    def place_ffn(self, layer, which, n):
        self.ffn_n0[layer, which] = n
        self.groups[layer, which] = []
        for gi, (f0, nf) in enumerate(GROUPS):
            g = Group()
            g.f0, g.nf, g.turns, g.up, g.chunk0 = f0, nf, nf // 2, n, self.chunks
            with_ada = layer == 0 or (which == 0 and gi != 1)
            g.order = UP_ADA if with_ada else UP
            n += g.turns * len(g.order)
            self.chunks += g.turns if with_ada else 0
            g.straight = None
            if (layer, which) == (0, 0):
                g.straight = self.chunks
                n = self.place_chunk(n)
            g.down = n
            n += KC
            self.groups[layer, which].append(g)
        return n

    def timeline(self, layer, n):
        nt = TT if layer == 0 else LT

        def slabs(b):
            nq = 2
            out = [("slab", b, "qu", s) for s in range(nq)]
            if b != "na":
                out += [("slab", b, "qr", s) for s in range(nq)]
            return out + [("slab", b, "k", s) for s in range(1 if b == "gqa" else 2)]

        def attention(b):
            us = [(b, h, t) for h in heads_of(b) for t in range(nt)]
            out = []
            for i in range(len(us) + 2):
                turn = []
                if i >= 2:
                    turn.append(("mix", *us[i - 2]))
                    if us[i - 2][2] == nt - 1:
                        turn.append(("head", us[i - 2][0], us[i - 2][1]))
                if 1 <= i <= len(us):
                    turn.append(("turn", *us[i - 1]))
                if i < len(us):
                    turn.append(("score", *us[i]))
                out.append(turn)
            return out

        def outs(b):
            return [("turn_out", b, s) for s in range(2)]

        proj = [x for c in range(len(CHUNKS)) for kp in range(4) for x in job_pieces("proj", c, kp)]
        merge = [merge_jobs(b, range(8)) for b in range(4)]
        na, gqa, diff = attention("na"), attention("gqa"), attention("diff")
        def norm(name):
            return [("stats", name, t) for t in range(nt if name == "sub" else TT)] + [("norm", name)]

        def laced(*lists):
            marked = [((i + 1) / (len(x) + 1), q, i, e) for q, x in enumerate(lists) for i, e in enumerate(x)]
            return [m[-1] for m in sorted(marked, key=lambda m: m[:3])]

        mid = len(na) // 2
        steps = [("gain",)] + proj[:32] + norm("na") + proj[32:52]
        steps += spread(slabs("na") + laced(na[:mid], norm("gqa")), proj[52:64])
        steps += spread(laced(na[mid:], norm("diff")), proj[64:74])
        steps += spread(slabs("gqa") + outs(0), proj[74:])
        steps += spread(laced(gqa, norm("mlac")), merge[0][:25])
        steps += spread(slabs("diff") + [("turn_c", s) for s in range(3)] + outs(1), merge[0][25:35])
        cut = [len(diff) // 6, len(diff) // 3, 2 * len(diff) // 3]
        steps += spread(diff[:cut[0]], merge[0][35:])
        steps += job_pieces("up", "q") + job_pieces("up", "kv") + [("build_k",)]
        steps += spread(diff[cut[0]:cut[1]], merge[1][:6])
        steps += spread(laced(diff[cut[1]:cut[2]], norm("mlaqk")), merge[1][6:18])
        steps += spread(diff[cut[2]:], merge[1][18:30])
        steps += spread(norm("sub") + slabs("mla0"), merge[1][30:]) + outs(2)
        steps += spread(attention("mla0") + slabs("mla1") + attention("mla1"), merge[2][:35])
        steps += merge[2][35:] + outs(3)
        steps += merge[3]
        steps += [("y_last",)]
        steps += [x for m in range(8) for x in job_pieces("out", m)]

        done, bank_user = [], {b: n - 4 + ((b - n) % 4) for b in range(4)}
        order = [s for s in steps]
        self.n = n
        unit_of, cur = {}, None
        for s in order:
            kind = s[0]
            rec = {"step": s, "kind": kind}
            if kind in ("proj", "gate", "up", "out"):
                if s[-1] == 0:
                    cur = self.n
                    self.n += 1
                rec["n"] = cur
                self.jobs[cur] = s
            elif kind == "branch":
                rec["n"] = self.n
                self.jobs[self.n] = s
                self.n += 1
            elif kind == "score":
                unit_of[s[1:]] = len(self.units)
                rec["u"] = len(self.units)
                self.units.append((layer, *s[1:]))
            elif kind in ("turn", "mix"):
                rec["u"] = unit_of[s[1:]]
            elif kind == "head":
                rec["h"] = len(self.head_last)
                rec["u"] = unit_of[(s[1], s[2], nt - 1)]
                self.head_last.append(rec["u"])
            elif kind in ("slab", "turn_out", "turn_c"):
                rec["x"] = self.slabs
                self.slabs += 1
            elif kind == "norm":
                rec["v"] = self.norms
                self.norms += 1
            done.append(rec)
        for rec in done:
            if "n" not in rec or rec["n"] in self.need_drained:
                continue
            m, s = rec["n"], rec["step"]
            if s[0] == "proj":
                c0 = m - s[2]
                self.need_drained[m] = None
            elif s[0] == "up":
                self.need_drained[m] = m
                for b in range(4):
                    bank_user[b] = m
            else:
                self.need_drained[m] = bank_user[m % 4] + 1 if m % 4 in bank_user else m - 3
                self.need_drained[m] = max(self.need_drained[m], m - 3)
                bank_user[m % 4] = m
        return done


def build(nc, A, out):
    plan = Plan()
    scratch = nc.dram_tensor("rpb_rows", [64, DEPTH * 4 * RPB], F32, kind="Internal").ap()
    row = DEPTH * 4 * RPB

    with ExitStack() as ctx:
        def sb(name, shape, dt=F32):
            return ctx.enter_context(nc.sbuf_tensor(name, shape, dt))

        def sem(name):
            return ctx.enter_context(nc.semaphore(name))

        x = sb("x", [P, KC, NT])
        h_hi, h_lo = sb("h_hi", [P, KC, NT], F32R), sb("h_lo", [P, KC, NT], F32R)
        a_hi, a_lo = sb("a_hi", [P, 8, NT], F32R), sb("a_lo", [P, 8, NT], F32R)
        w_raw = sb("w_raw", [P, RING, 1024])
        w_hi, w_lo = sb("w_hi", [P, RING, 1024], F32R), sb("w_lo", [P, RING, 1024], F32R)
        arena = sb("arena", [P, ARENA])
        rope = sb("rope", [P, LT, 192])
        gains = sb("gains", [P, G_END])
        mods = sb("mods", [P, DEPTH * ADA_L, 2])
        vecs = sb("vecs", [P, P])
        b_ada = sb("b_ada", [P, DEPTH * ADA_L])
        cond = sb("cond", [P, KC, 2])
        both_parts = sb("both_parts", [P, 2])
        cond_parts = sb("cond_parts", [P, KC, 4], F32R)
        ident = sb("ident", [P, P])
        mean = sb("mean", [P, 2])
        mask = sb("mask", [P, GRID_W])
        scale_g = sb("scale_g", [P, KC, 2])
        gate_s = sb("gate_s", [P, KC, 2])
        var = sb("var", [P, VAR_END])
        tok_var = sb("tok_var", [P, 4])
        rowsum = sb("rowsum", [P, 2, 4])
        rinv = sb("rinv", [P, 4])
        top = sb("top", [P, 2])
        neg_top = sb("neg_top", [P, 2])
        neg_lam = sb("neg_lam", [P, DEPTH])
        lam_t = sb("lam_t", [P, 8])
        half_b = sb("half_b", [P, 64])
        banks = [ctx.enter_context(nc.psum_tensor(f"bank{i}", [P, 512], F32)) for i in range(8)]
        b_score, b_turn, b_slab, b_o = banks[4], banks[5], banks[6], banks[7]
        b_ada_ps, b_ada_t = banks[4], banks[7]
        b_rstd, b_ms = banks[5], banks[6]

        def at(o, *shape):
            v = arena[:, o:o + math.prod(shape)]
            if len(shape) == 1:
                return v
            names = "abcd"[:len(shape)]
            return v.rearrange(f"p ({' '.join(names)}) -> p {' '.join(names)}",
                               **{k: n for k, n in zip(names, shape)})

        na_in, gqa_in, diff_in, mla_in = at(NA0, 4, 768), at(GQA0, 4, 512), at(DIFF0, 4, 768), at(MLA0, 4, 416)
        kv_up = at(GQA0, 4, 512)
        qT_u, qT_r, kT = at(Q0, 2, 512), at(Q0 + 1024, 2, 256), at(Q0 + 1536, 2, 512)
        prob = at(P0, 512)
        gate_buf = at(P0 + 512, 512)
        probT = at(PT0, 4, P)
        outs = at(OUT0, 4, 256)
        set_t = at(OUT0, 128)
        ada_rows = at(OUT0 + 128, ADA_W)[0:4, :]
        bias_m = at(BM0, 2, LT, 256)
        sq_t = at(TMP0, 512)
        swap_t = at(TMP0 + 512, 256)
        rot_q = at(TMP0 + 768, 2, 256)
        rot_m = at(TMP0 + 768, 2, 384)
        th = at(Q0, 2, 512)
        s_t = at(Q0 + 1024, 512)
        a_t = at(Q0 + 1536, 2, 512)
        n_sq = at(6144, 2, 512)
        n_acc, n_rb, n_t = at(7168, 512), at(7680, 4, P), at(8192, 2, 512)

        def y_of(m, T=NT):
            return arena[:, m * 512:m * 512 + T] if m < 6 else arena[:, BM0 + (m - 6) * 512:BM0 + (m - 6) * 512 + T]

        oT_hi, oT_lo = [[a[:, o:o + 2, :] for o in (4, 6)] for a in (a_hi, a_lo)]
        cT_hi, cT_lo = a_hi[:, 0:3, :], a_lo[:, 0:3, :]

        in_land = sem("in_land"); const_land = sem("const_land"); rpb_land = sem("rpb_land")
        gain_land = sem("gain_land"); bias_land = [sem(f"bias_land{i}") for i in range(4)]
        landed = [sem(f"landed{i}") for i in range(RING)]
        hi_done = sem("hi_done"); lo_done = sem("lo_done"); job_done = sem("job_done"); drained = sem("drained")
        ada_out = sem("ada_out"); ada_turned = sem("ada_turned"); ada_saved = sem("ada_saved")
        cond_hi = sem("cond_hi")
        set_turned = sem("set_turned"); set_saved = sem("set_saved")
        cond_th = sem("cond_th"); cond_done = sem("cond_done"); lam_sum = sem("lam_sum"); lam_exp = sem("lam_exp")
        x_done = sem("x_done"); sq_done = sem("sq_done"); acc_done = sem("acc_done"); ms_done = sem("ms_done")
        mv_done = sem("mv_done"); mr_done = sem("mr_done"); rb_done = sem("rb_done"); rstd_done = sem("rstd_done")
        t_done = sem("t_done"); hh_done = sem("hh_done"); h_ready = sem("h_ready")
        th_done = sem("th_done"); ah_done = sem("ah_done"); a_ready = sem("a_ready")
        nv_done = sem("nv_done"); nr_done = sem("nr_done"); normed = sem("normed")
        slab_done = sem("slab_done"); slab_saved = sem("slab_saved"); slab_hi = sem("slab_hi")
        score_done = sem("score_done"); top_done = sem("top_done"); exp_done = sem("exp_done")
        turn_done = sem("turn_done"); turn_saved = sem("turn_saved"); mix_done = sem("mix_done")
        head_done = sem("head_done"); bias_built = sem("bias_built")
        gate_th = sem("gate_th"); y_sum = sem("y_sum"); yh_done = sem("yh_done"); y_ready = sem("y_ready")
        k_built = sem("k_built"); res_saved = sem("res_saved"); table_land = sem("table_land"); out_done = sem("out_done")
        dve_step = sem("dve_step"); pool_step = sem("pool_step")

        NORM_T = {(0, 0): NT, (0, 1): NT, (0, 2): NT, (1, 0): NT, (1, 1): NT, (1, 2): S}
        norm_no = {k: i for i, k in enumerate(sorted(NORM_T))}
        tiles_of = lambda l: TT if l == 0 else LT
        toks_of = lambda l: NT if l == 0 else S
        ffn_T = lambda l, w: S if (l, w) == (1, 1) else NT
        ffn_no = lambda l, w: 2 * l + w

        def mod(l, i, m=None):
            o = l * ADA_L + i * KC
            return mods[:, o:o + KC, :] if m is None else mods[:, o + m, :]

        def halves(T):
            return [(0, slice(0, S))] + ([(1, slice(S, NT))] if T == NT else [])

        def unit_ap(b, head):
            if b == "na":
                return head // 2, head // 2, 64 * (head % 2), 64
            if b == "gqa":
                return head % 2, 0, 64 * (head // 2), 64
            if b == "diff":
                return head // 4, head // 4, 32 * (head % 4), 32
            return head % 2, head % 2, 0, 96

        def value_ap(b, head, t):
            if b == "na":
                return na_in[:, t, 512 + 64 * head:576 + 64 * head]
            if b == "gqa":
                return gqa_in[:, t, 384 + 64 * (head // 2):448 + 64 * (head // 2)]
            if b == "diff":
                return diff_in[:, t, 512 + 64 * (head // 2):576 + 64 * (head // 2)]
            return kv_up[:, t, 128 * head + 64:128 * head + 128]

        def slab_source(b, what, s, t):
            if b == "na":
                o = (0 if what == "qu" else 256) + 128 * s
                return na_in[:, t, o:o + 128]
            if b == "gqa":
                if what == "k":
                    return gqa_in[:, t, 256:384]
                return (gqa_in if what == "qu" else rot_q)[:, t, 128 * s:128 * s + 128]
            if b == "diff":
                if what == "qr":
                    return rot_q[:, t, 128 * s:128 * s + 128]
                o = (0 if what == "qu" else 256) + 128 * s
                return diff_in[:, t, o:o + 128]
            hh = 2 * int(b[-1]) + s
            if what == "k":
                return diff_in[:, t, 96 * hh:96 * hh + 96]
            return (mla_in if what == "qu" else rot_m)[:, t, 96 * hh:96 * hh + 96]

        def slab_tiles(l, what):
            return {"qu": tiles_of(l), "qr": LT, "k": TT}[what]

        def slab_dest(what, s):
            return {"qu": qT_u, "qr": qT_r, "k": kT}[what][:, s, :]

        def norm_views(name, t):
            def g(o, n, d, rep):
                v = gains[:, o:o + n * d].rearrange("p (n d) -> p n d", n=n)
                return v.unsqueeze(2).broadcast_to([P, n, rep, d])
            if name == "na":
                return [(na_in[:, t, 0:512], 8, 64, (2, 4), g(G_NA, 2, 64, 4))]
            if name == "gqa":
                return [(gqa_in[:, t, 0:384], 6, 64, (3, 2), g(G_GQA, 3, 64, 2))]
            if name == "diff":
                return [(diff_in[:, t, 0:512], 16, 32, (2, 8), g(G_DIFF, 2, 32, 8))]
            if name == "mlac":
                return [(mla_in[:, t, 0:256], 1, 256, (1, 1), g(G_CQ, 1, 256, 1)),
                        (mla_in[:, t, 256:384], 1, 128, (1, 1), g(G_CKV, 1, 128, 1))]
            if name == "mlaqk":
                return [(mla_in[:, t, 0:384], 4, 96, (1, 4), g(G_MQ, 1, 96, 4)),
                        (diff_in[:, t, 0:384], 4, 96, (1, 4), g(G_MK, 1, 96, 4))]
            return [(outs[:, t, :], 4, 64, (1, 4), g(G_SUB, 1, 64, 4))]

        def norm_tiles(name, l):
            return tiles_of(l) if name == "sub" else TT

        def norm_var(name, t):
            o = VAR0[name]
            out = []
            for _, n, *_ in reversed(norm_views(name, t)):
                out.append(var[:, o + t * n:o + t * n + n])
                o += TT * n
            return out[::-1]

        def var_cols(name, l):
            n = sum(v[1] for t in range(norm_tiles(name, l)) for i, v in enumerate(norm_views(name, t))
                    if not skip_part(name, l, t, i))
            return VAR0[name], VAR0[name] + n

        def skip_part(name, l, t, i):
            return name == "mlaqk" and i == 0 and t >= tiles_of(l)

        x_jobs = {norm_no[l, 1]: plan.groups[l, 0][-1].down for l in range(DEPTH)}
        x_jobs.update({norm_no[l, 2]: plan.ffn_n0[l, 1] - KC for l in range(DEPTH)})
        x_jobs[norm_no[1, 0]] = plan.groups[0, 1][-1].down
        ada_saved_by = {norm_no[l, w]: plan.groups[l, 0 if w == 0 else 1][0].chunk0 for l in range(DEPTH) for w in range(3)}

        def shift_no(l, w):
            return l * ADA_L + 3 * w * KC

        def slab_shape(l, s):
            return (96 if s[1].startswith("mla") else P), P * slab_tiles(l, s[2])

        def width(n):
            if n in plan.jobs:
                s = plan.jobs[n]
                if s[0] == "proj":
                    return 2 * CHUNKS[s[1]][1]
                if s[0] == "up":
                    return 768 if s[1] == "q" else 512
                return 256 if s[0] == "branch" else 1024
            for groups in plan.groups.values():
                for g in groups:
                    if g.down <= n < g.down + KC:
                        return g.nf * P
            return 1024

        gate_no, prev_branch, y_last_job, up_job, proj_job = {}, {}, {}, {}, {}
        slab_for, o_slab, c_slab, slab_hi_no, rot_free = {}, {}, {}, {}, {}
        normed_for, heads_before, sub_before, head_seq, head_first = {}, {}, {}, {}, {}
        n_head, n_sub, last_branch = 0, 0, 0
        for l, line in enumerate(plan.timelines):
            for rec in line:
                s, kind = rec["step"], rec["kind"]
                if kind == "gate" and finishes(s):
                    gate_no[rec["n"]] = len(gate_no)
                    prev_branch[rec["n"]] = last_branch
                elif kind == "branch":
                    last_branch = y_last_job[l] = rec["n"]
                elif kind == "up":
                    up_job[l] = rec["n"]
                elif kind == "proj":
                    proj_job.setdefault(l, rec["n"])
                elif kind == "slab":
                    slab_for[l, s[1]] = rec["x"]
                    if s[2] == "qr":
                        after = {"gqa": (l, "diff"), "diff": (l, "mlaqk"), "mla0": None, "mla1": (l + 1, "gqa")}[s[1]]
                        if after:
                            rot_free[after] = rec["x"] + 1
                    if s[1] == "diff":
                        rot_free[l, "mlaqk"] = rec["x"] + 1
                elif kind in ("turn_out", "turn_c"):
                    slab_hi_no[rec["x"]] = len(slab_hi_no)
                    if kind == "turn_c":
                        c_slab[l] = rec["x"]
                    else:
                        o_slab[l, s[1]] = rec["x"]
                        heads_before[rec["x"]] = n_head
                        if s[1] == 2:
                            sub_before[rec["x"]] = n_sub
                elif kind == "norm":
                    normed_for[l, s[1]] = rec["v"] + 1
                    if s[1] == "mlaqk":
                        normed_for[l, "mla0"] = normed_for[l, "mla1"] = rec["v"] + 1
                    if s[1] == "sub":
                        n_sub = rec["v"] + 1
                elif kind == "head":
                    head_seq[rec["u"]] = n_head
                    n_head += 1
                elif kind == "score" and s[3] == 0:
                    head_first[rec["u"]] = len(head_first)

        rpb_t = A["na_rpb"].tensor

        def load_bias(queue, l, head):
            for t in range(LT):
                for r in range(2):
                    o = (l * 4 + head) * RPB + (7 - (2 * t + r)) * 31 + 15
                    src = bass.AP(scratch.tensor, o, [[row - 1, 64], [31, 4], [1, 64]])
                    dst = bias_m[64 * r:64 * r + 64, head % 2, t, :].rearrange("p (a c) -> p a c", a=4)
                    queue.dma_start(dst, src).then_inc(bias_land[head], 16)

        block = ctx.enter_context(nc.Block())

        @block.sync
        def _(sp):
            stage_x = at(Q0, 4, D)
            w_ada = [A["w_ada"][l].rearrange("(k p) n -> p k n", p=P) for l in range(DEPTH)]

            def ada_jobs(chunk):
                l, c = divmod(chunk, ADA_LC)
                for kp in range(ADA_JOBS):
                    n = plan.ada_n0[chunk] + kp
                    load(n, w_raw[:, n % RING, :].rearrange("p (k c) -> p k c", k=2),
                         w_ada[l][:, 2 * kp:2 * kp + 2, c * ADA_W:(c + 1) * ADA_W])

            sp.dma_start(stage_x[:, 0:2, :], A["x"][0].rearrange("(t p) d -> p t d", p=P)).then_inc(in_land, 16)
            sp.dma_start(stage_x[:, 2:4, :], A["ctx"][0].rearrange("(t p) d -> p t d", p=P)).then_inc(in_land, 16)

            def load(n, dst, src):
                sp.wait_ge(lo_done, n - RING + 1)
                sp.dma_start(dst, src).then_inc(landed[n % RING], 16)

            def ffn(l, w):
                w13 = [A[k][l, w].rearrange("(k p) n -> p k n", p=P) for k in ("ffn_w1", "ffn_w3")]
                w2 = A["ffn_w2"][l, w].rearrange("(k p) n -> p k n", p=P)

                def slot(n, blocks):
                    return w_raw[:, n % RING, 0:blocks * P].rearrange("p (k c) -> p k c", k=blocks)

                for g in plan.groups[l, w]:
                    stride = len(g.order)
                    with sp.Fori(0, g.turns) as i:
                        kp = 0
                        for o, what in enumerate(g.order):
                            n = g.up + o
                            sp.wait_ge(lo_done, stride * i + (n - RING + 1))
                            if what == "a":
                                la, c = divmod(g.chunk0, ADA_LC)
                                src = w_ada[la][:, 2 * kp:2 * kp + 2, bass.ds(ADA_W * i + c * ADA_W, ADA_W)]
                                dst = w_raw[:, n % RING, :].rearrange("p (k c) -> p k c", k=2)
                                kp += 1
                            else:
                                src = w13[what % 2][:, :, bass.ds(2 * P * i + (g.f0 + what // 2) * P, P)]
                                dst = slot(n, KC)
                            sp.dma_start(dst, src).then_inc(landed[n % RING], 16)
                    if g.straight is not None:
                        ada_jobs(g.straight)
                    with sp.Fori(0, KC // 4) as i:
                        for j in range(4):
                            n = g.down + j
                            sp.wait_ge(lo_done, 4 * i + (n - RING + 1))
                            sp.dma_start(slot(n, g.nf), w2[:, g.f0:g.f0 + g.nf, bass.ds(4 * P * i + j * P, P)])\
                                .then_inc(landed[n % RING], 16)

            def mixer(l):
                w_in = A["w_in"][l].rearrange("(k p) n -> p k n", p=P)
                w_gate = A["w_gate"][l].rearrange("b (k p) n -> b p k n", p=P)
                w_br = A["w_branch"][l].rearrange("b (k p) n -> b p k n", p=P)
                w_out = A["w_out"][l].rearrange("(k p) n -> p k n", p=P)
                for rec in plan.timelines[l]:
                    s, kind = rec["step"], rec["kind"]
                    if "n" not in rec or (kind != "branch" and s[-1] > 0):
                        continue
                    n = rec["n"]
                    if kind == "proj":
                        c0, cw = CHUNKS[s[1]]
                        src = w_in[:, 2 * s[2]:2 * s[2] + 2, c0:c0 + cw]
                    elif kind == "gate":
                        src = w_gate[s[1]][:, :, s[2] * P:(s[2] + 1) * P]
                    elif kind == "branch":
                        src = w_br[s[1]][:, :, s[2] * P:(s[2] + 1) * P]
                    elif kind == "up" and s[1] == "q":
                        src = A["mla_w_uq"][l].rearrange("(k p) n -> p k n", p=P)
                    elif kind == "up":
                        src = A["mla_w_ukv"][l].rearrange("(k p) n -> p k n", p=P)
                    else:
                        src = w_out[:, :, s[1] * P:(s[1] + 1) * P]
                    k, w = src.shape[1], src.shape[2]
                    load(n, w_raw[:, n % RING, 0:k * w].rearrange("p (k c) -> p k c", k=k), src)

            for chunk in range(ADA_PRE):
                ada_jobs(chunk)
            for l in range(DEPTH):
                ffn(l, 0)
                mixer(l)
                ffn(l, 1)
            sp.wait_ge(res_saved, 4)
            sp.dma_start(out[0].rearrange("(t p) d -> p t d", p=P), at(0, LT, D)).then_inc(out_done, 16)
            sp.wait_ge(out_done, 16)

        @block.gpsimd
        def _(pool):
            count = [0]

            def link(ins):
                count[0] += 1
                ins.then_inc(pool_step, 1)
                pool.wait_ge(pool_step, count[0])

            pool.dma_start(ident[:, :], A["ident"]).then_inc(const_land, 16)
            stage = at(TMP0, 4, P)
            pool.dma_start(stage[0:48, 0, :], A["norm_g"].rearrange("l w (m p) -> (l w m) p", p=P)).then_inc(const_land, 16)
            pool.dma_start(stage[48:112, 0, :], A["b_gate"].rearrange("l w (m p) -> (l w m) p", p=P)).then_inc(const_land, 16)
            pool.dma_start(stage[112:120, 0, :], A["c"].rearrange("b (m p) -> (b m) p", p=P)).then_inc(const_land, 16)
            pool.dma_start(stage[120:128, 0, :], A["c_ctx"].rearrange("(m p) -> m p", p=P)).then_inc(const_land, 16)
            pool.dma_start(stage[0:ADA_L, 1:3, :], A["b_ada"].rearrange("l (m p) -> m l p", p=P)).then_inc(const_land, 16)
            pool.dma_start(mask[:, :], A["mask"]).then_inc(table_land, 16)
            pool.dma_start(rope[:, :, :], A["rope"].rearrange("(t p) c -> p t c", p=P)).then_inc(table_land, 16)
            lam_s = at(TMP0 + 512, DEPTH, 4, 32)
            pool.dma_start(lam_s, A["diff_lambda"].unsqueeze(0).broadcast_to([P, DEPTH, 4, 32])).then_inc(table_land, 16)
            pool.dma_start(scratch, bass.AP(rpb_t, 0, [[0, 64], [1, row]])).then_inc(rpb_land, 16)

            def load_gains(l):
                for o, name in ((G_NA, "na_g_q"), (G_NA + 64, "na_g_k"), (G_GQA, "gqa_g_q"), (G_GQA + 64, "gqa_g_q"),
                                (G_GQA + 128, "gqa_g_k"), (G_DIFF, "diff_g_q"), (G_DIFF + 32, "diff_g_k"),
                                (G_SUB, "diff_g_sub"), (G_CQ, "mla_g_cq"), (G_CKV, "mla_g_ckv"), (G_MQ, "mla_g_q"),
                                (G_MK, "mla_g_k")):
                    v = A[name][l:l + 1, :]
                    pool.dma_start(gains[:, o:o + v.shape[1]], v.broadcast_to([P, v.shape[1]])).then_inc(gain_land, 16)

            def build_k(l):
                pool.wait_ge(drained, up_job[l] + 1)
                pool.wait_ge(slab_done, rot_free[l, "mlaqk"])
                for t in range(TT):
                    k = diff_in[:, t, 0:384].rearrange("p (h d) -> p h d", h=4)
                    link(pool.tensor_copy(k[:, :, 0:64],
                                          kv_up[:, t, :].rearrange("p (h d) -> p h d", h=4)[:, :, 0:64]))
                    last = pool.tensor_copy(k[:, :, 64:96], mla_in[:, t:t + 1, 384:416].broadcast_to([P, 4, 32]))
                    if t == TT - 1:
                        last.then_inc(k_built, 1)
                    else:
                        link(last)

            def norm(l, name, v):
                pool.wait_ge(nr_done, v + 1)
                for t in range(norm_tiles(name, l)):
                    for i, ((ap, n, d, gd, g), vv) in enumerate(zip(norm_views(name, t), norm_var(name, t))):
                        if skip_part(name, l, t, i):
                            continue
                        x3 = ap.rearrange("p (n d) -> p n d", n=n)
                        link(pool.tensor_tensor(x3, x3, vv.unsqueeze(2).broadcast_to([P, n, d]), ALU.mult))
                        x4 = ap.rearrange("p (a b d) -> p a b d", a=gd[0], b=gd[1])
                        link(pool.tensor_tensor(x4, x4, g, ALU.mult))
                if name in ("gqa", "diff", "mlaqk"):
                    if (l, name) != (0, "gqa"):
                        pool.wait_ge(slab_done, rot_free[l, name])
                    rotate(l, name)
                pool.sem_inc(normed, 1)

            def rotate(l, name):
                for t in range(LT):
                    if name == "mlaqk":
                        heads, d, o = 4, 32, 128
                        k = diff_in[:, t, 0:384].rearrange("p (h d) -> p h d", h=4)[:, :, 64:96]
                        qs = mla_in[:, t, 0:384].rearrange("p (h d) -> p h d", h=4)[:, :, 64:96]
                        q = rot_m[:, t, :].rearrange("p (h d) -> p h d", h=4)
                        link(pool.tensor_copy(rot_m[:, t, :], mla_in[:, t, 0:384]))
                        parts = [(k, k, 4), (qs, q[:, :, 64:96], 4)]
                    elif name == "gqa":
                        d, o = 64, 0
                        parts = [(gqa_in[:, t, 256:384].rearrange("p (h d) -> p h d", h=2),) * 2 + (2,),
                                 (gqa_in[:, t, 0:256].rearrange("p (h d) -> p h d", h=4),
                                  rot_q[:, t, :].rearrange("p (h d) -> p h d", h=4), 4)]
                    else:
                        d, o = 32, 128
                        parts = [(diff_in[:, t, 256:512].rearrange("p (h d) -> p h d", h=8),) * 2 + (8,),
                                 (diff_in[:, t, 0:256].rearrange("p (h d) -> p h d", h=8),
                                  rot_q[:, t, :].rearrange("p (h d) -> p h d", h=8), 8)]
                    cos, sin = rope[:, t, o:o + d], rope[:, t, o + d:o + 2 * d]
                    for src, dst, n in parts:
                        e = d // 4
                        sw = swap_t[:, 0:n * d].rearrange("p (h d) -> p h d", h=n)
                        for half in range(2):
                            for pair in range(2):
                                a, b = (2 * pair + half) * e, (2 * pair + 1 - half) * e
                                link(pool.tensor_tensor(sw[:, :, a:a + e], src[:, :, b:b + e],
                                                        sin[:, a:a + e].unsqueeze(1).broadcast_to([P, n, e]), ALU.mult))
                        link(pool.tensor_tensor(dst, src, cos.unsqueeze(1).broadcast_to([P, n, d]), ALU.mult))
                        link(pool.tensor_tensor(dst, dst, sw, ALU.add))

            load_gains(0)
            pool.wait_ge(table_land, 16 * 3)
            for l in range(DEPTH):
                pool.wait_ge(rpb_land, 16)
                pool.wait_ge(gain_land, 16 * 12 * (l + 1))
                load_bias(pool, l, 0)
                load_bias(pool, l, 1)
                for rec in plan.timelines[l]:
                    s = rec["step"]
                    if rec["kind"] == "norm":
                        norm(l, s[1], rec["v"])
                    elif rec["kind"] == "build_k":
                        build_k(l)
                if l == 0:
                    pool.wait_ge(y_ready, KC * (l + 1))
                    load_gains(1)

        @block.scalar
        def _(act):
            def hi_loop(n, i, stride=4):
                act.wait_ge(landed[n % RING], 16 * (stride // RING) * i + 16 * (n // RING))
                act.wait_ge(job_done, stride * i + (n - RING + 1))
                act.activation(w_hi[:, n % RING, :], w_raw[:, n % RING, :], ACT.Copy).then_inc(hi_done, 1)

            def hi_mixed(n):
                if n >= plan.total:
                    return
                act.wait_ge(landed[n % RING], 16 * (n // RING))
                act.wait_ge(job_done, n - RING + 1)
                act.activation(w_hi[:, n % RING, 0:width(n)], w_raw[:, n % RING, 0:width(n)], ACT.Copy).then_inc(hi_done, 1)

            def ada_rows_out(chunk, last_job, i=None, stride=0):
                if i is None:
                    act.wait_ge(job_done, last_job + 1)
                    if chunk:
                        act.wait_ge(ada_turned, chunk)
                else:
                    act.wait_ge(job_done, stride * i + (last_job + 1))
                    act.wait_ge(ada_turned, 1 * i + chunk)
                act.activation(ada_rows, b_ada_ps[0:4, :], ACT.Copy).then_inc(ada_out, 1)

            def ada_chunk(chunk):
                n = plan.ada_n0[chunk]
                for k in range(ADA_JOBS):
                    hi_mixed(n + k + 4)
                ada_rows_out(chunk, n + ADA_JOBS - 1)

            def norm_stats(l, w):
                T, v = NORM_T[l, w], norm_no[l, w]
                for m in range(KC):
                    if v == 0:
                        act.wait_ge(x_done, m + 1)
                    else:
                        act.wait_ge(drained, x_jobs[v] + m + 1)
                    if m >= 3:
                        act.wait_ge(acc_done, (KC - 1) * v + m - 2)
                    dst = n_acc if m == 0 else n_sq[:, m % 2, :]
                    act.activation(dst[:, 0:T], x[:, m, 0:T], ACT.Square).then_inc(sq_done, 1)
                act.wait_ge(mv_done, v + 1)
                act.activation(tok_var[:, 0:T // P], tok_var[:, 0:T // P], ACT.Sqrt).then_inc(mr_done, 1)

            def norm_apply(l, w):
                T, v = NORM_T[l, w], norm_no[l, w]
                for k in range(KC):
                    act.wait_ge(t_done, KC * v + k + 1)
                    for c, cols in halves(T):
                        last = act.activation(h_hi[:, k, cols], n_t[:, k % 2, cols], ACT.Identity,
                                              bias=mods[:, shift_no(l, w) + k, c:c + 1])
                    last.then_inc(hh_done, 1)

            def norm(l, w):
                norm_stats(l, w)
                norm_apply(l, w)

            def ffn(l, w):
                T = ffn_T(l, w)
                a0 = FC * ffn_no(l, w)
                for g in plan.groups[l, w]:
                    stride = len(g.order)
                    with act.Fori(0, g.turns) as i:
                        for o, what in enumerate(g.order):
                            n = g.up + o
                            if what in (0, 2):
                                j = what // 2
                                act.wait_ge(job_done, stride * i + (n + 1))
                                act.wait_ge(drained, stride * i + (n - 3))
                                act.activation(th[:, j, 0:T], banks[(g.up + what) % 4][:, 0:T], ACT.Tanh, scale=0.5)\
                                   .then_inc(th_done, 1)
                            elif what in (1, 3):
                                j = what // 2
                                act.wait_ge(drained, stride * i + (n + 1))
                                act.wait_ge(hi_done, n + 3)
                                act.activation(a_hi[:, bass.ds(2 * i + j, 1), 0:T], a_t[:, j:j + 1, 0:T],
                                               ACT.Copy).then_inc(ah_done, 1)
                            hi_loop(n + 4, i, stride)
                            if what == "a" and "a" not in g.order[o + 1:]:
                                ada_rows_out(g.chunk0, n, i, stride)
                    if g.straight is not None:
                        ada_chunk(g.straight)
                    if g is not plan.groups[l, w][-1]:
                        with act.Fori(0, 2) as i:
                            for j in range(4):
                                hi_loop(g.down + j + 4, i)
                    else:
                        for m in range(KC):
                            hi_mixed(g.down + m + 4)

            def mixer(l):
                T, nt = toks_of(l), tiles_of(l)
                for rec in plan.timelines[l]:
                    s, kind = rec["step"], rec["kind"]
                    if kind in ("proj", "up") and finishes(s):
                        hi_mixed(rec["n"] + 4)
                    elif kind == "gate" and finishes(s):
                        n = rec["n"]
                        hi_mixed(n + 4)
                        act.wait_ge(job_done, n + 1)
                        g = gate_no[n]
                        if g >= 1:
                            act.wait_ge(drained, prev_branch[n] + 1)
                        o = l * 32 + s[1] * KC + s[2]
                        act.activation(gate_buf[:, 0:T], banks[n % 4][:, 0:T], ACT.Tanh, scale=0.5,
                                       bias=half_b[:, o:o + 1]).then_inc(gate_th, 1)
                    elif kind == "branch":
                        hi_mixed(rec["n"] + 4)
                        if s[1] == 3 and s[2] < 6:
                            act.wait_ge(y_sum, 24 * l + 16 + s[2] + 1)
                            act.activation(a_hi[:, s[2], 0:T], y_of(s[2], T), ACT.Copy).then_inc(yh_done, 1)
                    elif kind == "y_last":
                        for m in (6, 7):
                            act.wait_ge(y_sum, 24 * l + 16 + m + 1)
                            act.wait_ge(job_done, y_last_job[l] + 1)
                            act.activation(a_hi[:, m, 0:T], y_of(m, T), ACT.Copy).then_inc(yh_done, 1)
                    elif kind == "out" and finishes(s):
                        hi_mixed(rec["n"] + 4)
                    elif kind == "head" and s[1] == "na" and s[2] < 2:
                        act.wait_ge(mix_done, rec["u"] + 1)
                        load_bias(act, l, s[2] + 2)
                    elif kind == "norm":
                        v = rec["v"]
                        act.wait_ge(nv_done, v + 1)
                        o0, o1 = var_cols(s[1], l)
                        act.activation(var[:, o0:o1], var[:, o0:o1], ACT.Sqrt).then_inc(nr_done, 1)
                    elif kind == "score":
                        u = rec["u"]
                        b, head, t = s[1:]
                        keys = NT if t < LT else S
                        act.wait_ge(top_done, u + 1)
                        if u:
                            act.wait_ge(turn_done, u)
                        act.activation(prob[:, 0:keys], b_score[:, 0:keys], ACT.Exp,
                                       bias=neg_top[:, u % 2:u % 2 + 1], scale=SCALE[b],
                                       accum_out=rowsum[:, head % 2, t:t + 1]).then_inc(exp_done, 1)
                    elif kind == "turn" and rec["u"] % 2 == 1:
                        u = rec["u"]
                        keys = NT if s[3] < LT else S
                        act.wait_ge(turn_done, u + 1)
                        act.wait_ge(mix_done, u)
                        act.activation(arena[:, PT0:PT0 + keys], b_turn[:, 0:keys], ACT.Copy).then_inc(turn_saved, 1)
                    elif kind == "slab" and rec["x"] % 2 == 1:
                        act.wait_ge(slab_done, rec["x"] + 1)
                        w_, n_ = slab_shape(l, s)
                        act.activation(slab_dest(s[2], s[3])[0:w_, 0:n_], b_slab[0:w_, 0:n_], ACT.Copy)\
                           .then_inc(slab_saved, 1)
                    elif kind == "turn_out":
                        act.wait_ge(slab_done, rec["x"] + 1)
                        act.activation(oT_hi[s[1] % 2][:, s[2], 0:T], b_slab[:, 0:T], ACT.Copy).then_inc(slab_hi, 1)
                    elif kind == "turn_c":
                        act.wait_ge(slab_done, rec["x"] + 1)
                        act.activation(cT_hi[:, s[1], :], b_slab[:, :], ACT.Copy).then_inc(slab_hi, 1)

            act.wait_ge(set_saved, 2)
            act.activation(set_t[:, 0:16], vecs[:, 112:128], ACT.Tanh, scale=0.5).then_inc(cond_th, 1)
            act.wait_ge(cond_done, 1)
            act.activation(cond_parts[:, :, 0:2], cond[:, :, :], ACT.Copy).then_inc(cond_hi, 1)
            act.wait_ge(lam_sum, 1)
            act.activation(lam_t[:, 0:4], lam_t[:, 0:4], ACT.Exp).then_inc(lam_exp, 1)
            act.sem_inc(hi_done, RING)
            norm_stats(0, 0)
            for n in range(RING, 2 * RING):
                hi_mixed(n)
            for chunk in range(ADA_PRE):
                ada_chunk(chunk)
            for l in range(DEPTH):
                if l:
                    norm_stats(l, 0)
                norm_apply(l, 0)
                ffn(l, 0)
                norm(l, 1)
                mixer(l)
                norm(l, 2)
                ffn(l, 1)

        @block.vector
        def _(dve):
            count = [0]

            def link(ins):
                count[0] += 1
                ins.then_inc(dve_step, 1)
                dve.wait_ge(dve_step, count[0])

            def lo(n, w=1024):
                dve.wait_ge(hi_done, n + 1)
                dve.tensor_tensor(w_lo[:, n % RING, 0:w], w_raw[:, n % RING, 0:w], w_hi[:, n % RING, 0:w].bitcast(F32),
                                  ALU.subtract).then_inc(lo_done, 1)

            def lo_loop(n, i, stride=4):
                dve.wait_ge(hi_done, stride * i + (n + 1))
                dve.tensor_tensor(w_lo[:, n % RING, :], w_raw[:, n % RING, :], w_hi[:, n % RING, :].bitcast(F32),
                                  ALU.subtract).then_inc(lo_done, 1)

            def lo_mixed(n):
                if n < plan.total:
                    lo(n, width(n))

            def ada_save(chunk, i=None):
                if i is None:
                    dve.wait_ge(ada_turned, chunk + 1)
                    dst, bia = mods[:, ADA_Q * chunk:ADA_Q * (chunk + 1), :], b_ada[:, ADA_Q * chunk:ADA_Q * (chunk + 1)]
                else:
                    dve.wait_ge(ada_turned, 1 * i + (chunk + 1))
                    dst = mods[:, bass.ds(ADA_Q * i + ADA_Q * chunk, ADA_Q), :]
                    bia = b_ada[:, bass.ds(ADA_Q * i + ADA_Q * chunk, ADA_Q)]
                sums = b_ada_t[:, 0:2 * ADA_Q].rearrange("p (q c) -> p q c", c=2)
                dve.tensor_tensor(dst, sums, bia.unsqueeze(2).broadcast_to([P, ADA_Q, 2]), ALU.add).then_inc(ada_saved, 1)

            def ada_chunk(chunk):
                dve.sem_inc(drained, ADA_JOBS)
                for k in range(ADA_JOBS):
                    lo_mixed(plan.ada_n0[chunk] + k + 4)
                ada_save(chunk)

            def norm_stats(l, w):
                T, v = NORM_T[l, w], norm_no[l, w]
                ntile = T // P
                for m in range(1, KC):
                    dve.wait_ge(sq_done, KC * v + m + 1)
                    if m >= 2:
                        dve.wait_ge(acc_done, (KC - 1) * v + m - 1)
                    dve.tensor_tensor(n_acc[:, 0:T], n_acc[:, 0:T], n_sq[:, m % 2, 0:T], ALU.add).then_inc(acc_done, 1)
                dve.wait_ge(ms_done, v + 1)
                link(dve.tensor_scalar(tok_var[:, 0:ntile], b_ms[:, 0:2 * ntile:2], EPS, None, ALU.add))
                dve.reciprocal(tok_var[:, 0:ntile], tok_var[:, 0:ntile]).then_inc(mv_done, 1)
                dve.wait_ge(mr_done, v + 1)
                dve.tensor_copy(n_rb[:, 0:ntile, :], tok_var[:, 0:ntile].unsqueeze(2).broadcast_to([P, ntile, P]))\
                    .then_inc(rb_done, 1)

            def norm_apply(l, w):
                T, v = NORM_T[l, w], norm_no[l, w]
                g0, sc = l * 24 + w * KC, shift_no(l, w) + KC
                dve.wait_ge(ada_saved, ada_saved_by[v])
                link(dve.scalar_tensor_tensor(scale_g[:, :, :], mods[:, sc:sc + KC, :], 1.0,
                                              vecs[:, g0:g0 + KC].unsqueeze(2).broadcast_to([P, KC, 2]), ALU.add, ALU.mult))
                dve.wait_ge(rstd_done, v + 1)

                def times(k):
                    if k >= 2:
                        dve.wait_ge(h_ready, KC * v + k - 1)
                    for c, cols in halves(T):
                        last = dve.scalar_tensor_tensor(n_t[:, k % 2, cols], x[:, k, cols], scale_g[:, k, c:c + 1],
                                                        b_rstd[:, cols], ALU.mult, ALU.mult)
                    last.then_inc(t_done, 1)

                def rest(k):
                    dve.wait_ge(hh_done, KC * v + k + 1)
                    for c, cols in halves(T):
                        last = dve.scalar_tensor_tensor(h_lo[:, k, cols], n_t[:, k % 2, cols],
                                                        mods[:, shift_no(l, w) + k, c:c + 1],
                                                        h_hi[:, k, cols].bitcast(F32), ALU.add, ALU.subtract)
                    last.then_inc(h_ready, 1)

                for k in range(KC + 1):
                    if k < KC:
                        times(k)
                    if k:
                        rest(k - 1)

            def norm(l, w):
                norm_stats(l, w)
                norm_apply(l, w)

            def gates(l, w):
                gt = shift_no(l, w) + 2 * KC
                link(dve.tensor_scalar(gate_s[:, :, :], mods[:, gt:gt + KC, :], 0.5 if w == 1 else 0.25, None, ALU.mult))

            def ffn(l, w):
                T = ffn_T(l, w)
                a0 = FC * ffn_no(l, w)
                for g in plan.groups[l, w]:
                    stride = len(g.order)
                    counts = [0, 0, 0, 0]
                    for what in g.order:
                        last = last if what == "a" else what
                        counts[last] += 1
                    with dve.Fori(0, g.turns) as i:
                        for o, what in enumerate(g.order):
                            n, j = g.up + o, 0 if what == "a" else what // 2
                            f = a0 + g.f0 + j
                            if what in (0, 2):
                                dve.wait_ge(th_done, 2 * i + (f + 1))
                                dve.scalar_tensor_tensor(s_t[:, 0:T], th[:, j, 0:T], 1.0, banks[(g.up + what) % 4][:, 0:T],
                                                         ALU.add, ALU.mult).then_inc(drained, counts[what])
                            elif what in (1, 3):
                                dve.wait_ge(drained, stride * i + n)
                                dve.wait_ge(job_done, stride * i + (n + 1))
                                dve.tensor_tensor(a_t[:, j, 0:T], s_t[:, 0:T], banks[(g.up + what) % 4][:, 0:T],
                                                  ALU.mult).then_inc(drained, counts[what])
                                dve.wait_ge(ah_done, 2 * i + (f + 1))
                                dve.tensor_tensor(a_lo[:, bass.ds(2 * i + j, 1), 0:T], a_t[:, j:j + 1, 0:T],
                                                  a_hi[:, bass.ds(2 * i + j, 1), 0:T].bitcast(F32),
                                                  ALU.subtract).then_inc(a_ready, 1)
                            lo_loop(n + 4, i, stride)
                        if "a" in g.order:
                            ada_save(g.chunk0, i)
                    if g.straight is not None:
                        ada_chunk(g.straight)
                    if g.f0 == 0:
                        if (l, w) == (0, 0):
                            dve.wait_ge(ada_saved, g.straight + 1)
                        gates(l, 0 if w == 0 else 2)
                    if g is not plan.groups[l, w][-1]:
                        with dve.Fori(0, 2) as i:
                            for j in range(4):
                                n = g.down + j
                                dve.wait_ge(job_done, 4 * i + (n + 1))
                                for c, cols in halves(T):
                                    xs = x[:, bass.ds(4 * i + j, 1), cols]
                                    last = dve.scalar_tensor_tensor(
                                        xs, banks[n % 4][:, cols].unsqueeze(1), gate_s[:, bass.ds(4 * i + j, 1), c],
                                        xs, ALU.mult, ALU.add)
                                last.then_inc(drained, 1)
                                lo_loop(n + 4, i)
                    else:
                        for m in range(KC):
                            n = g.down + m
                            dve.wait_ge(job_done, n + 1)
                            for c, cols in halves(T):
                                last = dve.scalar_tensor_tensor(x[:, m, cols], banks[n % 4][:, cols],
                                                                gate_s[:, m, c:c + 1], x[:, m, cols], ALU.mult, ALU.add)
                            last.then_inc(drained, 1)
                            lo_mixed(n + 4)

            def mixer(l):
                T, nt = toks_of(l), tiles_of(l)
                for rec in plan.timelines[l]:
                    s, kind = rec["step"], rec["kind"]
                    if kind == "gain":
                        dve.wait_ge(gain_land, 16 * 12 * (l + 1))
                        g = gains[:, G_SUB:G_SUB + 64]
                        link(dve.tensor_scalar(g, g, 1.0 - LAM_INIT[l], None, ALU.mult))
                        gates(l, 1)
                    elif kind == "proj" and finishes(s):
                        n, c = rec["n"], s[1]
                        if s[2] == 3:
                            dve.wait_ge(job_done, n + 1)
                            c0, cw = CHUNKS[c]
                            first = n - 3
                            for t in range(TT):
                                for a, b, base, width_ in SEGMENTS:
                                    u, v = max(a, c0), min(b, c0 + cw)
                                    if u < v:
                                        o = base + t * width_ + u - a
                                        dst, src = arena[:, o:o + v - u], banks[(first + t) % 4][:, u - c0:v - c0]
                                        if base == GQA0 and c == 1:
                                            dst = dst.rearrange("p (r g d) -> p r g d", r=2, g=2)
                                            src = src.rearrange("p (g r d) -> p r g d", r=2, g=2)
                                        last = dve.tensor_copy(dst, src)
                                last.then_inc(drained, 1)
                        lo_mixed(n + 4)
                    elif kind == "up" and finishes(s):
                        n = rec["n"]
                        dve.wait_ge(job_done, n + 1)
                        for t in range(nt if s[1] == "q" else TT):
                            dst = mla_in[:, t, 0:384] if s[1] == "q" else kv_up[:, t, :]
                            last = dve.tensor_copy(dst, banks[t][:, 0:dst.shape[1]])
                        last.then_inc(drained, 1)
                        lo_mixed(n + 4)
                    elif kind == "gate" and finishes(s):
                        lo_mixed(rec["n"] + 4)
                    elif kind == "branch":
                        n, b, m = rec["n"], s[1], s[2]
                        dve.wait_ge(gate_th, gate_no[n - 1] + 1)
                        dve.wait_ge(job_done, n + 1)
                        y = y_of(m, T)
                        if b == 0:
                            dve.scalar_tensor_tensor(y, gate_buf[:, 0:T], 1.0, banks[n % 4][:, 0:T], ALU.add, ALU.mult)\
                               .then_inc(drained, 2)
                        else:
                            dve.scalar_tensor_tensor(sq_t[:, 0:T], gate_buf[:, 0:T], 1.0, banks[n % 4][:, 0:T],
                                                     ALU.add, ALU.mult).then_inc(drained, 2)
                            dve.wait_ge(drained, n + 1)
                            dve.tensor_tensor(y, y, sq_t[:, 0:T], ALU.add).then_inc(y_sum, 1)
                        lo_mixed(n + 4)
                        if b:
                            dve.wait_ge(y_sum, 24 * l + 8 * (b - 1) + m + 1)
                        if b == 3 and m < 6:
                            y_low(l, m, T)
                    elif kind == "y_last":
                        y_low(l, 6, T)
                        y_low(l, 7, T)
                    elif kind == "out" and finishes(s):
                        n, m = rec["n"], s[1]
                        dve.wait_ge(job_done, n + 1)
                        for c, cols in halves(T):
                            last = dve.scalar_tensor_tensor(x[:, m, cols], banks[n % 4][:, cols],
                                                            gate_s[:, m, c:c + 1], x[:, m, cols], ALU.mult, ALU.add)
                        last.then_inc(drained, 1)
                        lo_mixed(n + 4)
                    elif kind == "stats":
                        head_stats(l, s[1], s[2])
                    elif kind == "norm":
                        head_norm(l, s[1], rec["v"])
                    elif kind == "score":
                        u = rec["u"]
                        b, head, t = s[1:]
                        keys = NT if t < LT else S
                        dve.wait_ge(score_done, u + 1)
                        link(dve.reduce_max(top[:, u % 2:u % 2 + 1], b_score[:, 0:keys], AX_X))
                        dve.tensor_scalar(neg_top[:, u % 2:u % 2 + 1], top[:, u % 2:u % 2 + 1], -SCALE[b], None,
                                          ALU.mult).then_inc(top_done, 1)
                    elif kind == "turn" and rec["u"] % 2 == 0:
                        u = rec["u"]
                        keys = NT if s[3] < LT else S
                        dve.wait_ge(turn_done, u + 1)
                        if u:
                            dve.wait_ge(mix_done, u)
                        dve.tensor_copy(arena[:, PT0:PT0 + keys], b_turn[:, 0:keys]).then_inc(turn_saved, 1)
                    elif kind == "head":
                        head_out(l, s[1], s[2], rec["u"])
                    elif kind == "slab" and rec["x"] % 2 == 0:
                        dve.wait_ge(slab_done, rec["x"] + 1)
                        w_, n_ = slab_shape(l, s)
                        dve.tensor_copy(slab_dest(s[2], s[3])[0:w_, 0:n_], b_slab[0:w_, 0:n_]).then_inc(slab_saved, 1)
                    elif kind in ("turn_out", "turn_c"):
                        dve.wait_ge(slab_hi, slab_hi_no[rec["x"]] + 1)
                        if kind == "turn_out":
                            dst, hi_, W = oT_lo[s[1] % 2][:, s[2], 0:T], oT_hi[s[1] % 2][:, s[2], 0:T], T
                        else:
                            dst, hi_, W = cT_lo[:, s[1], :], cT_hi[:, s[1], :], NT
                        dve.tensor_tensor(dst, b_slab[:, 0:W], hi_.bitcast(F32),
                                          ALU.subtract).then_inc(slab_saved, 1)
                    if kind == "slab" and s[1] == "na" and s[2:] == ("qu", 0):
                        build_bias(l, 0)
                        build_bias(l, 1)
                    if kind == "score" and s[1] == "na" and s[2] in (1, 2) and s[3] == nt - 1:
                        build_bias(l, s[2] + 1)

            def build_bias(l, head):
                dve.wait_ge(bias_land[head], 64 * (l + 1))
                for t in range(LT):
                    v = bias_m[:, head % 2, t, :].rearrange("p (a c) -> p a c", a=4)
                    last = dve.scalar_tensor_tensor(v, v, 1.0 / SCALE["na"], mask[:, :].unsqueeze(1).broadcast_to([P, 4, 64]),
                                                    ALU.mult, ALU.add)
                last.then_inc(bias_built, 1)

            def y_low(l, m, T):
                dve.wait_ge(yh_done, 8 * l + m + 1)
                dve.tensor_tensor(a_lo[:, m, 0:T], y_of(m, T), a_hi[:, m, 0:T].bitcast(F32), ALU.subtract)\
                   .then_inc(y_ready, 1)

            def head_stats(l, name, t):
                if t == 0 and name == "mlaqk":
                    dve.wait_ge(k_built, l + 1)
                elif t == 0 and name != "sub":
                    dve.wait_ge(drained, proj_job[l] + 4 * (1 + {"na": 1, "gqa": 2, "diff": 3, "mlac": 4}[name]))
                for i, ((ap, n, d, gd, g), vv) in enumerate(zip(norm_views(name, t), norm_var(name, t))):
                    if skip_part(name, l, t, i):
                        continue
                    sq = sq_t[:, 0:n * d]
                    link(dve.tensor_tensor(sq, ap, ap, ALU.mult))
                    link(dve.tensor_reduce(vv, sq.rearrange("p (n d) -> p n d", n=n), AX_X, ALU.add))

            def head_norm(l, name, v):
                o0, o1 = var_cols(name, l)
                parts = {}
                for t in range(norm_tiles(name, l)):
                    for i, (view, vv) in enumerate(zip(norm_views(name, t), norm_var(name, t))):
                        if not skip_part(name, l, t, i):
                            parts.setdefault(view[2], []).append(view[1])
                o = o0
                for d, ns in reversed(parts.items()):
                    link(dve.tensor_scalar(var[:, o:o + sum(ns)], var[:, o:o + sum(ns)], 1.0 / d, EPS, ALU.mult, ALU.add))
                    o += sum(ns)
                dve.reciprocal(var[:, o0:o1], var[:, o0:o1]).then_inc(nv_done, 1)

            def head_out(l, b, head, u):
                nt = tiles_of(l)
                dve.wait_ge(mix_done, u + 1)
                link(dve.reciprocal(rinv[:, 0:nt], rowsum[:, head % 2, 0:nt]))
                o = b_o[:, 0:nt * 64].rearrange("p (t d) -> p t d", t=nt)
                if b == "diff":
                    dst = outs[:, 0:nt, 64 * (head // 2):64 * (head // 2) + 64]
                    if head % 2:
                        link(dve.tensor_scalar(rinv[:, 0:nt], rinv[:, 0:nt], neg_lam[:, l:l + 1], None, ALU.mult))
                        for t in range(nt):
                            last = dve.scalar_tensor_tensor(dst[:, t, :], o[:, t, :], rinv[:, t:t + 1], dst[:, t, :],
                                                            ALU.mult, ALU.add)
                        last.then_inc(head_done, 1)
                        dve.wait_ge(head_done, head_seq[u] + 1)
                        return
                else:
                    dst = outs[:, 0:nt, 64 * head:64 * head + 64]
                dve.tensor_tensor(dst, o, rinv[:, 0:nt].unsqueeze(2).broadcast_to([P, nt, 64]), ALU.mult)\
                    .then_inc(head_done, 1)
                dve.wait_ge(head_done, head_seq[u] + 1)

            dve.sem_inc(drained, RING)
            dve.sem_inc(lo_done, RING)
            dve.memset(mean[:, :], 1.0 / D).then_inc(set_saved, 1)
            dve.wait_ge(set_turned, 1)
            dve.tensor_copy(vecs[:, :], b_slab[:, 0:P]).then_inc(set_saved, 1)
            for g in range(2):
                last = dve.tensor_copy(b_ada[:, g * ADA_L:(g + 1) * ADA_L], b_slab[:, P + g * P:P + g * P + ADA_L])
            link(last)
            dve.wait_ge(cond_th, 1)
            for c in range(2):
                last = dve.scalar_tensor_tensor(cond[:, :, c], set_t[:, 8 * c:8 * c + 8], 1.0,
                                                vecs[:, 112 + 8 * c:120 + 8 * c], ALU.add, ALU.mult)
            link(last)
            dve.tensor_scalar(cond[:, :, :], cond[:, :, :], 0.5, None, ALU.mult).then_inc(cond_done, 1)
            dve.tensor_tensor(both_parts[0:4, :], ident[0:4, 0:2], ident[0:4, 2:4], ALU.add)
            dve.wait_ge(cond_hi, 1)
            dve.tensor_tensor(cond_parts[:, :, 2:4], cond[:, :, :], cond_parts[:, :, 0:2].bitcast(F32), ALU.subtract)\
               .then_inc(cond_done, 1)
            dve.tensor_scalar(half_b[:, :], vecs[:, 48:112], 0.5, None, ALU.mult).then_inc(cond_done, 1)
            dve.wait_ge(table_land, 16 * 3)
            lam_s = at(TMP0 + 512, DEPTH, 4, 32)
            for l in range(DEPTH):
                link(dve.tensor_tensor(set_t[:, 16:80].rearrange("p (a d) -> p a d", a=2), lam_s[:, l, 0:4:2, :],
                                       lam_s[:, l, 1:4:2, :], ALU.mult))
                link(dve.tensor_reduce(lam_t[:, 2 * l:2 * l + 2], set_t[:, 16:80].rearrange("p (a d) -> p a d", a=2),
                                       AX_X, ALU.add))
            dve.sem_inc(lam_sum, 1)
            dve.wait_ge(lam_exp, 1)
            for l in range(DEPTH):
                link(dve.tensor_tensor(neg_lam[:, l:l + 1], lam_t[:, 2 * l + 1:2 * l + 2], lam_t[:, 2 * l:2 * l + 1],
                                       ALU.subtract))
                link(dve.tensor_scalar(neg_lam[:, l:l + 1], neg_lam[:, l:l + 1], -LAM_INIT[l], None, ALU.add))
            for m in range(KC):
                dve.wait_ge(set_turned, m + 2)
                dve.tensor_copy(x[:, m, :], banks[m % 4][:, :]).then_inc(x_done, 1)
            norm_stats(0, 0)
            for n in range(RING, 2 * RING):
                lo(n)
            for chunk in range(ADA_PRE):
                ada_chunk(chunk)
            for l in range(DEPTH):
                if l:
                    norm_stats(l, 0)
                norm_apply(l, 0)
                ffn(l, 0)
                norm(l, 1)
                mixer(l)
                norm(l, 2)
                ffn(l, 1)
            res = at(0, LT, D)
            for g in range(4):
                dve.wait_ge(set_turned, 10 + g)
                dve.tensor_copy(res[:, g // 2, 512 * (g % 2):512 * (g % 2) + 512], banks[g][:, :]).then_inc(res_saved, 1)

        @block.tensor
        def _(pe):
            def block_products(out_ap, wh, wl, xh, xl, first, last):
                pe.matmul(out_ap, wh, xh, start=first, stop=False)
                pe.matmul(out_ap, wh, xl, start=False, stop=False)
                return pe.matmul(out_ap, wl, xh, start=False, stop=last)

            def wblock(w, n, k, width_=P):
                return w[:, n % RING, k * width_:(k + 1) * width_]

            def ada_product(n, kp):
                for k in range(2):
                    for w_ in (w_hi, w_lo):
                        last = pe.matmul(b_ada_ps[0:4, :], cond_parts[:, 2 * kp + k, :],
                                         w_[:, n % RING, k * ADA_W:(k + 1) * ADA_W],
                                         start=(kp == 0 and k == 0 and w_ is w_hi),
                                         stop=(kp == ADA_JOBS - 1 and k == 1 and w_ is w_lo))
                last.then_inc(job_done, 1)

            def ada_turn():
                for q in range(ADA_Q):
                    last = pe.matmul(b_ada_t[:, 2 * q:2 * q + 2], ada_rows[:, q * P:(q + 1) * P], both_parts[0:4, :],
                                     start=True, stop=True)
                last.then_inc(ada_turned, 1)

            def ada_chunk(chunk):
                for kp in range(ADA_JOBS):
                    n = plan.ada_n0[chunk] + kp
                    pe.wait_ge(lo_done, n + 1)
                    ada_product(n, kp)
                pe.wait_ge(ada_out, chunk + 1)
                if chunk:
                    pe.wait_ge(ada_saved, chunk)
                ada_turn()

            def norm_stats(l, w):
                T, v = NORM_T[l, w], norm_no[l, w]
                pe.wait_ge(acc_done, (KC - 1) * (v + 1))
                for t in range(T // P):
                    last = pe.matmul(b_ms[:, 2 * t:2 * t + 2], n_acc[:, t * P:(t + 1) * P], mean[:, :], start=True, stop=True)
                last.then_inc(ms_done, 1)
                pe.wait_ge(rb_done, v + 1)
                for t in range(T // P):
                    last = pe.matmul(b_rstd[:, t * P:(t + 1) * P], n_rb[:, t, :], ident[:, :], start=True, stop=True)
                last.then_inc(rstd_done, 1)

            def ffn(l, w):
                T = ffn_T(l, w)
                v = norm_no[l, 0 if w == 0 else 2]
                a0 = FC * ffn_no(l, w)
                for g in plan.groups[l, w]:
                    stride = len(g.order)
                    with pe.Fori(0, g.turns) as i:
                        kp = 0
                        for o, what in enumerate(g.order):
                            n = g.up + o
                            pe.wait_ge(lo_done, stride * i + (n + 1))
                            if what == "a":
                                ada_product(n, kp)
                                kp += 1
                                continue
                            pe.wait_ge(drained, stride * i + (g.up + what - 3))
                            for k in range(KC):
                                if g.f0 == 0 and what == 0:
                                    pe.wait_ge(h_ready, KC * v + k + 1)
                                last = block_products(banks[(g.up + what) % 4][:, 0:T], wblock(w_hi, n, k),
                                                      wblock(w_lo, n, k), h_hi[:, k, 0:T], h_lo[:, k, 0:T],
                                                      k == 0, k == KC - 1)
                            last.then_inc(job_done, 1)
                        if "a" in g.order:
                            pe.wait_ge(ada_out, 1 * i + (g.chunk0 + 1))
                            pe.wait_ge(ada_saved, 1 * i + g.chunk0)
                            ada_turn()
                    if g.straight is not None:
                        ada_chunk(g.straight)

                    with pe.Fori(0, KC // 4) as i:
                        for j in range(4):
                            n = g.down + j
                            pe.wait_ge(lo_done, 4 * i + (n + 1))
                            pe.wait_ge(drained, 4 * i + (n - 3))
                            for k in range(g.nf):
                                if j == 0:
                                    pe.wait_ge(a_ready, a0 + g.f0 + k + 1)
                                last = block_products(banks[n % 4][:, 0:T], wblock(w_hi, n, k), wblock(w_lo, n, k),
                                                      a_hi[:, k, 0:T], a_lo[:, k, 0:T], k == 0, k == g.nf - 1)
                            last.then_inc(job_done, 1)

            def mixer(l):
                T, nt = toks_of(l), tiles_of(l)
                v = norm_no[l, 1]
                for rec in plan.timelines[l]:
                    s, kind = rec["step"], rec["kind"]
                    if kind == "proj":
                        n, c, kp, t = rec["n"], s[1], s[2], s[3]
                        first = n - kp
                        cw = CHUNKS[c][1]
                        if t == 0:
                            pe.wait_ge(lo_done, n + 1)
                        if kp == 0:
                            pe.wait_ge(drained, first + t - 3)
                        for kk in range(2):
                            k = 2 * kp + kk
                            if c == 0 and t == 0:
                                pe.wait_ge(h_ready, KC * v + k + 1)
                            o = banks[(first + t) % 4][:, 0:cw]
                            toks = slice(t * P, (t + 1) * P)
                            wh = w_hi[:, n % RING, kk * cw:(kk + 1) * cw]
                            wl = w_lo[:, n % RING, kk * cw:(kk + 1) * cw]
                            pe.matmul(o, h_hi[:, k, toks], wh, start=(k == 0), stop=False)
                            pe.matmul(o, h_hi[:, k, toks], wl, start=False, stop=False)
                            last = pe.matmul(o, h_lo[:, k, toks], wh, start=False, stop=(k == KC - 1))
                        if finishes(s):
                            last.then_inc(job_done, 1)
                    elif kind == "up":
                        if s[-1] > 0:
                            continue
                        n = rec["n"]
                        pe.wait_ge(lo_done, n + 1)
                        pe.wait_ge(drained, n)
                        pe.wait_ge(slab_saved, c_slab[l] + 1)
                        ks, cw = ([0, 1], 384) if s[1] == "q" else ([2], 512)
                        for t in range(nt if s[1] == "q" else TT):
                            toks = slice(t * P, (t + 1) * P)
                            for q, k in enumerate(ks):
                                o = banks[t][:, 0:cw]
                                wh, wl = (w_[:, n % RING, q * cw:(q + 1) * cw] for w_ in (w_hi, w_lo))
                                pe.matmul(o, cT_hi[:, k, toks], wh, start=(q == 0), stop=False)
                                pe.matmul(o, cT_hi[:, k, toks], wl, start=False, stop=False)
                                last = pe.matmul(o, cT_lo[:, k, toks], wh, start=False, stop=(q == len(ks) - 1))
                        last.then_inc(job_done, 1)
                    elif kind in ("gate", "out"):
                        n, piece = rec["n"], s[-1]
                        if piece == 0:
                            pe.wait_ge(lo_done, n + 1)
                            pe.wait_ge(drained, plan.need_drained[n])
                        src_hi, src_lo = (h_hi, h_lo) if kind == "gate" else (a_hi, a_lo)
                        for k in range(2 * piece, 2 * piece + 2):
                            if kind == "out" and s[1] == 0:
                                pe.wait_ge(y_ready, KC * l + k + 1)
                            last = block_products(banks[n % 4][:, 0:T], wblock(w_hi, n, k), wblock(w_lo, n, k),
                                                  src_hi[:, k, 0:T], src_lo[:, k, 0:T], k == 0, k == KC - 1)
                        if finishes(s):
                            last.then_inc(job_done, 1)
                    elif kind == "branch":
                        n = rec["n"]
                        pe.wait_ge(lo_done, n + 1)
                        pe.wait_ge(drained, plan.need_drained[n])
                        pe.wait_ge(slab_saved, o_slab[l, s[1]] + 1)
                        for k in range(2):
                            last = block_products(banks[n % 4][:, 0:T], wblock(w_hi, n, k), wblock(w_lo, n, k),
                                                  oT_hi[s[1] % 2][:, k, 0:T], oT_lo[s[1] % 2][:, k, 0:T], k == 0, k == 1)
                        last.then_inc(job_done, 1)
                    elif kind in ("slab", "turn_out", "turn_c"):
                        xno = rec["x"]
                        if kind == "slab":
                            pe.wait_ge(normed, normed_for[l, s[1]])
                            tiles = slab_tiles(l, s[2])
                            srcs = [slab_source(s[1], s[2], s[3], t) for t in range(tiles)]
                        elif kind == "turn_out":
                            pe.wait_ge(head_done, heads_before[xno])
                            if xno in sub_before:
                                pe.wait_ge(normed, sub_before[xno])
                            srcs = [outs[:, t, s[2] * P:(s[2] + 1) * P] for t in range(nt)]
                        else:
                            pe.wait_ge(normed, normed_for[l, "mlac"])
                            srcs = [mla_in[:, t, s[1] * P:(s[1] + 1) * P] for t in range(TT)]
                        if xno:
                            pe.wait_ge(slab_saved, xno)
                        for t, src in enumerate(srcs):
                            w_ = math.prod(src.shape[1:])
                            last = pe.transpose(b_slab[0:w_, t * P:(t + 1) * P], src, ident[:, :])
                        last.then_inc(slab_done, 1)
                    elif kind == "score":
                        u = rec["u"]
                        b, head, t = s[1:]
                        sq, sk, p0, d = unit_ap(b, head)
                        pe.wait_ge(slab_saved, slab_for[l, b] + 1)
                        if u:
                            pe.wait_ge(exp_done, u)
                        rows = slice(p0, p0 + d)
                        toks = slice(t * P, (t + 1) * P)
                        qu = qT_u[rows, sq, toks]
                        if t >= LT:
                            last = pe.matmul(b_score[:, 0:S], qu, kT[rows, sk, S:NT], start=True, stop=True)
                        elif b == "na":
                            pe.wait_ge(bias_built, 4 * l + head + 1)
                            pe.matmul(b_score[:, 0:S], qu, kT[rows, sk, 0:S], start=True, stop=False)
                            pe.matmul(b_score[:, 0:S], ident[:, :], bias_m[:, head % 2, t, :], start=False, stop=True)
                            last = pe.matmul(b_score[:, S:NT], qu, kT[rows, sk, S:NT], start=True, stop=True)
                        else:
                            pe.matmul(b_score[:, 0:S], qT_r[rows, sq, toks], kT[rows, sk, 0:S], start=True, stop=True)
                            last = pe.matmul(b_score[:, S:NT], qu, kT[rows, sk, S:NT], start=True, stop=True)
                        last.then_inc(score_done, 1)
                    elif kind == "turn":
                        u, t = rec["u"], s[3]
                        pe.wait_ge(exp_done, u + 1)
                        if u:
                            pe.wait_ge(turn_saved, u)
                        for q in range(4 if t < LT else 2):
                            last = pe.transpose(b_turn[:, q * P:(q + 1) * P], prob[:, q * P:(q + 1) * P], ident[:, :])
                        last.then_inc(turn_done, 1)
                    elif kind == "mix":
                        u = rec["u"]
                        b, head, t = s[1:]
                        pe.wait_ge(turn_saved, u + 1)
                        if t == 0 and head_first[u]:
                            pe.wait_ge(head_done, head_first[u])
                        tiles = range(TT) if t < LT else range(LT, TT)
                        for q, kt in enumerate(tiles):
                            last = pe.matmul(b_o[:, 64 * t:64 * t + 64], probT[:, q, :], value_ap(b, head, kt),
                                             start=(q == 0), stop=(q == len(tiles) - 1))
                        last.then_inc(mix_done, 1)

            pe.sem_inc(job_done, RING)
            stage = at(TMP0, 4, P)
            stage_x = at(Q0, 4, D)
            pe.wait_ge(const_land, 16 * 6)
            pe.transpose(b_slab[:, 0:P], stage[:, 0, :], ident[:, :])
            for g in range(2):
                last = pe.transpose(b_slab[:, P + g * P:P + g * P + ADA_L], stage[0:ADA_L, 1 + g, :],
                                    ident[0:ADA_L, 0:ADA_L])
            last.then_inc(set_turned, 1)
            pe.wait_ge(in_land, 32)
            for m in range(KC):
                if m >= 4:
                    pe.wait_ge(x_done, m - 3)
                for t in range(TT):
                    last = pe.transpose(banks[m % 4][:, t * P:(t + 1) * P], stage_x[:, t, m * P:(m + 1) * P], ident[:, :])
                last.then_inc(set_turned, 1)
            pe.wait_ge(set_saved, 1)
            norm_stats(0, 0)
            pe.wait_ge(cond_done, 2)
            for chunk in range(ADA_PRE):
                ada_chunk(chunk)
            for l in range(DEPTH):
                if l:
                    norm_stats(l, 0)
                ffn(l, 0)
                norm_stats(l, 1)
                mixer(l)
                norm_stats(l, 2)
                ffn(l, 1)
            for g in range(4):
                t, half = g // 2, g % 2
                pe.wait_ge(drained, plan.total)
                for q in range(4):
                    last = pe.transpose(banks[g][:, q * P:(q + 1) * P], x[:, 4 * half + q, t * P:(t + 1) * P], ident[:, :])
                last.then_inc(set_turned, 1)


_INS = ["x", "c", "ctx", "c_ctx", "w_ada", "b_ada", "norm_g", "ffn_w1", "ffn_w3", "ffn_w2", "w_in", "na_g_q", "na_g_k",
        "na_rpb", "gqa_g_q", "gqa_g_k", "diff_g_q", "diff_g_k", "diff_lambda", "diff_g_sub", "mla_g_cq", "mla_g_ckv",
        "mla_w_uq", "mla_w_ukv", "mla_g_q", "mla_g_k", "w_gate", "b_gate", "w_branch", "w_out"]


def shape_tables():
    import numpy as np
    col = np.arange(GRID_W)
    c0 = np.clip(col - 8, 0, GRID_W - 16)
    inside = (col[None, :] >= c0[:, None]) & (col[None, :] < c0[:, None] + 16)
    window = np.where(inside, 0.0, -1e30).astype(np.float32)
    tok = np.arange(S)
    tables = []
    for d in (64, 32):
        n = d // 4
        inv = (np.float32(10000.0) ** (-np.arange(n, dtype=np.float32) / np.float32(n))).astype(np.float32)
        ar = (tok // GRID_W).astype(np.float32)[:, None] * inv[None, :]
        ac = (tok % GRID_W).astype(np.float32)[:, None] * inv[None, :]
        ang = np.concatenate([ar, ar, ac, ac], axis=1).astype(np.float64)
        sign = np.concatenate([-np.ones(n), np.ones(n), -np.ones(n), np.ones(n)])
        tables += [np.cos(ang), np.sin(ang) * sign]
    return {"ident": np.eye(P, dtype=np.float32), "mask": np.concatenate([window, window], axis=0),
            "rope": np.concatenate(tables, axis=1).astype(np.float32)}


def kernel(**inputs):
    import numpy as _np
    import concourse.bacc as _bacc
    from concourse import mybir as _mybir
    from concourse.bass_utils import run_bass_kernel_spmd as _run

    nc = _bacc.Bacc("TRN2", target_bir_lowering=False, num_devices=1)
    arrays, A = {}, {}
    for name in _INS:
        arrays[f"in_{name}"] = _np.ascontiguousarray(inputs[name])
    for name, a in shape_tables().items():
        arrays[f"in_{name}"] = a
    for name, a in arrays.items():
        A[name[3:]] = nc.dram_tensor(name, a.shape, _mybir.dt.from_np(a.dtype), kind="ExternalInput").ap()
    out = nc.dram_tensor("out_0", (1, S, D), F32, kind="ExternalOutput").ap()
    build(nc, A, out)
    r = _run(nc, [arrays], core_ids=[0])
    return r.results[0]["out_0"]
```

```python
import math
from contextlib import ExitStack

import concourse.bass as bass
from concourse import mybir
from concourse.alu_op_type import AluOpType as ALU

F32 = mybir.dt.float32
F32R = mybir.dt.float32r
ACT = mybir.ActivationFunctionType
AX_X = mybir.AxisListType.X

P = 128
D = 1024
KC = D // P
S = 256
NT = 512
TT = NT // P
LT = S // P
DEPTH = 2
GRID_W = 64
EPS = 1e-6
FC = 22
GROUPS = [(0, 8), (8, 8), (16, 6)]
NMOD = 9
IN_COLS = 2464
RPB = 15 * 31
RING = 4
ADA_W = 512
ADA_Q = ADA_W // P
ADA_JOBS = 4
ADA_L = NMOD * KC
ADA_LC = ADA_L // ADA_Q
ADA_PRE = 2 * KC // ADA_Q
UP = [0, 1, 2, 3]
UP_ADA = [0, "a", 1, "a", 2, "a", "a", 3]
LAM_INIT = [0.8 - 0.6 * math.exp(-0.3 * i) for i in range(DEPTH)]

NA0, GQA0, DIFF0, MLA0, PIN_END = 0, 3072, 5120, 8192, 9856
Q0, P0, PT0, OUT0, BM0, TMP0, ARENA = 9856, 12416, 13440, 13952, 14976, 16000, 17536
SEGMENTS = [(0, 768, NA0, 768), (768, 1280, GQA0, 512), (1280, 2048, DIFF0, 768), (2048, 2464, MLA0, 416)]
CHUNKS = [(0, 512), (512, 512), (1024, 512), (1536, 512), (2048, 416)]

G_NA, G_GQA, G_DIFF, G_SUB, G_CQ, G_CKV, G_MQ, G_MK, G_END = 0, 128, 320, 384, 448, 704, 832, 928, 1024

VAR0 = {"na": 0, "gqa": 32, "diff": 56, "mlac": 120, "mlaqk": 128, "sub": 160}
VAR_END = 176

BRANCHES = ["na", "gqa", "diff", "mla0", "mla1"]
HEAD_D = {"na": 64, "gqa": 64, "diff": 32, "mla0": 96, "mla1": 96}
SCALE = {b: float(d) ** -0.5 for b, d in HEAD_D.items()}


PIECES = 4


def spread(steps, pieces):
    out, done = [], 0
    for i, s in enumerate(steps):
        out += s if isinstance(s, list) else [s]
        want = (i + 1) * len(pieces) // len(steps)
        out += pieces[done:want]
        done = want
    return out + pieces[done:]


def job_pieces(kind, *a):
    return [(kind, *a, piece) for piece in range(PIECES)]


def finishes(s):
    return s[-1] == PIECES - 1


def merge_jobs(b, ms):
    out = []
    for m in ms:
        out += job_pieces("gate", b, m) + [("branch", b, m)]
    return out


def heads_of(b):
    if b == "mla0":
        return [0, 1]
    if b == "mla1":
        return [2, 3]
    return list(range(8 if b == "diff" else 4))


class Group:
    pass


class Plan:

    def __init__(self):
        self.timelines = []
        self.units = []
        self.head_last = []
        self.slabs = 0
        self.norms = 0
        n = RING
        self.ada_n0 = {}
        self.groups = {}
        self.chunks = 0
        for _ in range(ADA_PRE):
            n = self.place_chunk(n)
        self.ffn_n0 = {}
        self.need_drained = {}
        self.jobs = {}
        for layer in range(DEPTH):
            n = self.place_ffn(layer, 0, n)
            self.timelines.append(self.timeline(layer, n))
            n = self.n
            n = self.place_ffn(layer, 1, n)
        self.total = n

    def place_chunk(self, n):
        self.ada_n0[self.chunks] = n
        self.chunks += 1
        return n + ADA_JOBS

    def place_ffn(self, layer, which, n):
        self.ffn_n0[layer, which] = n
        self.groups[layer, which] = []
        for gi, (f0, nf) in enumerate(GROUPS):
            g = Group()
            g.f0, g.nf, g.turns, g.up, g.chunk0 = f0, nf, nf // 2, n, self.chunks
            with_ada = layer == 0 or (which == 0 and gi != 1)
            g.order = UP_ADA if with_ada else UP
            n += g.turns * len(g.order)
            self.chunks += g.turns if with_ada else 0
            g.straight = None
            if (layer, which) == (0, 0):
                g.straight = self.chunks
                n = self.place_chunk(n)
            g.down = n
            n += KC
            self.groups[layer, which].append(g)
        return n

    def timeline(self, layer, n):
        nt = TT if layer == 0 else LT

        def slabs(b):
            nq = 2
            out = [("slab", b, "qu", s) for s in range(nq)]
            if b != "na":
                out += [("slab", b, "qr", s) for s in range(nq)]
            return out + [("slab", b, "k", s) for s in range(1 if b == "gqa" else 2)]

        def attention(b):
            us = [(b, h, t) for h in heads_of(b) for t in range(nt)]
            out = []
            for i in range(len(us) + 2):
                turn = []
                if i >= 2:
                    turn.append(("mix", *us[i - 2]))
                    if us[i - 2][2] == nt - 1:
                        turn.append(("head", us[i - 2][0], us[i - 2][1]))
                if 1 <= i <= len(us):
                    turn.append(("turn", *us[i - 1]))
                if i < len(us):
                    turn.append(("score", *us[i]))
                out.append(turn)
            return out

        def outs(b):
            return [("turn_out", b, s) for s in range(2)]

        proj = [x for c in range(len(CHUNKS)) for kp in range(4) for x in job_pieces("proj", c, kp)]
        merge = [merge_jobs(b, range(8)) for b in range(4)]
        na, gqa, diff = attention("na"), attention("gqa"), attention("diff")
        def norm(name):
            return [("stats", name, t) for t in range(nt if name == "sub" else TT)] + [("norm", name)]

        def laced(*lists):
            marked = [((i + 1) / (len(x) + 1), q, i, e) for q, x in enumerate(lists) for i, e in enumerate(x)]
            return [m[-1] for m in sorted(marked, key=lambda m: m[:3])]

        mid = len(na) // 2
        steps = [("gain",)] + proj[:32] + norm("na") + proj[32:52]
        steps += spread(slabs("na") + laced(na[:mid], norm("gqa")), proj[52:64])
        steps += spread(laced(na[mid:], norm("diff")), proj[64:74])
        steps += spread(slabs("gqa") + outs(0), proj[74:])
        steps += spread(laced(gqa, norm("mlac")), merge[0][:25])
        steps += spread(slabs("diff") + [("turn_c", s) for s in range(3)] + outs(1), merge[0][25:35])
        cut = [len(diff) // 6, len(diff) // 3, 2 * len(diff) // 3]
        steps += spread(diff[:cut[0]], merge[0][35:])
        steps += job_pieces("up", "q") + diff[cut[0]] + job_pieces("up", "kv") + [("build_k",)]
        steps += spread(diff[cut[0] + 1:cut[1]], merge[1][:6])
        steps += spread(laced(diff[cut[1]:cut[2]], norm("mlaqk")), merge[1][6:18])
        steps += spread(diff[cut[2]:], merge[1][18:30])
        steps += spread(norm("sub") + slabs("mla0"), merge[1][30:])
        steps += spread(outs(2), merge[2][:4])
        steps += spread(attention("mla0") + slabs("mla1") + attention("mla1"), merge[2][4:37])
        steps += merge[2][37:] + spread(outs(3), merge[3][:4]) + merge[3][4:]
        steps += [("y_last",)]
        steps += [x for m in range(8) for x in job_pieces("out", m)]

        done, bank_user = [], {b: n - 4 + ((b - n) % 4) for b in range(4)}
        order = [s for s in steps]
        self.n = n
        unit_of, cur = {}, None
        for s in order:
            kind = s[0]
            rec = {"step": s, "kind": kind}
            if kind in ("proj", "gate", "up", "out"):
                if s[-1] == 0:
                    cur = self.n
                    self.n += 1
                rec["n"] = cur
                self.jobs[cur] = s
            elif kind == "branch":
                rec["n"] = self.n
                self.jobs[self.n] = s
                self.n += 1
            elif kind == "score":
                unit_of[s[1:]] = len(self.units)
                rec["u"] = len(self.units)
                self.units.append((layer, *s[1:]))
            elif kind in ("turn", "mix"):
                rec["u"] = unit_of[s[1:]]
            elif kind == "head":
                rec["h"] = len(self.head_last)
                rec["u"] = unit_of[(s[1], s[2], nt - 1)]
                self.head_last.append(rec["u"])
            elif kind in ("slab", "turn_out", "turn_c"):
                rec["x"] = self.slabs
                self.slabs += 1
            elif kind == "norm":
                rec["v"] = self.norms
                self.norms += 1
            done.append(rec)
        done = self.place_later(done)
        for rec in done:
            if "n" not in rec or rec["n"] in self.need_drained:
                continue
            m, s = rec["n"], rec["step"]
            if s[0] == "proj":
                c0 = m - s[2]
                self.need_drained[m] = None
            elif s[0] == "up":
                self.need_drained[m] = m
                for b in range(4):
                    bank_user[b] = m
            else:
                self.need_drained[m] = bank_user[m % 4] + 1 if m % 4 in bank_user else m - 3
                self.need_drained[m] = max(self.need_drained[m], m - 3)
                bank_user[m % 4] = m
        return done


    @staticmethod
    def place_later(line):
        out, pending = [], []
        for rec in line:
            kind = rec["kind"]
            ends_job = kind == "branch" or ("n" in rec and finishes(rec["step"]))
            if ends_job or kind in ("stats", "norm", "y_last", "turn_out", "turn_c"):
                out += pending
                pending = []
            out.append(rec)
            if kind == "branch":
                pending.append({"kind": "add", "step": ("add",) + rec["step"][1:]})
            if ends_job:
                pending.append({"kind": "split", "step": ("split",), "after": rec["n"]})
            if kind == "score":
                out += pending
                pending = []
        return out + pending


def build(nc, A, out):
    plan = Plan()
    scratch = nc.dram_tensor("rpb_rows", [64, DEPTH * 4 * RPB], F32, kind="Internal").ap()
    row = DEPTH * 4 * RPB

    with ExitStack() as ctx:
        def sb(name, shape, dt=F32):
            return ctx.enter_context(nc.sbuf_tensor(name, shape, dt))

        def sem(name):
            return ctx.enter_context(nc.semaphore(name))

        x = sb("x", [P, KC, NT])
        h_hi, h_lo = sb("h_hi", [P, KC, NT], F32R), sb("h_lo", [P, KC, NT], F32R)
        a_hi, a_lo = sb("a_hi", [P, 8, NT], F32R), sb("a_lo", [P, 8, NT], F32R)
        w_raw = sb("w_raw", [P, RING, 1024])
        w_hi, w_lo = sb("w_hi", [P, RING, 1024], F32R), sb("w_lo", [P, RING, 1024], F32R)
        arena = sb("arena", [P, ARENA])
        rope = sb("rope", [P, LT, 192])
        gains = sb("gains", [P, G_END])
        mods = sb("mods", [P, DEPTH * ADA_L, 2])
        vecs = sb("vecs", [P, P])
        b_ada = sb("b_ada", [P, DEPTH * ADA_L])
        cond = sb("cond", [P, KC, 2])
        both_parts = sb("both_parts", [P, 2])
        cond_parts = sb("cond_parts", [P, KC, 4], F32R)
        ident = sb("ident", [P, P])
        mean = sb("mean", [P, 2])
        root_set = sb("root_set", [P, 6])
        tok_var = sb("tok_var", [P, 4])
        mask = sb("mask", [P, GRID_W])
        scale_g = sb("scale_g", [P, KC, 2])
        gate_s = sb("gate_s", [P, KC, 2])
        var = sb("var", [P, VAR_END])
        rowsum = sb("rowsum", [P, 2, 4])
        rinv = sb("rinv", [P, 4])
        top = sb("top", [P, 2])
        neg_top = sb("neg_top", [P, 2])
        neg_lam = sb("neg_lam", [P, DEPTH])
        lam_t = sb("lam_t", [P, 8])
        half_b = sb("half_b", [P, 64])
        banks = [ctx.enter_context(nc.psum_tensor(f"bank{i}", [P, 512], F32)) for i in range(8)]
        b_score, b_turn, b_slab, b_o = banks[4], banks[5], banks[6], banks[7]
        b_ada_ps, b_ada_t = banks[4], banks[7]
        b_rstd, b_ms = banks[5], banks[6]

        def at(o, *shape):
            v = arena[:, o:o + math.prod(shape)]
            if len(shape) == 1:
                return v
            names = "abcd"[:len(shape)]
            return v.rearrange(f"p ({' '.join(names)}) -> p {' '.join(names)}",
                               **{k: n for k, n in zip(names, shape)})

        na_in, gqa_in, diff_in, mla_in = at(NA0, 4, 768), at(GQA0, 4, 512), at(DIFF0, 4, 768), at(MLA0, 4, 416)
        kv_up = at(GQA0, 4, 512)
        qT_u, qT_r, kT = at(Q0, 2, 512), at(Q0 + 1024, 2, 256), at(Q0 + 1536, 2, 512)
        prob = at(P0, 512)
        gate_buf = at(P0 + 512, 512)
        probT = at(PT0, 4, P)
        outs = at(OUT0, 4, 256)
        set_t = at(OUT0, 128)
        ada_rows = at(OUT0 + 128, ADA_W)[0:4, :]
        bias_m = at(BM0, 2, LT, 256)
        sq_t = at(TMP0, 512)
        swap_t = at(TMP0 + 512, 256)
        rot_q = at(TMP0 + 768, 2, 256)
        rot_m = at(TMP0 + 768, 2, 384)
        th = at(Q0, 2, 512)
        s_t = at(Q0 + 1024, 512)
        a_t = at(Q0 + 1536, 2, 512)
        n_sq = at(6144, 2, 512)
        n_xs = at(0, KC, 512)
        n_t = at(4096, 4, 512)
        n_acc, n_rb = at(7168, 512), at(7680, 4, P)

        def y_of(m, T=NT):
            return arena[:, m * 512:m * 512 + T] if m < 6 else arena[:, BM0 + (m - 6) * 512:BM0 + (m - 6) * 512 + T]

        oT_hi, oT_lo = [[a[:, o:o + 2, :] for o in (4, 6)] for a in (a_hi, a_lo)]
        cT_hi, cT_lo = a_hi[:, 0:3, :], a_lo[:, 0:3, :]

        in_land = sem("in_land"); const_land = sem("const_land"); rpb_land = sem("rpb_land")
        gain_land = sem("gain_land"); bias_land = [sem(f"bias_land{i}") for i in range(4)]
        landed = [sem(f"landed{i}") for i in range(RING)]
        hi_done = sem("hi_done"); lo_done = sem("lo_done"); job_done = sem("job_done"); drained = sem("drained")
        ada_out = sem("ada_out"); ada_turned = sem("ada_turned"); ada_saved = sem("ada_saved")
        cond_hi = sem("cond_hi")
        set_turned = sem("set_turned"); set_saved = sem("set_saved")
        cond_th = sem("cond_th"); cond_done = sem("cond_done"); lam_sum = sem("lam_sum"); lam_exp = sem("lam_exp")
        x_done = sem("x_done"); sq_done = sem("sq_done"); acc_done = sem("acc_done"); ms_done = sem("ms_done")
        mv_done = sem("mv_done"); mr_done = sem("mr_done"); rb_done = sem("rb_done"); rstd_done = sem("rstd_done")
        scale_done = sem("scale_done"); xs_done = sem("xs_done"); hc_ready = sem("hc_ready")
        t_done = sem("t_done"); hh_done = sem("hh_done"); h_ready = sem("h_ready")
        th_done = sem("th_done"); ah_done = sem("ah_done"); a_ready = sem("a_ready")
        nv_done = sem("nv_done"); nr_done = sem("nr_done"); normed = sem("normed")
        slab_done = sem("slab_done"); slab_saved = sem("slab_saved"); slab_hi = sem("slab_hi")
        score_done = sem("score_done"); top_done = sem("top_done"); exp_done = sem("exp_done")
        turn_done = sem("turn_done"); turn_saved = sem("turn_saved"); mix_done = sem("mix_done")
        head_done = sem("head_done"); bias_built = sem("bias_built")
        gate_th = sem("gate_th"); y_sum = sem("y_sum"); yh_done = sem("yh_done"); y_ready = sem("y_ready")
        k_built = sem("k_built"); res_saved = sem("res_saved"); table_land = sem("table_land"); out_done = sem("out_done")
        dve_step = sem("dve_step"); pool_step = sem("pool_step")

        NORM_T = {(0, 0): NT, (0, 1): NT, (0, 2): NT, (1, 0): NT, (1, 1): NT, (1, 2): S}
        norm_no = {k: i for i, k in enumerate(sorted(NORM_T))}
        tiles_of = lambda l: TT if l == 0 else LT
        toks_of = lambda l: NT if l == 0 else S
        ffn_T = lambda l, w: S if (l, w) == (1, 1) else NT
        ffn_no = lambda l, w: 2 * l + w

        def mod(l, i, m=None):
            o = l * ADA_L + i * KC
            return mods[:, o:o + KC, :] if m is None else mods[:, o + m, :]

        def halves(T):
            return [(0, slice(0, S))] + ([(1, slice(S, NT))] if T == NT else [])

        def unit_ap(b, head):
            if b == "na":
                return head // 2, head // 2, 64 * (head % 2), 64
            if b == "gqa":
                return head % 2, 0, 64 * (head // 2), 64
            if b == "diff":
                return head // 4, head // 4, 32 * (head % 4), 32
            return head % 2, head % 2, 0, 96

        def value_ap(b, head, t):
            if b == "na":
                return na_in[:, t, 512 + 64 * head:576 + 64 * head]
            if b == "gqa":
                return gqa_in[:, t, 384 + 64 * (head // 2):448 + 64 * (head // 2)]
            if b == "diff":
                return diff_in[:, t, 512 + 64 * (head // 2):576 + 64 * (head // 2)]
            return kv_up[:, t, 128 * head + 64:128 * head + 128]

        def slab_source(b, what, s, t):
            if b == "na":
                o = (0 if what == "qu" else 256) + 128 * s
                return na_in[:, t, o:o + 128]
            if b == "gqa":
                if what == "k":
                    return gqa_in[:, t, 256:384]
                return (gqa_in if what == "qu" else rot_q)[:, t, 128 * s:128 * s + 128]
            if b == "diff":
                if what == "qr":
                    return rot_q[:, t, 128 * s:128 * s + 128]
                o = (0 if what == "qu" else 256) + 128 * s
                return diff_in[:, t, o:o + 128]
            hh = 2 * int(b[-1]) + s
            if what == "k":
                return diff_in[:, t, 96 * hh:96 * hh + 96]
            return (mla_in if what == "qu" else rot_m)[:, t, 96 * hh:96 * hh + 96]

        def slab_tiles(l, what):
            return {"qu": tiles_of(l), "qr": LT, "k": TT}[what]

        def slab_dest(what, s):
            return {"qu": qT_u, "qr": qT_r, "k": kT}[what][:, s, :]

        def norm_views(l, name, t):
            def g(o, n, d, rep):
                v = gains[:, o:o + n * d].rearrange("p (n d) -> p n d", n=n)
                return v.unsqueeze(2).broadcast_to([P, n, rep, d])
            keys_only = t >= tiles_of(l)
            if name == "na":
                return [(na_in[:, t, 256:512], 4, 64, (1, 4), g(G_NA + 64, 1, 64, 4))] if keys_only else \
                    [(na_in[:, t, 0:512], 8, 64, (2, 4), g(G_NA, 2, 64, 4))]
            if name == "gqa":
                return [(gqa_in[:, t, 256:384], 2, 64, (1, 2), g(G_GQA + 128, 1, 64, 2))] if keys_only else \
                    [(gqa_in[:, t, 0:384], 6, 64, (3, 2), g(G_GQA, 3, 64, 2))]
            if name == "diff":
                return [(diff_in[:, t, 256:512], 8, 32, (1, 8), g(G_DIFF + 32, 1, 32, 8))] if keys_only else \
                    [(diff_in[:, t, 0:512], 16, 32, (2, 8), g(G_DIFF, 2, 32, 8))]
            if name == "mlac":
                kv = (mla_in[:, t, 256:384], 1, 128, (1, 1), g(G_CKV, 1, 128, 1))
                return [kv] if keys_only else [(mla_in[:, t, 0:256], 1, 256, (1, 1), g(G_CQ, 1, 256, 1)), kv]
            if name == "mlaqk":
                k = (diff_in[:, t, 0:384], 4, 96, (1, 4), g(G_MK, 1, 96, 4))
                return [k] if keys_only else [(mla_in[:, t, 0:384], 4, 96, (1, 4), g(G_MQ, 1, 96, 4)), k]
            return [(outs[:, t, :], 4, 64, (1, 4), g(G_SUB, 1, 64, 4))]

        def norm_tiles(name, l):
            return tiles_of(l) if name == "sub" else TT

        def norm_var(l, name):
            tiles = range(norm_tiles(name, l))
            views = [norm_views(l, name, t) for t in tiles]
            o, where, ends = VAR0[name], [[None] * len(v) for v in views], []
            for d in sorted({part[2] for v in views for part in v}):
                for t in tiles:
                    for i, part in enumerate(views[t]):
                        if part[2] == d:
                            where[t][i] = var[:, o:o + part[1]]
                            o += part[1]
                ends.append((d, o))
            return where, ends

        x_jobs = {norm_no[l, 1]: plan.groups[l, 0][-1].down for l in range(DEPTH)}
        x_jobs.update({norm_no[l, 2]: plan.ffn_n0[l, 1] - KC for l in range(DEPTH)})
        x_jobs[norm_no[1, 0]] = plan.groups[0, 1][-1].down
        ada_saved_by = {norm_no[l, w]: plan.groups[l, 0 if w == 0 else 1][0].chunk0 for l in range(DEPTH) for w in range(3)}

        def c_tiles(l, s):
            return tiles_of(l) if s < 2 else TT

        def proj_cols(l, c, t):
            cw = CHUNKS[c][1]
            return ((256, cw), (0, 256), (0, 256), (0, cw), (256, cw))[c] if t >= tiles_of(l) else (0, cw)

        def next_norm(l, w):
            return (l, 1) if w == 0 else ((l + 1, 0) if l + 1 < DEPTH else None)

        def shift_no(l, w):
            return l * ADA_L + 3 * w * KC

        def slab_shape(l, s):
            return (96 if s[1].startswith("mla") else P), P * slab_tiles(l, s[2])

        def width(n):
            if n in plan.jobs:
                s = plan.jobs[n]
                if s[0] == "proj":
                    return 2 * CHUNKS[s[1]][1]
                if s[0] == "up":
                    return 768 if s[1] == "q" else 512
                return 256 if s[0] == "branch" else 1024
            for groups in plan.groups.values():
                for g in groups:
                    if g.down <= n < g.down + KC:
                        return g.nf * P
            return 1024

        gate_no, prev_branch, y_last_job, up_job, proj_job, branch_job = {}, {}, {}, {}, {}, {}
        slab_for, o_slab, c_slab, slab_hi_no, rot_free = {}, {}, {}, {}, {}
        normed_for, heads_before, sub_before, head_seq, head_first = {}, {}, {}, {}, {}
        n_head, n_sub, last_branch = 0, 0, 0
        for l, line in enumerate(plan.timelines):
            for rec in line:
                s, kind = rec["step"], rec["kind"]
                if kind == "gate" and finishes(s):
                    gate_no[rec["n"]] = len(gate_no)
                    prev_branch[rec["n"]] = last_branch
                elif kind == "branch":
                    last_branch = y_last_job[l] = branch_job[l, s[1], s[2]] = rec["n"]
                elif kind == "up":
                    up_job[l] = rec["n"]
                elif kind == "proj":
                    proj_job.setdefault(l, rec["n"])
                elif kind == "slab":
                    slab_for[l, s[1]] = rec["x"]
                    if s[2] == "qr":
                        after = {"gqa": (l, "diff"), "diff": (l, "mlaqk"), "mla0": None, "mla1": (l + 1, "gqa")}[s[1]]
                        if after:
                            rot_free[after] = rec["x"] + 1
                    if s[1] == "diff":
                        rot_free[l, "mlaqk"] = rec["x"] + 1
                elif kind in ("turn_out", "turn_c"):
                    slab_hi_no[rec["x"]] = len(slab_hi_no)
                    if kind == "turn_c":
                        c_slab[l] = rec["x"]
                    else:
                        o_slab[l, s[1]] = rec["x"]
                        heads_before[rec["x"]] = n_head
                        if s[1] == 2:
                            sub_before[rec["x"]] = n_sub
                elif kind == "norm":
                    normed_for[l, s[1]] = rec["v"] + 1
                    if s[1] == "mlaqk":
                        normed_for[l, "mla0"] = normed_for[l, "mla1"] = rec["v"] + 1
                    if s[1] == "sub":
                        n_sub = rec["v"] + 1
                elif kind == "head":
                    head_seq[rec["u"]] = n_head
                    n_head += 1
                elif kind == "score" and s[3] == 0:
                    head_first[rec["u"]] = len(head_first)

        rpb_t = A["na_rpb"].tensor

        def load_bias(queue, l, head):
            for t in range(LT):
                for r in range(2):
                    o = (l * 4 + head) * RPB + (7 - (2 * t + r)) * 31 + 15
                    src = bass.AP(scratch.tensor, o, [[row - 1, 64], [31, 4], [1, 64]])
                    dst = bias_m[64 * r:64 * r + 64, head % 2, t, :].rearrange("p (a c) -> p a c", a=4)
                    queue.dma_start(dst, src).then_inc(bias_land[head], 16)

        block = ctx.enter_context(nc.Block())

        @block.sync
        def _(sp):
            stage_x = at(Q0, 4, D)
            w_ada = [A["w_ada"][l].rearrange("(k p) n -> p k n", p=P) for l in range(DEPTH)]

            def ada_jobs(chunk):
                l, c = divmod(chunk, ADA_LC)
                for kp in range(ADA_JOBS):
                    n = plan.ada_n0[chunk] + kp
                    load(n, w_raw[:, n % RING, :].rearrange("p (k c) -> p k c", k=2),
                         w_ada[l][:, 2 * kp:2 * kp + 2, c * ADA_W:(c + 1) * ADA_W])

            sp.dma_start(ident[:, :], A["ident"]).then_inc(const_land, 16)
            stage = at(TMP0, 4, P)
            sp.dma_start(stage[0:48, 0, :], A["norm_g"].rearrange("l w (m p) -> (l w m) p", p=P)).then_inc(const_land, 16)
            sp.dma_start(stage[48:112, 0, :], A["b_gate"].rearrange("l w (m p) -> (l w m) p", p=P)).then_inc(const_land, 16)
            sp.dma_start(stage[112:120, 0, :], A["c"].rearrange("b (m p) -> (b m) p", p=P)).then_inc(const_land, 16)
            sp.dma_start(stage[120:128, 0, :], A["c_ctx"].rearrange("(m p) -> m p", p=P)).then_inc(const_land, 16)
            sp.dma_start(stage[0:ADA_L, 1:3, :], A["b_ada"].rearrange("l (m p) -> m l p", p=P)).then_inc(const_land, 16)
            sp.dma_start(stage_x[:, 0:2, :], A["x"][0].rearrange("(t p) d -> p t d", p=P)).then_inc(in_land, 16)
            sp.dma_start(stage_x[:, 2:4, :], A["ctx"][0].rearrange("(t p) d -> p t d", p=P)).then_inc(in_land, 16)

            def load(n, dst, src):
                sp.wait_ge(lo_done, n - RING + 1)
                sp.dma_start(dst, src).then_inc(landed[n % RING], 16)

            def ffn(l, w):
                w13 = [A[k][l, w].rearrange("(k p) n -> p k n", p=P) for k in ("ffn_w1", "ffn_w3")]
                w2 = A["ffn_w2"][l, w].rearrange("(k p) n -> p k n", p=P)

                def slot(n, blocks):
                    return w_raw[:, n % RING, 0:blocks * P].rearrange("p (k c) -> p k c", k=blocks)

                for g in plan.groups[l, w]:
                    stride = len(g.order)
                    with sp.Fori(0, g.turns) as i:
                        kp = 0
                        for o, what in enumerate(g.order):
                            n = g.up + o
                            sp.wait_ge(lo_done, stride * i + (n - RING + 1))
                            if what == "a":
                                la, c = divmod(g.chunk0, ADA_LC)
                                src = w_ada[la][:, 2 * kp:2 * kp + 2, bass.ds(ADA_W * i + c * ADA_W, ADA_W)]
                                dst = w_raw[:, n % RING, :].rearrange("p (k c) -> p k c", k=2)
                                kp += 1
                            else:
                                src = w13[what % 2][:, :, bass.ds(2 * P * i + (g.f0 + what // 2) * P, P)]
                                dst = slot(n, KC)
                            sp.dma_start(dst, src).then_inc(landed[n % RING], 16)
                    if g.straight is not None:
                        ada_jobs(g.straight)
                    with sp.Fori(0, KC // 4) as i:
                        for j in range(4):
                            n = g.down + j
                            sp.wait_ge(lo_done, 4 * i + (n - RING + 1))
                            sp.dma_start(slot(n, g.nf), w2[:, g.f0:g.f0 + g.nf, bass.ds(4 * P * i + j * P, P)])\
                                .then_inc(landed[n % RING], 16)

            def mixer(l):
                w_in = A["w_in"][l].rearrange("(k p) n -> p k n", p=P)
                w_gate = A["w_gate"][l].rearrange("b (k p) n -> b p k n", p=P)
                w_br = A["w_branch"][l].rearrange("b (k p) n -> b p k n", p=P)
                w_out = A["w_out"][l].rearrange("(k p) n -> p k n", p=P)
                for rec in plan.timelines[l]:
                    s, kind = rec["step"], rec["kind"]
                    if "n" not in rec or (kind != "branch" and s[-1] > 0):
                        continue
                    n = rec["n"]
                    if kind == "proj":
                        c0, cw = CHUNKS[s[1]]
                        src = w_in[:, 2 * s[2]:2 * s[2] + 2, c0:c0 + cw]
                    elif kind == "gate":
                        src = w_gate[s[1]][:, :, s[2] * P:(s[2] + 1) * P]
                    elif kind == "branch":
                        src = w_br[s[1]][:, :, s[2] * P:(s[2] + 1) * P]
                    elif kind == "up" and s[1] == "q":
                        src = A["mla_w_uq"][l].rearrange("(k p) n -> p k n", p=P)
                    elif kind == "up":
                        src = A["mla_w_ukv"][l].rearrange("(k p) n -> p k n", p=P)
                    else:
                        src = w_out[:, :, s[1] * P:(s[1] + 1) * P]
                    k, w = src.shape[1], src.shape[2]
                    load(n, w_raw[:, n % RING, 0:k * w].rearrange("p (k c) -> p k c", k=k), src)

            for chunk in range(ADA_PRE):
                ada_jobs(chunk)
            for l in range(DEPTH):
                ffn(l, 0)
                mixer(l)
                ffn(l, 1)
            sp.wait_ge(res_saved, 4)
            sp.dma_start(out[0].rearrange("(t p) d -> p t d", p=P), at(0, LT, D)).then_inc(out_done, 16)
            sp.wait_ge(out_done, 16)

        @block.gpsimd
        def _(pool):
            count = [0]

            def link(ins):
                count[0] += 1
                ins.then_inc(pool_step, 1)
                pool.wait_ge(pool_step, count[0])

            pool.dma_start(mask[:, :], A["mask"]).then_inc(table_land, 16)
            pool.dma_start(rope[:, :, :], A["rope"].rearrange("(t p) c -> p t c", p=P)).then_inc(table_land, 16)
            lam_s = at(TMP0 + 512, DEPTH, 4, 32)
            pool.dma_start(lam_s, A["diff_lambda"].unsqueeze(0).broadcast_to([P, DEPTH, 4, 32])).then_inc(table_land, 16)
            pool.dma_start(scratch, bass.AP(rpb_t, 0, [[0, 64], [1, row]])).then_inc(rpb_land, 16)

            def load_gains(l):
                for o, name in ((G_NA, "na_g_q"), (G_NA + 64, "na_g_k"), (G_GQA, "gqa_g_q"), (G_GQA + 64, "gqa_g_q"),
                                (G_GQA + 128, "gqa_g_k"), (G_DIFF, "diff_g_q"), (G_DIFF + 32, "diff_g_k"),
                                (G_SUB, "diff_g_sub"), (G_CQ, "mla_g_cq"), (G_CKV, "mla_g_ckv"), (G_MQ, "mla_g_q"),
                                (G_MK, "mla_g_k")):
                    v = A[name][l:l + 1, :]
                    pool.dma_start(gains[:, o:o + v.shape[1]], v.broadcast_to([P, v.shape[1]])).then_inc(gain_land, 16)

            def build_k(l):
                pool.wait_ge(drained, up_job[l] + 1)
                pool.wait_ge(slab_done, rot_free[l, "mlaqk"])
                for t in range(TT):
                    k = diff_in[:, t, 0:384].rearrange("p (h d) -> p h d", h=4)
                    link(pool.tensor_copy(k[:, :, 0:64],
                                          kv_up[:, t, :].rearrange("p (h d) -> p h d", h=4)[:, :, 0:64]))
                    last = pool.tensor_copy(k[:, :, 64:96], mla_in[:, t:t + 1, 384:416].broadcast_to([P, 4, 32]))
                    if t == TT - 1:
                        last.then_inc(k_built, 1)
                    else:
                        link(last)

            def norm(l, name, v):
                pool.wait_ge(nr_done, v + 1)
                for t in range(norm_tiles(name, l)):
                    for (ap, n, d, gd, g), vv in zip(norm_views(l, name, t), norm_var(l, name)[0][t]):
                        x3 = ap.rearrange("p (n d) -> p n d", n=n)
                        link(pool.tensor_tensor(x3, x3, vv.unsqueeze(2).broadcast_to([P, n, d]), ALU.mult))
                        x4 = ap.rearrange("p (a b d) -> p a b d", a=gd[0], b=gd[1])
                        link(pool.tensor_tensor(x4, x4, g, ALU.mult))
                if name in ("gqa", "diff", "mlaqk"):
                    if (l, name) != (0, "gqa"):
                        pool.wait_ge(slab_done, rot_free[l, name])
                    rotate(l, name)
                pool.sem_inc(normed, 1)

            def rotate(l, name):
                for t in range(LT):
                    if name == "mlaqk":
                        heads, d, o = 4, 32, 128
                        k = diff_in[:, t, 0:384].rearrange("p (h d) -> p h d", h=4)[:, :, 64:96]
                        qs = mla_in[:, t, 0:384].rearrange("p (h d) -> p h d", h=4)[:, :, 64:96]
                        q = rot_m[:, t, :].rearrange("p (h d) -> p h d", h=4)
                        link(pool.tensor_copy(rot_m[:, t, :], mla_in[:, t, 0:384]))
                        parts = [(k, k, 4), (qs, q[:, :, 64:96], 4)]
                    elif name == "gqa":
                        d, o = 64, 0
                        parts = [(gqa_in[:, t, 256:384].rearrange("p (h d) -> p h d", h=2),) * 2 + (2,),
                                 (gqa_in[:, t, 0:256].rearrange("p (h d) -> p h d", h=4),
                                  rot_q[:, t, :].rearrange("p (h d) -> p h d", h=4), 4)]
                    else:
                        d, o = 32, 128
                        parts = [(diff_in[:, t, 256:512].rearrange("p (h d) -> p h d", h=8),) * 2 + (8,),
                                 (diff_in[:, t, 0:256].rearrange("p (h d) -> p h d", h=8),
                                  rot_q[:, t, :].rearrange("p (h d) -> p h d", h=8), 8)]
                    cos, sin = rope[:, t, o:o + d], rope[:, t, o + d:o + 2 * d]
                    for src, dst, n in parts:
                        e = d // 4
                        sw = swap_t[:, 0:n * d].rearrange("p (h d) -> p h d", h=n)
                        for half in range(2):
                            for pair in range(2):
                                a, b = (2 * pair + half) * e, (2 * pair + 1 - half) * e
                                link(pool.tensor_tensor(sw[:, :, a:a + e], src[:, :, b:b + e],
                                                        sin[:, a:a + e].unsqueeze(1).broadcast_to([P, n, e]), ALU.mult))
                        link(pool.tensor_tensor(dst, src, cos.unsqueeze(1).broadcast_to([P, n, d]), ALU.mult))
                        link(pool.tensor_tensor(dst, dst, sw, ALU.add))

            def norm_low(l, w):
                T, v = NORM_T[l, w], norm_no[l, w]
                if T < NT:
                    return
                for k in range(KC):
                    pool.wait_ge(hh_done, KC * v + k + 1)
                    pool.tensor_tensor(h_lo[:, k, S:NT], n_t[:, k % 4, S:NT], h_hi[:, k, S:NT].bitcast(F32), ALU.subtract)\
                        .then_inc(hc_ready, 1)

            load_gains(0)
            pool.wait_ge(table_land, 16 * 3)
            for l in range(DEPTH):
                pool.wait_ge(rpb_land, 16)
                pool.wait_ge(gain_land, 16 * 12 * (l + 1))
                load_bias(pool, l, 0)
                load_bias(pool, l, 1)
                norm_low(l, 0)
                norm_low(l, 1)
                for rec in plan.timelines[l]:
                    s = rec["step"]
                    if rec["kind"] == "norm":
                        norm(l, s[1], rec["v"])
                    elif rec["kind"] == "build_k":
                        build_k(l)
                if l == 0:
                    pool.wait_ge(y_ready, KC * (l + 1))
                    load_gains(1)
                norm_low(l, 2)

        @block.scalar
        def _(act):
            def hi_loop(n, i, stride=4):
                act.wait_ge(landed[n % RING], 16 * (stride // RING) * i + 16 * (n // RING))
                act.wait_ge(job_done, stride * i + (n - RING + 1))
                act.activation(w_hi[:, n % RING, :], w_raw[:, n % RING, :], ACT.Copy).then_inc(hi_done, 1)

            def hi_mixed(n):
                if n >= plan.total:
                    return
                act.wait_ge(landed[n % RING], 16 * (n // RING))
                act.wait_ge(job_done, n - RING + 1)
                act.activation(w_hi[:, n % RING, 0:width(n)], w_raw[:, n % RING, 0:width(n)], ACT.Copy).then_inc(hi_done, 1)

            def ada_rows_out(chunk, last_job, i=None, stride=0):
                if i is None:
                    act.wait_ge(job_done, last_job + 1)
                    if chunk:
                        act.wait_ge(ada_turned, chunk)
                else:
                    act.wait_ge(job_done, stride * i + (last_job + 1))
                    act.wait_ge(ada_turned, 1 * i + chunk)
                act.activation(ada_rows, b_ada_ps[0:4, :], ACT.Copy).then_inc(ada_out, 1)

            def ada_chunk(chunk):
                n = plan.ada_n0[chunk]
                for k in range(ADA_JOBS):
                    hi_mixed(n + k + 4)
                ada_rows_out(chunk, n + ADA_JOBS - 1)

            def scaled(l, w, m):
                v = norm_no[l, w]
                act.wait_ge(scale_done, v + 1)
                for c, cols in halves(NORM_T[l, w]):
                    last = act.activation(n_xs[:, m, cols], x[:, m, cols], ACT.Identity, scale=scale_g[:, m, c:c + 1])
                last.then_inc(xs_done, 1)

            def square(l, w, m):
                T, v = NORM_T[l, w], norm_no[l, w]
                if v == 0:
                    act.wait_ge(x_done, m + 1)
                else:
                    act.wait_ge(drained, x_jobs[v] + m + 1)
                if m >= 3:
                    act.wait_ge(acc_done, (KC - 2) * v + m - 2)
                dst = n_acc if m == 0 else n_sq[:, m % 2, :]
                act.activation(dst[:, 0:T], x[:, m, 0:T], ACT.Square).then_inc(sq_done, 1)
                if v:
                    scaled(l, w, m)

            def fetch_root(l, w):
                v = norm_no[l, w]
                act.activation(root_set[:, v:v + 1], mean[:, 0:1], ACT.Sqrt)

            def root(l, w):
                T, v = NORM_T[l, w], norm_no[l, w]
                act.wait_ge(mv_done, v + 1)
                act.activation(tok_var[:, 0:T // P], tok_var[:, 0:T // P], ACT.Sqrt).then_inc(mr_done, 1)

            def norm_apply(l, w):
                T, v = NORM_T[l, w], norm_no[l, w]
                if v == 0:
                    scaled(l, w, 0)
                    scaled(l, w, 1)
                for k in range(KC):
                    if v == 0 and k + 2 < KC:
                        scaled(l, w, k + 2)
                    act.wait_ge(t_done, KC * v + k + 1)
                    for c, cols in halves(T):
                        last = act.activation(h_hi[:, k, cols], n_t[:, k % 4, cols], ACT.Identity,
                                              bias=mods[:, shift_no(l, w) + k, c:c + 1])
                    if T == NT:
                        last = act.activation(n_t[:, k % 4, S:NT], n_t[:, k % 4, S:NT], ACT.Identity,
                                              bias=mods[:, shift_no(l, w) + k, 1:2])
                    last.then_inc(hh_done, 1)

            def ffn(l, w):
                T = ffn_T(l, w)
                after = next_norm(l, w)
                a0 = FC * ffn_no(l, w)
                for g in plan.groups[l, w]:
                    stride = len(g.order)
                    with act.Fori(0, g.turns) as i:
                        for o, what in enumerate(g.order):
                            n = g.up + o
                            if what in (0, 2):
                                j = what // 2
                                act.wait_ge(job_done, stride * i + (n + 1))
                                act.wait_ge(drained, stride * i + (n - 3))
                                act.activation(th[:, j, 0:T], banks[(g.up + what) % 4][:, 0:T], ACT.Tanh, scale=0.5)\
                                   .then_inc(th_done, 1)
                            elif what in (1, 3):
                                j = what // 2
                                act.wait_ge(drained, stride * i + (n + 1))
                                act.wait_ge(hi_done, n + 3)
                                act.activation(a_hi[:, bass.ds(2 * i + j, 1), 0:T], a_t[:, j:j + 1, 0:T],
                                               ACT.Copy).then_inc(ah_done, 1)
                            hi_loop(n + 4, i, stride)
                            if what == "a" and "a" not in g.order[o + 1:]:
                                ada_rows_out(g.chunk0, n, i, stride)
                    if g.straight is not None:
                        ada_chunk(g.straight)
                    if g is not plan.groups[l, w][-1]:
                        with act.Fori(0, 2) as i:
                            for j in range(4):
                                hi_loop(g.down + j + 4, i)
                    else:
                        for m in range(KC):
                            if m and after:
                                square(*after, m - 1)
                            if m == KC - 1 and after:
                                fetch_root(*after)
                                square(*after, m)
                            hi_mixed(g.down + m + 4)
                if after:
                    root(*after)

            def mixer(l):
                T, nt = toks_of(l), tiles_of(l)
                for rec in plan.timelines[l]:
                    s, kind = rec["step"], rec["kind"]
                    if kind == "split":
                        hi_mixed(rec["after"] + 4)
                    elif kind == "gate" and finishes(s):
                        n = rec["n"]
                        act.wait_ge(job_done, n + 1)
                        g = gate_no[n]
                        if g >= 1:
                            act.wait_ge(drained, prev_branch[n] + 1)
                        o = l * 32 + s[1] * KC + s[2]
                        act.activation(gate_buf[:, 0:T], banks[n % 4][:, 0:T], ACT.Tanh, scale=0.5,
                                       bias=half_b[:, o:o + 1]).then_inc(gate_th, 1)
                    elif kind == "branch":
                        if s[1] == 3 and s[2] < 6:
                            act.wait_ge(y_sum, 24 * l + 16 + s[2] + 1)
                            act.activation(a_hi[:, s[2], 0:T], y_of(s[2], T), ACT.Copy).then_inc(yh_done, 1)
                    elif kind == "y_last":
                        for m in (6, 7):
                            act.wait_ge(y_sum, 24 * l + 16 + m + 1)
                            act.wait_ge(job_done, y_last_job[l] + 1)
                            act.activation(a_hi[:, m, 0:T], y_of(m, T), ACT.Copy).then_inc(yh_done, 1)
                    elif kind == "out" and finishes(s):
                        if s[1]:
                            square(l, 2, s[1] - 1)
                        if s[1] == KC - 1:
                            fetch_root(l, 2)
                            square(l, 2, KC - 1)
                    elif kind == "head" and s[1] == "na" and s[2] < 2:
                        act.wait_ge(mix_done, rec["u"] + 1)
                        load_bias(act, l, s[2] + 2)
                    elif kind == "norm":
                        v = rec["v"]
                        act.wait_ge(nv_done, v + 1)
                        o0, o1 = VAR0[s[1]], norm_var(l, s[1])[1][-1][1]
                        act.activation(var[:, o0:o1], var[:, o0:o1], ACT.Sqrt).then_inc(nr_done, 1)
                    elif kind == "score":
                        u = rec["u"]
                        b, head, t = s[1:]
                        keys = NT if t < LT else S
                        act.wait_ge(top_done, u + 1)
                        if u:
                            act.wait_ge(turn_done, u)
                        act.activation(prob[:, 0:keys], b_score[:, 0:keys], ACT.Exp,
                                       bias=neg_top[:, u % 2:u % 2 + 1], scale=SCALE[b],
                                       accum_out=rowsum[:, head % 2, t:t + 1]).then_inc(exp_done, 1)
                    elif kind == "turn":
                        u = rec["u"]
                        keys = NT if s[3] < LT else S
                        act.wait_ge(turn_done, u + 1)
                        act.wait_ge(mix_done, u)
                        act.activation(arena[:, PT0:PT0 + keys], b_turn[:, 0:keys], ACT.Copy).then_inc(turn_saved, 1)
                    elif kind == "slab" and rec["x"] % 2 == 1:
                        act.wait_ge(slab_done, rec["x"] + 1)
                        w_, n_ = slab_shape(l, s)
                        act.activation(slab_dest(s[2], s[3])[0:w_, 0:n_], b_slab[0:w_, 0:n_], ACT.Copy)\
                           .then_inc(slab_saved, 1)
                    elif kind == "turn_out":
                        act.wait_ge(slab_done, rec["x"] + 1)
                        act.activation(oT_hi[s[1] % 2][:, s[2], 0:T], b_slab[:, 0:T], ACT.Copy).then_inc(slab_hi, 1)
                    elif kind == "turn_c":
                        act.wait_ge(slab_done, rec["x"] + 1)
                        W = c_tiles(l, s[1]) * P
                        act.activation(cT_hi[:, s[1], 0:W], b_slab[:, 0:W], ACT.Copy).then_inc(slab_hi, 1)

            act.wait_ge(set_saved, 2)
            act.activation(set_t[:, 0:16], vecs[:, 112:128], ACT.Tanh, scale=0.5).then_inc(cond_th, 1)
            act.wait_ge(cond_done, 1)
            act.activation(cond_parts[:, :, 0:2], cond[:, :, :], ACT.Copy).then_inc(cond_hi, 1)
            act.wait_ge(lam_sum, 1)
            act.activation(lam_t[:, 0:4], lam_t[:, 0:4], ACT.Exp).then_inc(lam_exp, 1)
            act.sem_inc(hi_done, RING)
            for m in range(KC):
                square(0, 0, m)
            for n in range(RING, 2 * RING):
                hi_mixed(n)
            root(0, 0)
            for chunk in range(ADA_PRE):
                ada_chunk(chunk)
            for l in range(DEPTH):
                norm_apply(l, 0)
                ffn(l, 0)
                norm_apply(l, 1)
                mixer(l)
                root(l, 2)
                norm_apply(l, 2)
                ffn(l, 1)

        @block.vector
        def _(dve):
            count = [0]

            def link(ins):
                count[0] += 1
                ins.then_inc(dve_step, 1)
                dve.wait_ge(dve_step, count[0])

            def lo(n, w=1024):
                dve.wait_ge(hi_done, n + 1)
                dve.tensor_tensor(w_lo[:, n % RING, 0:w], w_raw[:, n % RING, 0:w], w_hi[:, n % RING, 0:w].bitcast(F32),
                                  ALU.subtract).then_inc(lo_done, 1)

            def lo_loop(n, i, stride=4):
                dve.wait_ge(hi_done, stride * i + (n + 1))
                dve.tensor_tensor(w_lo[:, n % RING, :], w_raw[:, n % RING, :], w_hi[:, n % RING, :].bitcast(F32),
                                  ALU.subtract).then_inc(lo_done, 1)

            def lo_mixed(n):
                if n < plan.total:
                    lo(n, width(n))

            def ada_save(chunk, i=None):
                if i is None:
                    dve.wait_ge(ada_turned, chunk + 1)
                    dst, bia = mods[:, ADA_Q * chunk:ADA_Q * (chunk + 1), :], b_ada[:, ADA_Q * chunk:ADA_Q * (chunk + 1)]
                else:
                    dve.wait_ge(ada_turned, 1 * i + (chunk + 1))
                    dst = mods[:, bass.ds(ADA_Q * i + ADA_Q * chunk, ADA_Q), :]
                    bia = b_ada[:, bass.ds(ADA_Q * i + ADA_Q * chunk, ADA_Q)]
                sums = b_ada_t[:, 0:2 * ADA_Q].rearrange("p (q c) -> p q c", c=2)
                dve.tensor_tensor(dst, sums, bia.unsqueeze(2).broadcast_to([P, ADA_Q, 2]), ALU.add).then_inc(ada_saved, 1)

            def ada_chunk(chunk):
                dve.sem_inc(drained, ADA_JOBS)
                for k in range(ADA_JOBS):
                    lo_mixed(plan.ada_n0[chunk] + k + 4)
                ada_save(chunk)

            def scales(l, w):
                g0, sc = l * 24 + w * KC, shift_no(l, w) + KC
                v = norm_no[l, w]
                dve.wait_ge(ada_saved, ada_saved_by[v])
                if v:
                    dve.wait_ge(xs_done, KC * v)
                dve.scalar_tensor_tensor(scale_g[:, :, :], mods[:, sc:sc + KC, :], 1.0,
                                         vecs[:, g0:g0 + KC].unsqueeze(2).broadcast_to([P, KC, 2]), ALU.add, ALU.mult)\
                   .then_inc(scale_done, 1)

            def add_square(l, w, m):
                T, v = NORM_T[l, w], norm_no[l, w]
                dve.wait_ge(sq_done, KC * v + m + 1)
                if m >= 2:
                    dve.wait_ge(acc_done, (KC - 2) * v + m - 1)
                dve.tensor_tensor(n_acc[:, 0:T], n_acc[:, 0:T], n_sq[:, m % 2, 0:T], ALU.add).then_inc(acc_done, 1)

            def inverse(l, w):
                T, v = NORM_T[l, w], norm_no[l, w]
                ntile = T // P
                dve.wait_ge(ms_done, v + 1)
                link(dve.tensor_scalar(tok_var[:, 0:ntile], b_ms[:, 0:2 * ntile:2], EPS, None, ALU.add))
                dve.reciprocal(tok_var[:, 0:ntile], tok_var[:, 0:ntile]).then_inc(mv_done, 1)
                dve.wait_ge(mr_done, v + 1)
                dve.tensor_copy(n_rb[:, 0:ntile, :], tok_var[:, 0:ntile].unsqueeze(2).broadcast_to([P, ntile, P]))\
                    .then_inc(rb_done, 1)

            def norm_apply(l, w):
                T, v = NORM_T[l, w], norm_no[l, w]
                full = sum(NORM_T[k] == NT for k in sorted(NORM_T)[:v])

                dve.wait_ge(rstd_done, v + 1)

                def times(k):
                    dve.wait_ge(xs_done, KC * v + k + 1)
                    if k >= 4:
                        dve.wait_ge(h_ready, KC * v + k - 3)
                        if T == NT:
                            dve.wait_ge(hc_ready, KC * full + k - 3)
                    dve.tensor_tensor(n_t[:, k % 4, 0:T], n_xs[:, k, 0:T], b_rstd[:, 0:T], ALU.mult).then_inc(t_done, 1)

                def low(k):
                    dve.wait_ge(hh_done, KC * v + k + 1)
                    dve.scalar_tensor_tensor(h_lo[:, k, 0:S], n_t[:, k % 4, 0:S], mods[:, shift_no(l, w) + k, 0:1],
                                             h_hi[:, k, 0:S].bitcast(F32), ALU.add, ALU.subtract).then_inc(h_ready, 1)

                for k in range(KC + 1):
                    if k < KC:
                        times(k)
                    if k:
                        low(k - 1)

            def gates(l, w):
                gt = shift_no(l, w) + 2 * KC
                link(dve.tensor_scalar(gate_s[:, :, :], mods[:, gt:gt + KC, :], 0.5 if w == 1 else 0.25, None, ALU.mult))

            def ffn(l, w):
                T = ffn_T(l, w)
                after = next_norm(l, w)
                a0 = FC * ffn_no(l, w)
                for g in plan.groups[l, w]:
                    stride = len(g.order)
                    counts = [0, 0, 0, 0]
                    for what in g.order:
                        last = last if what == "a" else what
                        counts[last] += 1
                    with dve.Fori(0, g.turns) as i:
                        for o, what in enumerate(g.order):
                            n, j = g.up + o, 0 if what == "a" else what // 2
                            f = a0 + g.f0 + j
                            if what in (0, 2):
                                dve.wait_ge(th_done, 2 * i + (f + 1))
                                dve.scalar_tensor_tensor(s_t[:, 0:T], th[:, j, 0:T], 1.0, banks[(g.up + what) % 4][:, 0:T],
                                                         ALU.add, ALU.mult).then_inc(drained, counts[what])
                            elif what in (1, 3):
                                dve.wait_ge(drained, stride * i + n)
                                dve.wait_ge(job_done, stride * i + (n + 1))
                                dve.tensor_tensor(a_t[:, j, 0:T], s_t[:, 0:T], banks[(g.up + what) % 4][:, 0:T],
                                                  ALU.mult).then_inc(drained, counts[what])
                                dve.wait_ge(ah_done, 2 * i + (f + 1))
                                dve.tensor_tensor(a_lo[:, bass.ds(2 * i + j, 1), 0:T], a_t[:, j:j + 1, 0:T],
                                                  a_hi[:, bass.ds(2 * i + j, 1), 0:T].bitcast(F32),
                                                  ALU.subtract).then_inc(a_ready, 1)
                            lo_loop(n + 4, i, stride)
                        if "a" in g.order:
                            ada_save(g.chunk0, i)
                    if g.straight is not None:
                        ada_chunk(g.straight)
                    if g.f0 == 0:
                        if (l, w) == (0, 0):
                            dve.wait_ge(ada_saved, g.straight + 1)
                        gates(l, 0 if w == 0 else 2)
                    if g is not plan.groups[l, w][-1]:
                        with dve.Fori(0, 2) as i:
                            for j in range(4):
                                n = g.down + j
                                dve.wait_ge(job_done, 4 * i + (n + 1))
                                for c, cols in halves(T):
                                    xs = x[:, bass.ds(4 * i + j, 1), cols]
                                    last = dve.scalar_tensor_tensor(
                                        xs, banks[n % 4][:, cols].unsqueeze(1), gate_s[:, bass.ds(4 * i + j, 1), c],
                                        xs, ALU.mult, ALU.add)
                                last.then_inc(drained, 1)
                                lo_loop(n + 4, i)
                    else:
                        if after:
                            scales(*after)
                        for m in range(KC):
                            n = g.down + m
                            dve.wait_ge(job_done, n + 1)
                            for c, cols in halves(T):
                                last = dve.scalar_tensor_tensor(x[:, m, cols], banks[n % 4][:, cols],
                                                                gate_s[:, m, c:c + 1], x[:, m, cols], ALU.mult, ALU.add)
                            last.then_inc(drained, 1)
                            if m > 1 and after:
                                add_square(*after, m - 1)
                            if m == KC - 1 and after:
                                inverse(*after)
                            lo_mixed(n + 4)

            def mixer(l):
                T, nt = toks_of(l), tiles_of(l)
                first_job, last_job = proj_job[l], plan.ffn_n0[l, 1] - 1

                def split(n):
                    if n > first_job:
                        lo_mixed(n + 3)
                    if n == last_job:
                        lo_mixed(n + 4)

                for rec in plan.timelines[l]:
                    s, kind = rec["step"], rec["kind"]
                    if kind == "gain":
                        dve.wait_ge(gain_land, 16 * 12 * (l + 1))
                        g = gains[:, G_SUB:G_SUB + 64]
                        link(dve.tensor_scalar(g, g, 1.0 - LAM_INIT[l], None, ALU.mult))
                        gates(l, 1)
                    elif kind == "proj" and finishes(s):
                        n, c = rec["n"], s[1]
                        if s[2] == 3:
                            dve.wait_ge(job_done, n + 1)
                            c0, cw = CHUNKS[c]
                            first = n - 3
                            for t in range(TT):
                                for a, b, base, width_ in SEGMENTS:
                                    q0, q1 = proj_cols(l, c, t)
                                    u, v = max(a, c0 + q0), min(b, c0 + q1)
                                    if u < v:
                                        o = base + t * width_ + u - a
                                        dst, src = arena[:, o:o + v - u], banks[(first + t) % 4][:, u - c0:v - c0]
                                        if base == GQA0 and c == 1:
                                            dst = dst.rearrange("p (r g d) -> p r g d", r=2, g=2)
                                            src = src.rearrange("p (g r d) -> p r g d", r=2, g=2)
                                        last = dve.tensor_copy(dst, src)
                                last.then_inc(drained, 1)
                    elif kind == "up" and finishes(s):
                        n = rec["n"]
                        dve.wait_ge(job_done, n + 1)
                        for t in range(nt if s[1] == "q" else TT):
                            dst = mla_in[:, t, 0:384] if s[1] == "q" else kv_up[:, t, :]
                            last = dve.tensor_copy(dst, banks[t][:, 0:dst.shape[1]])
                        last.then_inc(drained, 1)
                    elif kind == "split":
                        split(rec["after"])
                    elif kind == "branch":
                        n, b, m = rec["n"], s[1], s[2]
                        dve.wait_ge(gate_th, gate_no[n - 1] + 1)
                        dve.wait_ge(job_done, n + 1)
                        y = y_of(m, T)
                        if b == 0:
                            dve.scalar_tensor_tensor(y, gate_buf[:, 0:T], 1.0, banks[n % 4][:, 0:T], ALU.add, ALU.mult)\
                               .then_inc(drained, 2)
                        else:
                            dve.scalar_tensor_tensor(sq_t[:, 0:T], gate_buf[:, 0:T], 1.0, banks[n % 4][:, 0:T],
                                                     ALU.add, ALU.mult).then_inc(drained, 2)
                    elif kind == "add":
                        b, m = s[1], s[2]
                        if b:
                            y = y_of(m, T)
                            dve.wait_ge(drained, branch_job[l, b, m] + 1)
                            dve.tensor_tensor(y, y, sq_t[:, 0:T], ALU.add).then_inc(y_sum, 1)
                        if b:
                            dve.wait_ge(y_sum, 24 * l + 8 * (b - 1) + m + 1)
                        if b == 3 and m < 6:
                            y_low(l, m, T)
                    elif kind == "y_last":
                        y_low(l, 6, T)
                        y_low(l, 7, T)
                        scales(l, 2)
                    elif kind == "out" and finishes(s):
                        n, m = rec["n"], s[1]
                        dve.wait_ge(job_done, n + 1)
                        for c, cols in halves(T):
                            last = dve.scalar_tensor_tensor(x[:, m, cols], banks[n % 4][:, cols],
                                                            gate_s[:, m, c:c + 1], x[:, m, cols], ALU.mult, ALU.add)
                        last.then_inc(drained, 1)
                        if m > 1:
                            add_square(l, 2, m - 1)
                        if m == KC - 1:
                            inverse(l, 2)
                    elif kind == "stats":
                        head_stats(l, s[1], s[2])
                    elif kind == "norm":
                        head_norm(l, s[1], rec["v"])
                    elif kind == "score":
                        u = rec["u"]
                        b, head, t = s[1:]
                        keys = NT if t < LT else S
                        dve.wait_ge(score_done, u + 1)
                        link(dve.reduce_max(top[:, u % 2:u % 2 + 1], b_score[:, 0:keys], AX_X))
                        dve.tensor_scalar(neg_top[:, u % 2:u % 2 + 1], top[:, u % 2:u % 2 + 1], -SCALE[b], None,
                                          ALU.mult).then_inc(top_done, 1)
                    elif kind == "head":
                        head_out(l, s[1], s[2], rec["u"])
                    elif kind == "slab" and rec["x"] % 2 == 0:
                        dve.wait_ge(slab_done, rec["x"] + 1)
                        w_, n_ = slab_shape(l, s)
                        dve.tensor_copy(slab_dest(s[2], s[3])[0:w_, 0:n_], b_slab[0:w_, 0:n_]).then_inc(slab_saved, 1)
                    elif kind in ("turn_out", "turn_c"):
                        dve.wait_ge(slab_hi, slab_hi_no[rec["x"]] + 1)
                        if kind == "turn_out":
                            dst, hi_, W = oT_lo[s[1] % 2][:, s[2], 0:T], oT_hi[s[1] % 2][:, s[2], 0:T], T
                        else:
                            W = c_tiles(l, s[1]) * P
                            dst, hi_ = cT_lo[:, s[1], 0:W], cT_hi[:, s[1], 0:W]
                        dve.tensor_tensor(dst, b_slab[:, 0:W], hi_.bitcast(F32),
                                          ALU.subtract).then_inc(slab_saved, 1)
                    if kind == "slab" and s[1] == "na" and s[2:] == ("qu", 0):
                        build_bias(l, 0)
                        build_bias(l, 1)
                    if kind == "score" and s[1] == "na" and s[2] in (1, 2) and s[3] == nt - 1:
                        build_bias(l, s[2] + 1)

            def build_bias(l, head):
                dve.wait_ge(bias_land[head], 64 * (l + 1))
                for t in range(LT):
                    v = bias_m[:, head % 2, t, :].rearrange("p (a c) -> p a c", a=4)
                    last = dve.scalar_tensor_tensor(v, v, 1.0 / SCALE["na"], mask[:, :].unsqueeze(1).broadcast_to([P, 4, 64]),
                                                    ALU.mult, ALU.add)
                last.then_inc(bias_built, 1)

            def y_low(l, m, T):
                dve.wait_ge(yh_done, 8 * l + m + 1)
                dve.tensor_tensor(a_lo[:, m, 0:T], y_of(m, T), a_hi[:, m, 0:T].bitcast(F32), ALU.subtract)\
                   .then_inc(y_ready, 1)

            def head_stats(l, name, t):
                if t == 0 and name == "mlaqk":
                    dve.wait_ge(k_built, l + 1)
                elif t == 0 and name != "sub":
                    dve.wait_ge(drained, proj_job[l] + 4 * (1 + {"na": 1, "gqa": 2, "diff": 3, "mlac": 4}[name]))
                for (ap, n, d, gd, g), vv in zip(norm_views(l, name, t), norm_var(l, name)[0][t]):
                    sq = sq_t[:, 0:n * d]
                    link(dve.tensor_tensor(sq, ap, ap, ALU.mult))
                    link(dve.tensor_reduce(vv, sq.rearrange("p (n d) -> p n d", n=n), AX_X, ALU.add))

            def head_norm(l, name, v):
                o = VAR0[name]
                for d, end in norm_var(l, name)[1]:
                    link(dve.tensor_scalar(var[:, o:end], var[:, o:end], 1.0 / d, EPS, ALU.mult, ALU.add))
                    o = end
                dve.reciprocal(var[:, VAR0[name]:o], var[:, VAR0[name]:o]).then_inc(nv_done, 1)

            def head_out(l, b, head, u):
                nt = tiles_of(l)
                dve.wait_ge(mix_done, u + 1)
                link(dve.reciprocal(rinv[:, 0:nt], rowsum[:, head % 2, 0:nt]))
                o = b_o[:, 0:nt * 64].rearrange("p (t d) -> p t d", t=nt)
                if b == "diff":
                    dst = outs[:, 0:nt, 64 * (head // 2):64 * (head // 2) + 64]
                    if head % 2:
                        link(dve.tensor_scalar(rinv[:, 0:nt], rinv[:, 0:nt], neg_lam[:, l:l + 1], None, ALU.mult))
                        for t in range(nt):
                            last = dve.scalar_tensor_tensor(dst[:, t, :], o[:, t, :], rinv[:, t:t + 1], dst[:, t, :],
                                                            ALU.mult, ALU.add)
                        last.then_inc(head_done, 1)
                        dve.wait_ge(head_done, head_seq[u] + 1)
                        return
                else:
                    dst = outs[:, 0:nt, 64 * head:64 * head + 64]
                dve.tensor_tensor(dst, o, rinv[:, 0:nt].unsqueeze(2).broadcast_to([P, nt, 64]), ALU.mult)\
                    .then_inc(head_done, 1)
                dve.wait_ge(head_done, head_seq[u] + 1)

            dve.sem_inc(drained, RING)
            dve.sem_inc(lo_done, RING)
            dve.memset(mean[:, :], 1.0 / D).then_inc(set_saved, 1)
            dve.wait_ge(set_turned, 1)
            dve.tensor_copy(vecs[:, :], b_slab[:, 0:P]).then_inc(set_saved, 1)
            for g in range(2):
                last = dve.tensor_copy(b_ada[:, g * ADA_L:(g + 1) * ADA_L], b_slab[:, P + g * P:P + g * P + ADA_L])
            link(last)
            dve.wait_ge(cond_th, 1)
            for c in range(2):
                last = dve.scalar_tensor_tensor(cond[:, :, c], set_t[:, 8 * c:8 * c + 8], 1.0,
                                                vecs[:, 112 + 8 * c:120 + 8 * c], ALU.add, ALU.mult)
            link(last)
            dve.tensor_scalar(cond[:, :, :], cond[:, :, :], 0.5, None, ALU.mult).then_inc(cond_done, 1)
            dve.tensor_tensor(both_parts[0:4, :], ident[0:4, 0:2], ident[0:4, 2:4], ALU.add)
            dve.wait_ge(cond_hi, 1)
            dve.tensor_tensor(cond_parts[:, :, 2:4], cond[:, :, :], cond_parts[:, :, 0:2].bitcast(F32), ALU.subtract)\
               .then_inc(cond_done, 1)
            dve.tensor_scalar(half_b[:, :], vecs[:, 48:112], 0.5, None, ALU.mult).then_inc(cond_done, 1)
            dve.wait_ge(table_land, 16 * 3)
            lam_s = at(TMP0 + 512, DEPTH, 4, 32)
            for l in range(DEPTH):
                link(dve.tensor_tensor(set_t[:, 16:80].rearrange("p (a d) -> p a d", a=2), lam_s[:, l, 0:4:2, :],
                                       lam_s[:, l, 1:4:2, :], ALU.mult))
                link(dve.tensor_reduce(lam_t[:, 2 * l:2 * l + 2], set_t[:, 16:80].rearrange("p (a d) -> p a d", a=2),
                                       AX_X, ALU.add))
            dve.sem_inc(lam_sum, 1)
            dve.wait_ge(lam_exp, 1)
            for l in range(DEPTH):
                link(dve.tensor_tensor(neg_lam[:, l:l + 1], lam_t[:, 2 * l + 1:2 * l + 2], lam_t[:, 2 * l:2 * l + 1],
                                       ALU.subtract))
                link(dve.tensor_scalar(neg_lam[:, l:l + 1], neg_lam[:, l:l + 1], -LAM_INIT[l], None, ALU.add))
            for m in range(KC):
                dve.wait_ge(set_turned, m + 2)
                dve.tensor_copy(x[:, m, :], banks[m % 4][:, :]).then_inc(x_done, 1)
            for m in range(1, KC - 1):
                add_square(0, 0, m)
            inverse(0, 0)
            for n in range(RING, 2 * RING):
                lo(n)
            for chunk in range(ADA_PRE):
                ada_chunk(chunk)
            scales(0, 0)
            for l in range(DEPTH):
                norm_apply(l, 0)
                ffn(l, 0)
                norm_apply(l, 1)
                mixer(l)
                norm_apply(l, 2)
                ffn(l, 1)
            res = at(0, LT, D)
            for g in range(4):
                dve.wait_ge(set_turned, 10 + g)
                dve.tensor_copy(res[:, g // 2, 512 * (g % 2):512 * (g % 2) + 512], banks[g][:, :]).then_inc(res_saved, 1)

        @block.tensor
        def _(pe):
            def block_products(out_ap, wh, wl, xh, xl, first, last):
                pe.matmul(out_ap, wh, xh, start=first, stop=False)
                pe.matmul(out_ap, wh, xl, start=False, stop=False)
                return pe.matmul(out_ap, wl, xh, start=False, stop=last)

            def wblock(w, n, k, width_=P):
                return w[:, n % RING, k * width_:(k + 1) * width_]

            def ada_product(n, kp):
                for k in range(2):
                    for w_ in (w_hi, w_lo):
                        last = pe.matmul(b_ada_ps[0:4, :], cond_parts[:, 2 * kp + k, :],
                                         w_[:, n % RING, k * ADA_W:(k + 1) * ADA_W],
                                         start=(kp == 0 and k == 0 and w_ is w_hi),
                                         stop=(kp == ADA_JOBS - 1 and k == 1 and w_ is w_lo))
                last.then_inc(job_done, 1)

            def ada_turn():
                for q in range(ADA_Q):
                    last = pe.matmul(b_ada_t[:, 2 * q:2 * q + 2], ada_rows[:, q * P:(q + 1) * P], both_parts[0:4, :],
                                     start=True, stop=True)
                last.then_inc(ada_turned, 1)

            def ada_chunk(chunk):
                for kp in range(ADA_JOBS):
                    n = plan.ada_n0[chunk] + kp
                    pe.wait_ge(lo_done, n + 1)
                    ada_product(n, kp)
                pe.wait_ge(ada_out, chunk + 1)
                if chunk:
                    pe.wait_ge(ada_saved, chunk)
                ada_turn()

            def norm_stats(l, w):
                T, v = NORM_T[l, w], norm_no[l, w]
                pe.wait_ge(acc_done, (KC - 2) * (v + 1))
                for t in range(T // P):
                    pe.matmul(b_ms[:, 2 * t:2 * t + 2], n_acc[:, t * P:(t + 1) * P], mean[:, :],
                              start=(t == 0), stop=False)
                pe.wait_ge(sq_done, KC * (v + 1))
                for t in range(T // P):
                    last = pe.matmul(b_ms[:, 2 * t:2 * t + 2], n_sq[:, (KC - 1) % 2, t * P:(t + 1) * P], mean[:, :],
                                     start=False, stop=(t == T // P - 1))
                last.then_inc(ms_done, 1)
                pe.wait_ge(rb_done, v + 1)
                for t in range(T // P):
                    last = pe.transpose(b_rstd[:, t * P:(t + 1) * P], n_rb[:, t, :], ident[:, :])
                last.then_inc(rstd_done, 1)

            def wait_h(l, w, k):
                v = norm_no[l, w]
                pe.wait_ge(h_ready, KC * v + k + 1)
                if NORM_T[l, w] == NT:
                    pe.wait_ge(hc_ready, KC * sum(NORM_T[q] == NT for q in sorted(NORM_T)[:v]) + k + 1)

            def ffn(l, w):
                T = ffn_T(l, w)
                a0 = FC * ffn_no(l, w)
                for g in plan.groups[l, w]:
                    stride = len(g.order)
                    with pe.Fori(0, g.turns) as i:
                        kp = 0
                        for o, what in enumerate(g.order):
                            n = g.up + o
                            pe.wait_ge(lo_done, stride * i + (n + 1))
                            if what == "a":
                                ada_product(n, kp)
                                kp += 1
                                continue
                            pe.wait_ge(drained, stride * i + (g.up + what - 3))
                            for k in range(KC):
                                if g.f0 == 0 and what == 0:
                                    wait_h(l, 0 if w == 0 else 2, k)
                                last = block_products(banks[(g.up + what) % 4][:, 0:T], wblock(w_hi, n, k),
                                                      wblock(w_lo, n, k), h_hi[:, k, 0:T], h_lo[:, k, 0:T],
                                                      k == 0, k == KC - 1)
                            last.then_inc(job_done, 1)
                        if "a" in g.order:
                            pe.wait_ge(ada_out, 1 * i + (g.chunk0 + 1))
                            pe.wait_ge(ada_saved, 1 * i + g.chunk0)
                            ada_turn()
                    if g.straight is not None:
                        ada_chunk(g.straight)

                    with pe.Fori(0, KC // 4) as i:
                        for j in range(4):
                            n = g.down + j
                            pe.wait_ge(lo_done, 4 * i + (n + 1))
                            pe.wait_ge(drained, 4 * i + (n - 3))
                            for k in range(g.nf):
                                if j == 0:
                                    pe.wait_ge(a_ready, a0 + g.f0 + k + 1)
                                last = block_products(banks[n % 4][:, 0:T], wblock(w_hi, n, k), wblock(w_lo, n, k),
                                                      a_hi[:, k, 0:T], a_lo[:, k, 0:T], k == 0, k == g.nf - 1)
                            last.then_inc(job_done, 1)

            def mixer(l):
                T, nt = toks_of(l), tiles_of(l)
                for rec in plan.timelines[l]:
                    s, kind = rec["step"], rec["kind"]
                    if kind == "proj":
                        n, c, kp, t = rec["n"], s[1], s[2], s[3]
                        first = n - kp
                        cw = CHUNKS[c][1]
                        if t == 0:
                            pe.wait_ge(lo_done, n + 1)
                        if kp == 0:
                            pe.wait_ge(drained, first + t - 3)
                        for kk in range(2):
                            k = 2 * kp + kk
                            if c == 0 and t == 0:
                                wait_h(l, 1, k)
                            q0, q1 = proj_cols(l, c, t)
                            o = banks[(first + t) % 4][:, q0:q1]
                            toks = slice(t * P, (t + 1) * P)
                            wh, wl = (w_[:, n % RING, kk * cw + q0:kk * cw + q1] for w_ in (w_hi, w_lo))
                            pe.matmul(o, h_hi[:, k, toks], wh, start=(k == 0), stop=False)
                            pe.matmul(o, h_hi[:, k, toks], wl, start=False, stop=False)
                            last = pe.matmul(o, h_lo[:, k, toks], wh, start=False, stop=(k == KC - 1))
                        if finishes(s):
                            last.then_inc(job_done, 1)
                    elif kind == "up":
                        if s[-1] > 0:
                            continue
                        n = rec["n"]
                        pe.wait_ge(lo_done, n + 1)
                        pe.wait_ge(drained, n)
                        pe.wait_ge(slab_saved, c_slab[l] + 1)
                        ks, cw = ([0, 1], 384) if s[1] == "q" else ([2], 512)
                        for t in range(nt if s[1] == "q" else TT):
                            toks = slice(t * P, (t + 1) * P)
                            for q, k in enumerate(ks):
                                o = banks[t][:, 0:cw]
                                wh, wl = (w_[:, n % RING, q * cw:(q + 1) * cw] for w_ in (w_hi, w_lo))
                                pe.matmul(o, cT_hi[:, k, toks], wh, start=(q == 0), stop=False)
                                pe.matmul(o, cT_hi[:, k, toks], wl, start=False, stop=False)
                                last = pe.matmul(o, cT_lo[:, k, toks], wh, start=False, stop=(q == len(ks) - 1))
                        last.then_inc(job_done, 1)
                    elif kind in ("gate", "out"):
                        n, piece = rec["n"], s[-1]
                        if piece == 0:
                            pe.wait_ge(lo_done, n + 1)
                            pe.wait_ge(drained, plan.need_drained[n])
                        src_hi, src_lo = (h_hi, h_lo) if kind == "gate" else (a_hi, a_lo)
                        for k in range(2 * piece, 2 * piece + 2):
                            if kind == "out" and s[1] == 0:
                                pe.wait_ge(y_ready, KC * l + k + 1)
                            last = block_products(banks[n % 4][:, 0:T], wblock(w_hi, n, k), wblock(w_lo, n, k),
                                                  src_hi[:, k, 0:T], src_lo[:, k, 0:T], k == 0, k == KC - 1)
                        if finishes(s):
                            last.then_inc(job_done, 1)
                    elif kind == "branch":
                        n = rec["n"]
                        pe.wait_ge(lo_done, n + 1)
                        pe.wait_ge(drained, plan.need_drained[n])
                        pe.wait_ge(slab_saved, o_slab[l, s[1]] + 1)
                        for k in range(2):
                            last = block_products(banks[n % 4][:, 0:T], wblock(w_hi, n, k), wblock(w_lo, n, k),
                                                  oT_hi[s[1] % 2][:, k, 0:T], oT_lo[s[1] % 2][:, k, 0:T], k == 0, k == 1)
                        last.then_inc(job_done, 1)
                    elif kind in ("slab", "turn_out", "turn_c"):
                        xno = rec["x"]
                        if kind == "slab":
                            pe.wait_ge(normed, normed_for[l, s[1]])
                            tiles = slab_tiles(l, s[2])
                            srcs = [slab_source(s[1], s[2], s[3], t) for t in range(tiles)]
                        elif kind == "turn_out":
                            pe.wait_ge(head_done, heads_before[xno])
                            if xno in sub_before:
                                pe.wait_ge(normed, sub_before[xno])
                            srcs = [outs[:, t, s[2] * P:(s[2] + 1) * P] for t in range(nt)]
                        else:
                            pe.wait_ge(normed, normed_for[l, "mlac"])
                            srcs = [mla_in[:, t, s[1] * P:(s[1] + 1) * P] for t in range(c_tiles(l, s[1]))]
                        if xno:
                            pe.wait_ge(slab_saved, xno)
                        for t, src in enumerate(srcs):
                            w_ = math.prod(src.shape[1:])
                            last = pe.transpose(b_slab[0:w_, t * P:(t + 1) * P], src, ident[:, :])
                        last.then_inc(slab_done, 1)
                    elif kind == "score":
                        u = rec["u"]
                        b, head, t = s[1:]
                        sq, sk, p0, d = unit_ap(b, head)
                        pe.wait_ge(slab_saved, slab_for[l, b] + 1)
                        if u:
                            pe.wait_ge(exp_done, u)
                        rows = slice(p0, p0 + d)
                        toks = slice(t * P, (t + 1) * P)
                        qu = qT_u[rows, sq, toks]
                        if t >= LT:
                            last = pe.matmul(b_score[:, 0:S], qu, kT[rows, sk, S:NT], start=True, stop=True)
                        elif b == "na":
                            pe.wait_ge(bias_built, 4 * l + head + 1)
                            pe.matmul(b_score[:, 0:S], qu, kT[rows, sk, 0:S], start=True, stop=False)
                            pe.matmul(b_score[:, 0:S], ident[:, :], bias_m[:, head % 2, t, :], start=False, stop=True)
                            last = pe.matmul(b_score[:, S:NT], qu, kT[rows, sk, S:NT], start=True, stop=True)
                        else:
                            pe.matmul(b_score[:, 0:S], qT_r[rows, sq, toks], kT[rows, sk, 0:S], start=True, stop=True)
                            last = pe.matmul(b_score[:, S:NT], qu, kT[rows, sk, S:NT], start=True, stop=True)
                        last.then_inc(score_done, 1)
                    elif kind == "turn":
                        u, t = rec["u"], s[3]
                        pe.wait_ge(exp_done, u + 1)
                        if u:
                            pe.wait_ge(turn_saved, u)
                        for q in range(4 if t < LT else 2):
                            last = pe.transpose(b_turn[:, q * P:(q + 1) * P], prob[:, q * P:(q + 1) * P], ident[:, :])
                        last.then_inc(turn_done, 1)
                    elif kind == "mix":
                        u = rec["u"]
                        b, head, t = s[1:]
                        pe.wait_ge(turn_saved, u + 1)
                        if t == 0 and head_first[u]:
                            pe.wait_ge(head_done, head_first[u])
                        tiles = range(TT) if t < LT else range(LT, TT)
                        for q, kt in enumerate(tiles):
                            last = pe.matmul(b_o[:, 64 * t:64 * t + 64], probT[:, q, :], value_ap(b, head, kt),
                                             start=(q == 0), stop=(q == len(tiles) - 1))
                        last.then_inc(mix_done, 1)

            pe.sem_inc(job_done, RING)
            stage = at(TMP0, 4, P)
            stage_x = at(Q0, 4, D)
            pe.wait_ge(const_land, 16 * 6)
            pe.transpose(b_slab[:, 0:P], stage[:, 0, :], ident[:, :])
            for g in range(2):
                last = pe.transpose(b_slab[:, P + g * P:P + g * P + ADA_L], stage[0:ADA_L, 1 + g, :],
                                    ident[0:ADA_L, 0:ADA_L])
            last.then_inc(set_turned, 1)
            pe.wait_ge(in_land, 32)
            for m in range(KC):
                if m >= 4:
                    pe.wait_ge(x_done, m - 3)
                for t in range(TT):
                    last = pe.transpose(banks[m % 4][:, t * P:(t + 1) * P], stage_x[:, t, m * P:(m + 1) * P], ident[:, :])
                last.then_inc(set_turned, 1)
            pe.wait_ge(set_saved, 1)
            norm_stats(0, 0)
            pe.wait_ge(cond_done, 2)
            for chunk in range(ADA_PRE):
                ada_chunk(chunk)
            for l in range(DEPTH):
                if l:
                    norm_stats(l, 0)
                ffn(l, 0)
                norm_stats(l, 1)
                mixer(l)
                norm_stats(l, 2)
                ffn(l, 1)
            for g in range(4):
                t, half = g // 2, g % 2
                pe.wait_ge(drained, plan.total)
                for q in range(4):
                    last = pe.transpose(banks[g][:, q * P:(q + 1) * P], x[:, 4 * half + q, t * P:(t + 1) * P], ident[:, :])
                last.then_inc(set_turned, 1)


_INS = ["x", "c", "ctx", "c_ctx", "w_ada", "b_ada", "norm_g", "ffn_w1", "ffn_w3", "ffn_w2", "w_in", "na_g_q", "na_g_k",
        "na_rpb", "gqa_g_q", "gqa_g_k", "diff_g_q", "diff_g_k", "diff_lambda", "diff_g_sub", "mla_g_cq", "mla_g_ckv",
        "mla_w_uq", "mla_w_ukv", "mla_g_q", "mla_g_k", "w_gate", "b_gate", "w_branch", "w_out"]


def shape_tables():
    import numpy as np
    col = np.arange(GRID_W)
    c0 = np.clip(col - 8, 0, GRID_W - 16)
    inside = (col[None, :] >= c0[:, None]) & (col[None, :] < c0[:, None] + 16)
    window = np.where(inside, 0.0, -1e30).astype(np.float32)
    tok = np.arange(S)
    tables = []
    for d in (64, 32):
        n = d // 4
        inv = (np.float32(10000.0) ** (-np.arange(n, dtype=np.float32) / np.float32(n))).astype(np.float32)
        ar = (tok // GRID_W).astype(np.float32)[:, None] * inv[None, :]
        ac = (tok % GRID_W).astype(np.float32)[:, None] * inv[None, :]
        ang = np.concatenate([ar, ar, ac, ac], axis=1).astype(np.float64)
        sign = np.concatenate([-np.ones(n), np.ones(n), -np.ones(n), np.ones(n)])
        tables += [np.cos(ang), np.sin(ang) * sign]
    return {"ident": np.eye(P, dtype=np.float32), "mask": np.concatenate([window, window], axis=0),
            "rope": np.concatenate(tables, axis=1).astype(np.float32)}


def kernel(**inputs):
    import numpy as _np
    import concourse.bacc as _bacc
    from concourse import mybir as _mybir
    from concourse.bass_utils import run_bass_kernel_spmd as _run

    nc = _bacc.Bacc("TRN2", target_bir_lowering=False, num_devices=1)
    arrays, A = {}, {}
    for name in _INS:
        arrays[f"in_{name}"] = _np.ascontiguousarray(inputs[name])
    for name, a in shape_tables().items():
        arrays[f"in_{name}"] = a
    for name, a in arrays.items():
        A[name[3:]] = nc.dram_tensor(name, a.shape, _mybir.dt.from_np(a.dtype), kind="ExternalInput").ap()
    out = nc.dram_tensor("out_0", (1, S, D), F32, kind="ExternalOutput").ap()
    build(nc, A, out)
    r = _run(nc, [arrays], core_ids=[0])
    return r.results[0]["out_0"]
```
